# Optimizing a Trainium2 kernel written in Bass

```python
import math
import jax, jax.numpy as jnp
from jax import lax
import numpy as np

D_MODEL = 1024
BATCH = 1
SEQ = 1024
DEPTH = 1
DEC_BATCH = 8
DEC_SEQ = 1
PAST_LEN = 1024
PAGE_SIZE = 128

HEAD_DIM = 64
A_HEADS = 8
A_KV_HEADS = 4
A_GROUP = A_HEADS // A_KV_HEADS
D_ATTN = A_HEADS * HEAD_DIM
IDX_HEADS = 8
IDX_DIM = 64
TOPK_MAX = 256
Q_BLOCK = 128
N_BUCKETS = 32
MAX_DISTANCE = 128
H_HEADS = 8
H_KEY = 64
H_VAL = 64
D_HKEY = H_HEADS * H_KEY
D_HGRN = H_HEADS * H_VAL
HG_CHUNK = 64
D_MIX = D_ATTN + D_HGRN
EPS = 1e-6
SPLIT_WIDTHS = (D_ATTN, A_KV_HEADS * HEAD_DIM, A_KV_HEADS * HEAD_DIM, D_ATTN,
                IDX_HEADS * IDX_DIM, IDX_HEADS, IDX_DIM,
                D_HKEY, D_HKEY, D_HGRN, D_HGRN)
D_IN = sum(SPLIT_WIDTHS)

kernel_name = 'hymba_dsa_hgrn2_step'

F32 = jnp.float32

def rms_norm(x, g):
    xf = x.astype(F32)
    y = xf * lax.rsqrt(jnp.mean(xf * xf, axis=-1, keepdims=True) + EPS) * g.astype(F32)
    return y.astype(x.dtype)

def split_columns(h):
    parts, o = [], 0
    for w in SPLIT_WIDTHS:
        parts.append(h[..., o:o + w])
        o += w
    return parts

def t5_bucket(n):
    n = jnp.maximum(n, 0)
    max_exact = N_BUCKETS // 2
    nf = jnp.maximum(n, 1).astype(F32)
    large = max_exact + (jnp.log(nf / max_exact) / math.log(MAX_DISTANCE / max_exact)
                         * (N_BUCKETS - max_exact)).astype(jnp.int32)
    large = jnp.minimum(large, N_BUCKETS - 1)
    return jnp.where(n < max_exact, n, large)

def branch_inputs(x, ln_g, w_in, q_g, k_g, lb):
    B, T = x.shape[:2]
    h = jnp.einsum('btd,de->bte', rms_norm(x, ln_g), w_in)
    a_q, a_k, a_v, a_gate, i_q, i_w, i_k, h_q, h_f, h_i, h_gate = split_columns(h)
    q = rms_norm(a_q.reshape(B, T, A_HEADS, HEAD_DIM), q_g)
    k = rms_norm(a_k.reshape(B, T, A_KV_HEADS, HEAD_DIM), k_g)
    v = a_v.reshape(B, T, A_KV_HEADS, HEAD_DIM)
    iq = i_q.reshape(B, T, IDX_HEADS, IDX_DIM)
    iw = i_w.astype(F32) * IDX_HEADS ** -0.5
    hq = jax.nn.silu(h_q.astype(F32)).reshape(B, T, H_HEADS, H_KEY) * H_KEY ** -0.5
    lb = lb.reshape(H_HEADS, H_KEY)
    f = lb + (1.0 - lb) * jax.nn.sigmoid(h_f.astype(F32).reshape(B, T, H_HEADS, H_KEY))
    hg = jnp.log(f)
    hk = 1.0 - f
    hv = h_i.astype(F32).reshape(B, T, H_HEADS, H_VAL)
    return q, k, v, a_gate, iq, iw, i_k, hq, hg, hk, hv, h_gate

def indexer_topk(iq, iw, ik, q_pos, topk):
    s = jnp.einsum('bthd,bsd->bths', iq.astype(F32), ik.astype(F32)) * IDX_DIM ** -0.5
    score = jnp.einsum('bths,bth->bts', jax.nn.relu(s), iw)
    L = ik.shape[1]
    causal = jnp.arange(L)[None, :] <= q_pos[:, None]
    score = jnp.where(causal[None], score, -jnp.inf)
    _, idx = lax.top_k(score, topk)
    valid = idx <= q_pos[None, :, None]
    return idx, valid

def sparse_attn(q, k_sel, v_sel, idx, q_pos, valid, rel_table):
    B, T = q.shape[:2]
    K = idx.shape[-1]
    qg = q.reshape(B, T, A_KV_HEADS, A_GROUP, HEAD_DIM)
    logits = jnp.einsum('btngd,btknd->btngk', qg, k_sel).astype(F32) * HEAD_DIM ** -0.5
    bias = rel_table.astype(F32)[t5_bucket(q_pos[None, :, None] - idx)]
    bias = bias.reshape(B, T, K, A_KV_HEADS, A_GROUP).transpose(0, 1, 3, 4, 2)
    logits = jnp.where(valid[:, :, None, None, :], logits + bias, -jnp.inf)
    p = jax.nn.softmax(logits, axis=-1)
    out = jnp.einsum('btngk,btknd->btngd', p.astype(v_sel.dtype), v_sel)
    return out.reshape(B, T, D_ATTN)

def attn_prompt(q, k, v, iq, iw, ik, rel_table):
    B, S = q.shape[:2]
    topk = min(TOPK_MAX, S // 4)
    nb = S // Q_BLOCK
    take = jax.vmap(lambda rows, ids: rows[ids])

    def block(args):
        qb, iqb, iwb, start = args
        q_pos = start + jnp.arange(Q_BLOCK, dtype=jnp.int32)
        idx, valid = indexer_topk(iqb, iwb, ik, q_pos, topk)
        return sparse_attn(qb, take(k, idx), take(v, idx), idx, q_pos, valid, rel_table)

    to_blocks = lambda a: jnp.moveaxis(a.reshape((B, nb, Q_BLOCK) + a.shape[2:]), 1, 0)
    starts = jnp.arange(nb, dtype=jnp.int32) * Q_BLOCK
    out = lax.map(block, (to_blocks(q), to_blocks(iq), to_blocks(iw), starts))
    return jnp.moveaxis(out, 0, 1).reshape(B, S, D_ATTN)

def attn_sample(q, k_new, v_new, iq, iw, ik_new, cache_k, cache_v, cache_ik, layer,
                page_table, rel_table):
    DB, T = q.shape[:2]
    past = page_table.shape[1] * PAGE_SIZE
    ik_past = cache_ik[layer, page_table].reshape(DB, past, IDX_DIM)
    ik_all = jnp.concatenate([ik_past, ik_new.astype(ik_past.dtype)], axis=1)
    topk = min(TOPK_MAX, (past + T) // 4)
    q_pos = past + jnp.arange(T, dtype=jnp.int32)
    idx, valid = indexer_topk(iq, iw, ik_all, q_pos, topk)
    in_past = idx < past
    jp = jnp.minimum(idx, past - 1)
    phys = jax.vmap(lambda pt, pg: pt[pg])(page_table, jp // PAGE_SIZE)
    off = jp % PAGE_SIZE
    jn = jnp.clip(idx - past, 0, T - 1)
    take = jax.vmap(lambda rows, ids: rows[ids])

    def select(pool, new):
        from_past = pool[layer, phys, off]
        from_new = take(new, jn).astype(from_past.dtype)
        return jnp.where(in_past[..., None, None], from_past, from_new)

    return sparse_attn(q, select(cache_k, k_new), select(cache_v, v_new), idx, q_pos,
                       valid, rel_table)

def gla_chunk(S0, q, g, k, v):
    C = q.shape[1]
    b = jnp.cumsum(g, axis=1)
    mask = jnp.tril(jnp.ones((C, C), dtype=bool))[None, :, :, None, None]
    diff = b[:, :, None] - b[:, None, :]
    decay = jnp.exp(jnp.where(mask, diff, -jnp.inf))
    A = jnp.einsum('bthk,bshk,btshk->bths', q, k, decay)
    o = jnp.einsum('bths,bshv->bthv', A, v) + jnp.einsum('bthk,bhkv->bthv', q * jnp.exp(b), S0)
    S_new = jnp.exp(b[:, -1])[..., None] * S0 + jnp.einsum(
        'bshk,bshv->bhkv', k * jnp.exp(b[:, -1:] - b), v)
    return S_new, o

def hgrn_prompt(q, g, k, v):
    B, S = q.shape[:2]
    nc = S // HG_CHUNK
    to_c = lambda a: jnp.moveaxis(a.reshape((B, nc, HG_CHUNK) + a.shape[2:]), 1, 0)
    S0 = jnp.zeros((B, H_HEADS, H_KEY, H_VAL), F32)
    S_fin, o = lax.scan(lambda s, xs: gla_chunk(s, *xs), S0, (to_c(q), to_c(g), to_c(k), to_c(v)))
    return S_fin, jnp.moveaxis(o, 0, 1).reshape(B, S, H_HEADS, H_VAL)

def out_merge(x, a_out, a_gate, h_out, h_gate, hn_g, w_out):
    B, T = x.shape[:2]
    h_n = rms_norm(h_out, hn_g).reshape(B, T, D_HGRN).astype(x.dtype)
    mix = jnp.concatenate([a_out.astype(x.dtype) * jax.nn.silu(a_gate),
                           h_n * jax.nn.silu(h_gate)], axis=-1)
    return x + jnp.einsum('bte,ed->btd', mix, w_out)

def setup_inputs(seed: int = 0) -> dict:
    key = jax.random.key(seed)
    ks = jax.random.split(key, 16)
    n_pages = PAST_LEN // PAGE_SIZE
    n_pool = (DEC_BATCH * n_pages * 5) // 4
    nrm = jax.random.normal
    page_table = jax.random.permutation(ks[0], n_pool)[:DEC_BATCH * n_pages]
    page_table = page_table.reshape(DEC_BATCH, n_pages).astype(jnp.int32)
    return {
        'x_prompt': nrm(ks[1], (BATCH, SEQ, D_MODEL), F32),
        'x_sample': nrm(ks[2], (DEC_BATCH, DEC_SEQ, D_MODEL), F32),
        'cache_k': nrm(ks[3], (DEPTH, n_pool, PAGE_SIZE, A_KV_HEADS, HEAD_DIM), F32),
        'cache_v': nrm(ks[4], (DEPTH, n_pool, PAGE_SIZE, A_KV_HEADS, HEAD_DIM), F32),
        'cache_ik': nrm(ks[5], (DEPTH, n_pool, PAGE_SIZE, IDX_DIM), F32),
        'state_hgrn': 0.5 * nrm(ks[6], (DEPTH, DEC_BATCH, H_HEADS, H_KEY, H_VAL), F32),
        'page_table': page_table,
        'rel_bias': 0.5 * nrm(ks[7], (N_BUCKETS, A_HEADS), F32),
        'ln_g': 1.0 + 0.1 * nrm(ks[8], (DEPTH, D_MODEL), F32),
        'w_in': nrm(ks[9], (DEPTH, D_MODEL, D_IN), F32) * D_MODEL ** -0.5,
        'q_norm_g': 1.0 + 0.1 * nrm(ks[10], (DEPTH, HEAD_DIM), F32),
        'k_norm_g': 1.0 + 0.1 * nrm(ks[11], (DEPTH, HEAD_DIM), F32),
        'hgrn_lb': nrm(ks[12], (DEPTH + 1, D_HKEY), F32),
        'hgrn_norm_g': 1.0 + 0.1 * nrm(ks[13], (DEPTH, H_VAL), F32),
        'w_out': nrm(ks[14], (DEPTH, D_MIX, D_MODEL), F32) * D_MIX ** -0.5,
    }

def reference(x_prompt, x_sample, cache_k, cache_v, cache_ik, state_hgrn, page_table,
              rel_bias, ln_g, w_in, q_norm_g, k_norm_g, hgrn_lb, hgrn_norm_g, w_out):
    lb_all = jnp.cumsum(jax.nn.softmax(hgrn_lb.astype(F32), axis=0), axis=0)
    xp, xs = x_prompt, x_sample
    kp_l, vp_l, ikp_l, sp_l, ks_l, vs_l, iks_l, ss_l = [], [], [], [], [], [], [], []
    for l in range(DEPTH):
        q, k, v, a_gate, iq, iw, ik, hq, hg, hk, hv, h_gate = branch_inputs(
            xp, ln_g[l], w_in[l], q_norm_g[l], k_norm_g[l], lb_all[l])
        a_out = attn_prompt(q, k, v, iq, iw, ik, rel_bias)
        s_fin, h_out = hgrn_prompt(hq, hg, hk, hv)
        xp = out_merge(xp, a_out, a_gate, h_out, h_gate, hgrn_norm_g[l], w_out[l])
        kp_l.append(k); vp_l.append(v); ikp_l.append(ik); sp_l.append(s_fin.astype(x_prompt.dtype))
        q, k, v, a_gate, iq, iw, ik, hq, hg, hk, hv, h_gate = branch_inputs(
            xs, ln_g[l], w_in[l], q_norm_g[l], k_norm_g[l], lb_all[l])
        a_out = attn_sample(q, k, v, iq, iw, ik, cache_k, cache_v, cache_ik, l, page_table, rel_bias)
        s_new, h_out = gla_chunk(state_hgrn[l].astype(F32), hq, hg, hk, hv)
        xs = out_merge(xs, a_out, a_gate, h_out, h_gate, hgrn_norm_g[l], w_out[l])
        ks_l.append(k); vs_l.append(v); iks_l.append(ik); ss_l.append(s_new.astype(state_hgrn.dtype))
    return (xp, xs, jnp.stack(kp_l), jnp.stack(vp_l), jnp.stack(ikp_l), jnp.stack(sp_l),
            jnp.stack(ks_l), jnp.stack(vs_l), jnp.stack(iks_l), jnp.stack(ss_l))


_drawn_inputs = setup_inputs


def setup_inputs(seed=0):
    import zlib

    import numpy as np

    out = dict(_drawn_inputs(seed))
    spreads = {}
    factors = {'rel_bias': 3.125, 'q_norm_g': 8.0}
    for name, (base, spread) in spreads.items():
        noise = np.random.default_rng([zlib.crc32(name.encode()), seed]).standard_normal(out[name].shape)
        drawn = base * np.exp(spread * noise) if base else spread * noise
        out[name] = __import__('jax').numpy.asarray(drawn.astype(out[name].dtype))
    for name, factor in factors.items():
        out[name] = (out[name] * factor).astype(out[name].dtype)
    return out
```

```python
import numpy as np
import concourse.bass as bass
from concourse import mybir
from contextlib import ExitStack

F32 = mybir.dt.float32
F32R = mybir.dt.float32r
BF16 = mybir.dt.bfloat16
F16 = mybir.dt.float16
I32 = mybir.dt.int32
ACT = mybir.ActivationFunctionType
ALU = mybir.AluOpType
AX = mybir.AxisListType

P = 128
D = 1024
KC = D // P
T = 1024
NT = T // P
SB = 8
TT = T + SB
PAST = 1024
NPG = PAST // P
NPOOL = 80
HD = 64
AH, KVH, IH, HH = 8, 4, 8, 8
NG = HH // 2
SUB = 32
NSUB = P // SUB
TOPK = 256
EPS = 1e-6
NEG = -1e30
UNSEEN = -3e38
UW = 256
NEAR = 2 * P
NCONST_ = 17 * 16
UL = 383
ROUNDS = 31
BR = SB * AH


def rows(i):
    return P if i < NT else SB


CHUNKS = [(0, 384), (384, 384), (768, 264)]
UNITS = [("iq", 0), ("iq", 1), ("ix", 0), ("hg", 0), ("hv", 0), ("hv", 1),
         ("hg", 1), ("gh", 0), ("k", 0), ("hg", 2), ("gh", 1), ("q", 0),
         ("hg", 3), ("ga", 0), ("q", 1), ("ga", 1), ("v", 0)]
NU = len(UNITS)
NUO = D // UW
UIX = UNITS.index(("ix", 0))
XW = IH + HD
HUNIT = {UNITS.index(("hv", 1)): 0, UNITS.index(("k", 0)): 1, UNITS.index(("q", 0)): 2,
         UNITS.index(("q", 1)): 3}


def width(u):
    return XW if u == UIX else UW


def jobs(u):
    kind = UNITS[u][0] if u < NU else "out"
    if kind == "iq":
        return [("T", b, c) for c in range(3) for b in range(2)]
    if kind == "hg":
        return [("T", b, c) for b in range(2) for c in range(3)]
    return [("N", i, 0) for i in range(NT + 1)]


JOB0 = [0]
for _u in range(NU + NUO):
    JOB0.append(JOB0[-1] + len(jobs(_u)))
PJ = 4
STAGED = ("v", "gh", "ga")
HGU = [UNITS.index(("hg", j)) for j in range(NG)]
NORMED = [UNITS.index(x) for x in (("k", 0), ("q", 0), ("q", 1))]
STG_UNITS = [u for u in range(NU) if UNITS[u][0] in STAGED]

SC0 = {t: sum(P * (x + 1) for x in range(2, t)) for t in range(2, NT)}
SCW = sum(P * (x + 1) for x in range(2, NT))


def hymba_step(nc, x_prompt, x_sample, w_main, w_ix, cache_kt, cache_v, cache_ikt, state, pages,
               rel, ln_g, q_g, k_g, hn_g, lbs, c_ident, c_oh, c_bits, c_e8, c_masks,
               y_prompt, y_sample, k_prompt, v_prompt, ik_prompt, s_prompt,
               k_sample, v_sample, ik_sample, s_sample):
    with ExitStack() as ctx:
        cur = [16512]

        def at(name, shape, dt, off):
            return nc.alloc_sbuf_tensor_at(name, [P] + shape, dt, offset=off)

        def size(shape, dt):
            return int(np.prod(shape)) * {F32: 4, F32R: 4, I32: 4, BF16: 2, F16: 2}[dt]

        def sb(name, shape, dt=F32):
            off = cur[0]
            cur[0] += (size(shape, dt) + 31) // 32 * 32
            assert cur[0] <= 229344, (name, cur[0])
            return at(name, shape, dt, off)

        def over(start, *parts):
            out = []
            for name, shape, dt in parts:
                out.append(at(name, shape, dt, start))
                start += (size(shape, dt) + 31) // 32 * 32
            out.append(start)
            return out

        def sem(name):
            return ctx.enter_context(nc.semaphore(name))

        def ge(eng, s, v):
            if v > 0:
                eng.wait_ge(s, v)

        IDN = sb("ident", [P])
        ANR = sb("antidiagonal_r", [P], F32R)
        IDB = sb("ident_b", [P], BF16)
        LNG = sb("ln_gain", [KC])
        QG = sb("q_gain", [HD])
        KG = sb("k_gain", [HD])
        HNG = sb("hgrn_gain", [HD])
        IW = sb("index_weight", [NT + 1, IH])
        STAT = sb("x_stats", [4, NT + 1])
        LBR = sb("lb_rows", [2, NG])
        LB = sb("lb", [NG])
        OML = sb("one_minus_lb", [NG])
        TRI = sb("causal_add", [P], BF16)
        FS = sb("f_sample", [NG, SB])
        QSS = sb("q_sample", [NG, SB])
        KSS = sb("k_sample_h", [NG, SB])
        IKNEW = sb("ik_new", [4])
        BITF = sb("bit_value", [ROUNDS])
        BITI = sb("bit", [ROUNDS], I32)
        CNT = sb("count", [7])
        NEED = sb("need", [7])
        U = sb("bits_so_far", [7], I32)
        XM = sb("sign_flip", [7], I32)
        CAND = sb("candidate", [7], I32)
        HIT = sb("bit_kept", [7], I32)
        NRM = sb("norm_stats", [3, 2, 4])
        DE = sb("chunk_decay", [2, NT])
        PT_ = sb("page_table", [SB * NPG], I32)
        E8 = sb("row_select", [BR])
        E8H = sb("head_select", [BR])
        HM = sb("head_mask", [2 * SB])
        E8B = sb("row_select_b", [BR], BF16)
        IWC = sb("index_weight_col", [1])
        WSEL = sb("index_weight_sel", [SB])
        HMT = sb("head_mask_tmp", [SB])
        MX = sb("row_max", [8])
        NB = sb("neg_max", [8])
        RS = sb("row_sum", [2, 8])
        RI = sb("row_sum_inv", [8])
        MN = sb("mix_stats", [2, 2, 8])
        UT = sb("bias_by_distance", [UL])
        EPSC = sb("eps", [1])
        ONE = sb("one", [1])
        TRF = sb("causal_add_f", [P])
        ANT = sb("antidiagonal", [P])

        XR0 = cur[0]
        XH = sb("xT_high", [KC, TT], F32R)
        XL = sb("xT_low", [KC, TT], F32R)
        QS, KA, KB, _ = over(XR0, ("qT_stack", [AH, T], F32R), ("kT_high_low", [KVH, T], F32R),
                             ("kT_low_high", [KVH, T], F32R))
        KS_, VS_, _ = over(XR0, ("keys_T", [2, 2, PAST], F32), ("values", [2, NPG, UW], F32))
        WR = sb("w_raw", [2, 4, UW])
        W0 = cur[0]
        WH = sb("w_high", [2, KC, UW], F32R)
        WL = sb("w_low", [2, KC, UW], F32R)
        BH, BL, VT, QR, KR, _e = over(W0, ("bias_high", [AH, NEAR], F32R), ("bias_low", [AH, NEAR], F32R),
                                      ("values_T", [NT, UW], F32), ("q_rows", [2, 512], F32),
                                      ("k_rows", [2, KVH, 2, HD], F32))
        assert _e <= cur[0]
        S0 = cur[0]
        SC = sb("scores", [SCW])
        SCS = sb("scores_sample", [PAST + 32])
        R0_ = cur[0]
        RB = sb("relu", [2, T])
        XB, _e = over(S0, ("x_rows", [6, D], F32))
        assert _e <= cur[0]
        MSK, = over(S0, ("mask", [2 * SCW], BF16))[:1]
        MSKS, = over(S0 + SCW * 4, ("mask_sample", [2 * PAST + 64], BF16))[:1]
        FB, QB, _ = over(R0_, ("decay_log", [T], F32), ("hq", [T], F32))
        PTS, _ = over(R0_, ("pT", [2, NT, P], F32))
        JK = sb("flag", [PAST + 8], F16)
        CU = sb("flag_count", [PAST + 8], F16)
        I0 = cur[0]
        IQS = sb("iqT_stack", [IH, T - 2 * P], F32R)
        IA = sb("ikT_high_low", [T], F32R)
        IB = sb("ikT_low_high", [T], F32R)
        HV, HK, QI, ATB, HO, _e = over(I0, ("hv", [NT + 1, 512], F32), ("hk", [T], F32), ("q_decayed", [T], F32),
                               ("intra", [2, 2, P], F32), ("ho_rows", [NT, P], F32))
        assert _e <= cur[0], (_e, cur[0])
        AO, PB, _e = over(I0, ("attn_out", [NT + 1, 512], F32), ("prob", [3, T], F32))
        assert _e <= cur[0]
        STG = sb("stage", [2, UW])
        H0 = cur[0]
        QT = sb("q_ref", [2, T])
        KT = sb("k_ref", [NT * SUB * 10])
        KTN = sb("k_rows_h", [2, P])
        INM = sb("intra_mask", [2, P])
        BM = sb("pair_mask", [P])
        ST_OFF = cur[0]
        ST = sb("hgrn_state", [NG, P])
        TMP = sb("state_add", [2, P])
        RM = sb("scan_keep", [T], BF16)
        NQ = sb("norm_rows", [2, UW])
        SQ = sb("norm_sq", [UW])
        JA, IKN, _e = over(H0, ("square_junk", [D], F32), ("ik_rows", [NT + 1, 2, HD], F32))
        IK0 = _e
        IKT, IQP, _e = over(IK0, ("index_keys_T", [2, PAST], F32), ("iq_padded", [4, BR], F32))
        assert _e <= H0 + 8192 + 10240
        RSM, _e = over(H0, ("relu_sample", [PAST + 1], F32))
        BRAW, _e = over(XR0, ("bias_raw", [AH, NEAR], F32))

        A0 = XR0 + 33024
        QPD, KNW, PSM, PTP, PTN, VN1, OSM, SMR, _e = over(
            A0, ("q_padded", [2, SB, BR], F32), ("k_new_T", [2, SB], F32), ("prob_sample", [PAST + 8], F32),
            ("prob_T", [NPG, BR], F32), ("prob_new", [BR], F32), ("v_new", [SB, UW], F32),
            ("out_by_head", [SB, UW], F32), ("sample_rows", [768], F32))
        assert _e <= XR0 + 66048
        S0T, VBT, QHP, _e = over(H0, ("state_in", [SB, NG, HD], F32), ("v_spread", [SB, NG, HD], F32),
                                 ("hq_padded", [SB * NG, BR], F32))
        HOSM, _e = over(_e, ("ho_sample", [HD], F32))
        assert _e <= cur[0], (_e, cur[0])
        HOR, HGR, AGR, MIX, _e = over(S0, ("ho_in", [2, 512], F32), ("hgate_in", [2, 512], F32),
                                      ("agate_in", [2, 512], F32), ("mix", [2, D], F32))
        SQM, XRS, YST, _e = over(_e, ("mix_sq", [512], F32), ("x_res", [2, UW], F32), ("y_rows", [2, UW], F32))
        assert _e <= R0_ + 8192, (_e, R0_)

        PSA = ctx.enter_context(nc.psum_tensor("psum", [P, 8 * 512], F32))

        def ps(bank, n=512, r=P, r0=0, o=0):
            return PSA[r0:r, bank * 512 + o:bank * 512 + o + n]

        d_q = nc.dram_tensor("q_spill", [TT, 512], F32).ap()
        d_ho = nc.dram_tensor("ho_spill", [TT, 512], F32).ap()
        d_gh = nc.dram_tensor("hgate_spill", [TT, 512], F32).ap()
        d_ga = nc.dram_tensor("agate_spill", [TT, 512], F32).ap()
        d_hv = nc.dram_tensor("hv_spill", [SB, 512], F32)
        d_ut = nc.dram_tensor("bias_spill", [AH, UL], F32)
        d_ao = nc.dram_tensor("attn_sample_spill", [SB, 512], F32).ap()

        s = {}

        class Sems(dict):
            def __missing__(self, name):
                self[name] = sem(name)
                return self[name]

        s = Sems()

        block = ctx.enter_context(nc.Block())

        def dup(ap):
            return bass.AP(ap.tensor, ap.offset, [ap.ap[0], [0, 2], ap.ap[1]])

        def bc(ap, n):
            return bass.AP(ap.tensor, ap.offset, list(ap.ap) + [[0, n]])

        def rep(ap, n):
            return bass.AP(ap.tensor, ap.offset, [ap.ap[0], [0, n]] + list(ap.ap[1:]))

        def f(ap):
            return ap.bitcast(F32)

        def x_rows(i):
            return x_prompt[0, i * P:(i + 1) * P, :] if i < NT else x_sample[:, 0, :]


        OH, REL, _ = over(ST_OFF, ("bucket_of_distance", [UL], F32), ("rel_bias", [AH], F32))

        def row0(i):
            return min(i, NT) * P

        JUNKB = 7

        ALLS = [sum(1 for g in range((NT + 1) * len(STG_UNITS)) if g % 2 == x) * 16 for x in range(2)]
        ALLN = [sum(1 for g in range((NT + 1) * len(NORMED)) if g % 2 == x) * 16 for x in range(2)]
        NA = NT * AH
        BUILD = {0: [0, 1]}
        for t in range(1, NT):
            BUILD[AH * (t - 1) + 3] = [2 * t]
            BUILD[AH * (t - 1) + 5] = [2 * t + 1]

        def load_weights(sp, u):
            w = width(u)
            for h in range(2):
                n = 2 * u + h
                ge(sp, s["wl_done"], n - 1)
                src = w_ix[h] if u == UIX else w_main[u if u < UIX else u - 1, h]
                sp.dma_start(WR[:, h, :, 0:w], src).then_inc(s[f"w_in{h}"], 16)


        def split_w(gp, u):
            w = width(u)
            for h in range(2):
                gp.wait_ge(s[f"w_in{h}"], 16 * (u + 1))
                if u < NU:
                    for k in range(4):
                        last = gp.tensor_scalar(WR[:, h, k, 0:w], WR[:, h, k, 0:w],
                                                LNG[:, 4 * h + k:4 * h + k + 1], 1.0, ALU.mult, ALU.mult)
                    last.then_inc(s["wg_done"], 1)
            if u < NU:
                gp.wait_ge(s["wg_done"], 2 * u + 2)
            for h in range(2):
                gp.wait_ge(s["wh_done"], 2 * u + h + 1)
                gp.tensor_tensor(WL[:, u % 2, 4 * h:4 * h + 4, 0:w], WR[:, h, :, 0:w],
                                 f(WH[:, u % 2, 4 * h:4 * h + 4, 0:w]), ALU.subtract)\
                    .then_inc(s["wl_done"], 1)


        def sp_tail(sp):
            sp.wait_ge(s["unit_pe"], NU)
            sp.wait_ge(s["tab_out"], 16)
            sp.dma_start(BRAW[:, :, :], bass.AP(d_ut, 0, [[1, P], [UL, AH], [1, NEAR]]))\
                .then_inc(s["braw_in"], 16)
            for x in range(2):
                sp.wait_ge(s[f"stg_out{x}"], ALLS[x])
                sp.wait_ge(s[f"nq_out{x}"], ALLN[x])
            sp.dma_start(VT[:, :, :], v_prompt[0, 0].rearrange("(t p) h d -> p t (h d)", p=P)).then_inc(s["kv_in"], 16)

            def load_rows(i):
                ge(sp, s["b_pe"], 2 * (i - 1))
                sl = i % 2
                kp = k_prompt[0, 0, i * P:(i + 1) * P]
                for x in range(2):
                    sp.dma_start(KR[:, sl, :, x, :], kp).then_inc(s[f"qr_in{sl}"], 16)
                sp.dma_start(QR[:, sl, :], d_q[i * P:(i + 1) * P, :]).then_inc(s[f"qr_in{sl}"], 16)

            for i in range(3):
                load_rows(i)
            sp.wait_ge(s["out_done"], 64)
            sp.dma_start(S0T[:, :, :, :], state.rearrange("a k b j v -> (a k) b j v")).then_inc(s["h0_in"], 16)
            sp.wait_ge(s["hv_out"], 32)
            for hh in range(2):
                for b in range(SB):
                    sp.dma_start(VBT[hh * HD:(hh + 1) * HD, b, :, :],
                                 bass.AP(d_hv, b * 512 + hh * HD, [[0, HD], [P, NG], [1, HD]])).then_inc(s["h0_in"], 16)
            for i in range(3, NT):
                load_rows(i)
            sp.wait_ge(s["hs_gp"], 1)
            for hh in range(2):
                for b in range(SB):
                    sp.dma_start(s_sample[0, b].rearrange("(j a) k v -> a k j v", a=2)[hh],
                                 S0T[hh * HD:(hh + 1) * HD, b, :, :]).then_inc(s["hso_out"], 16)
            sp.wait_ge(s["s_pe"], NA)
            sp.dma_start(SMR[0:SB, 0:512], d_q[T:TT, :]).then_inc(s["sm_in"], 16)
            sp.dma_start(SMR[0:SB, 512:768], k_sample[0, :, 0].rearrange("b h d -> b (h d)")).then_inc(s["sm_in"], 16)
            sp.dma_start(VN1[0:1, :, :], v_sample[:, :, 0].rearrange("a b h d -> a b (h d)")).then_inc(s["sm_in"], 16)

            def load_pages(b, dst, src, name, done):
                if b >= 2:
                    sp.wait_ge(s[done], b - 1)
                for g in range(NPG):
                    page = sp.value_load(PT_[0:1, b * NPG + g:b * NPG + g + 1], min_val=0, max_val=NPOOL - 1)
                    if name == "kc_in":
                        sp.dma_start(dst[:, b % 2, :, g * P:(g + 1) * P],
                                     src[bass.ds(page, 1)].rearrange("a d j k -> (a d) j k")).then_inc(s[f"{name}{b % 2}"], 16)
                    else:
                        sp.dma_start(dst[:, b % 2, g, :], src[bass.ds(page, 1)].rearrange("a k n -> (a k) n"))\
                            .then_inc(s[f"{name}{b % 2}"], 16)

            for b in range(2):
                load_pages(b, KS_, cache_kt, "kc_in", "ks_pe")
            for b in range(2):
                load_pages(b, VS_, cache_v, "vc_in", "vs_pe")
            for b in range(2, SB):
                load_pages(b, KS_, cache_kt, "kc_in", "ks_pe")
            for b in range(2, SB):
                load_pages(b, VS_, cache_v, "vc_in", "vs_pe")
            for u in (NU, NU + 1):
                load_weights(sp, u)

            def load_mix(i):
                ge(sp, s["mix_done"], i - 1)
                for dst, src in ((HOR, d_ho), (HGR, d_gh), (AGR, d_ga)):
                    sp.dma_start(dst[0:rows(i), i % 2, :], src[row0(i):row0(i) + rows(i), :])\
                        .then_inc(s[f"mix_in{i % 2}"], 16)

            sp.wait_ge(s["ks_pe"], SB)
            sp.wait_ge(s["ho_out"], 16 * NG)
            load_mix(0)
            load_mix(1)
            sp.wait_ge(s["vs_act"], 1)
            for kv in range(KVH):
                sp.dma_start(d_ao.rearrange("b (k g d) -> k g b d", g=2, d=HD)[kv],
                             OSM[2 * kv:2 * kv + 2, :, kv * HD:(kv + 1) * HD]).then_inc(s["aos_out"], 16)
            sp.wait_ge(s["aos_out"], 64)
            sp.dma_start(AO[0:SB, NT, :], d_ao).then_inc(s["aos_in"], 16)
            sp.wait_ge(s["hs_act"], 1)
            sp.dma_start(d_ho[T:TT, :].rearrange("b (h v) -> (b h) v", v=HD), HOSM[0:BR, :]).then_inc(s["ho_out"], 16)
            sp.wait_ge(s["ho_out"], 16 * (NG + 1))
            for i in range(2, NT + 1):
                load_mix(i)
            NY = NUO * (NT + 1)

            def y_part(n, a, b):
                u, i = n // (NT + 1), n % (NT + 1)
                c = slice(u * UW, (u + 1) * UW)
                return a[0, i * P:(i + 1) * P, c] if i < NT else b[:, 0, c]

            def load_res(n):
                ge(sp, s["y_add"], n - 1)
                sp.dma_start(XRS[0:rows(n % (NT + 1)), n % 2, :], y_part(n, x_prompt, x_sample))\
                    .then_inc(s[f"xr_in{n % 2}"], 16)

            load_res(0)
            load_res(1)
            for n in range(NY):
                if n % (NT + 1) == 4 and n // (NT + 1) + 2 < NUO:
                    load_weights(sp, NU + n // (NT + 1) + 2)
                sp.wait_ge(s["y_add"], n + 1)
                sp.dma_start(y_part(n, y_prompt, y_sample), YST[0:rows(n % (NT + 1)), n % 2, :])\
                    .then_inc(s[f"y_out{n % 2}"], 16)
                if n + 2 < NY:
                    load_res(n + 2)
            sp.wait_ge(s["y_out0"], NY * 8)
            sp.wait_ge(s["y_out1"], NY * 8)
            sp.wait_ge(s["hso_out"], 16 * 2 * SB)

        def gp_tail(gp, link):
            gp.wait_ge(s["h0_in"], 16 * (1 + 2 * SB))

            def spread(x):
                return bass.AP(x, 0, [[NG * SB, P], [1, SB], [SB, NG], [0, HD]])

            link(gp.tensor_tensor(S0T[:, :, :, :], S0T[:, :, :, :], spread(FS), ALU.mult))
            link(gp.tensor_tensor(VBT[:, :, :, :], VBT[:, :, :, :], spread(KSS), ALU.mult))
            gp.tensor_tensor(S0T[:, :, :, :], S0T[:, :, :, :], VBT[:, :, :, :], ALU.add).then_inc(s["hs_gp"], 1)
            link(gp.memset(QHP[:, :, :], 0.0))
            w = SB * NG * BR
            for hh in range(2):
                link(gp.tensor_scalar(bass.AP(QHP, hh * HD * w + hh, [[w, HD], [NG * BR + 8, SB], [BR + 2, NG]]),
                                      bass.AP(QSS, hh * HD * NG * SB, [[NG * SB, HD], [1, SB], [SB, NG]]),
                                      1.0, 0.0, ALU.mult, ALU.add))
            gp.wait_ge(s["hs_gp"], 1)
            gp.wait_ge(s["s_pe"], NA)
            gp.memset(QPD[:, :, :, :], 0.0).then_inc(s["hs_gp"], 1)
            def gain(i):
                r = rows(i)
                gp.wait_ge(s[f"mix_in{i % 2}"], 48 * (i // 2 + 1))
                hg = HGR[0:r, i % 2, :].rearrange("p (h d) -> p h d", d=HD)
                gp.tensor_tensor(hg, hg, rep(HNG[0:r, :], HH), ALU.mult).then_inc(s["mix_g"], 1)

            split_w(gp, NU)
            split_w(gp, NU + 1)
            for i in range(NT + 1):
                gain(i)
            split_w(gp, NU + 2)
            split_w(gp, NU + 3)

        def act_tail(act, link, high_w):
            act.wait_ge(s["unit_pe"], NU)
            act.wait_ge(s["braw_in"], 16)
            act.activation(BH[:, :, :], BRAW[:, :, :], ACT.Copy).then_inc(s["br_h"], 1)

            def build(n):
                i = n // 2
                c = slice(i * P, (i + 1) * P)
                lo, hi = ps(6, 512, HD).rearrange("p (j t) -> p j t", t=P), ps(6, 512, P, HD).rearrange("p (j t) -> p j t", t=P)
                if n == 0:
                    act.wait_ge(s["br_l"], 1)
                act.wait_ge(s["b_pe"], n + 1)
                if n % 2 == 0:
                    act.activation(KA[0:HD, :, c], lo, ACT.Copy)
                    act.activation(KB[HD:P, :, c], hi, ACT.Copy).then_inc(s["b_h"], 1)
                else:
                    act.activation(QS[0:HD, 0:AH:2, c], lo, ACT.Copy)
                    act.activation(QS[HD:P, 1:AH:2, c], hi, ACT.Copy).then_inc(s["b_h"], 1)

            for m in range(NA + 1):
                for n in BUILD.get(m, []):
                    build(n)
                if m < NA:
                    t, h = m // AH, m % AH
                    w = P * (t + 1)
                    act.wait_ge(s["s_max"], m + 1)
                    ge(act, s["p_pe"], m - 2)
                    act.activation(PB[:, m % 3, 0:w], ps(2 * (m % 2), w), ACT.Exp, scale=HD ** -0.5, bias=NB[:, h:h + 1],
                                   accum_out=RS[:, t % 2, h:h + 1]).then_inc(s["s_exp"], 1)
                m1 = m - 1
                if m1 >= 0 and m1 % 2 == 0:
                    w = P * (m1 // AH + 1)
                    act.wait_ge(s["p_pe"], m1 + 1)
                    ge(act, s["v_pe"], m1 - 1)
                    act.activation(PTS[:, m1 % 2, :, :].rearrange("p b t -> p (b t)")[:, 0:w], ps(4, w), ACT.Copy)\
                        .then_inc(s["p_act"], 1)
            act.wait_ge(s["sm_pe"], 1)
            act.wait_ge(s["hs_gp"], 2)
            qpd = QPD[:, :, :, :].rearrange("p a b n -> p (a b n)")
            for blk in range(2):
                act.activation(KNW[:, blk, :], ps(6, SB, o=32 + 8 * blk), ACT.Copy)
                for kv2 in range(2):
                    for g in range(2):
                        o = 512 * blk + 4 * blk + 2 * kv2 + g
                        last = act.activation(qpd[kv2 * HD:(kv2 + 1) * HD, o:512 * (blk + 1):BR + 8],
                                              ps(6, SB, (g + 1) * HD, g * HD, 8 * (2 * blk + kv2)), ACT.Copy)
            last.then_inc(s["sm_act"], 1)
            act.wait_ge(s["ks_max"], 1)
            act.activation(PSM[0:BR, 0:PAST + 1], ps(0, PAST + 1, BR), ACT.Exp, scale=HD ** -0.5, bias=NB[0:BR, 0:1],
                           accum_out=RS[0:BR, 0, 0:1]).then_inc(s["ks_exp"], 1)
            act.wait_ge(s["pt_pe"], 1)
            act.activation(PTP[:, :, :], ps(4, 512).rearrange("p (g n) -> p g n", n=BR), ACT.Copy)
            act.activation(PTN[0:1, :], ps(5, BR, 1), ACT.Copy).then_inc(s["pt_act"], 1)
            act.wait_ge(s["hs_pe"], 1)
            act.activation(HOSM[0:BR, :], ps(6, HD, BR, o=256), ACT.Copy).then_inc(s["hs_act"], 1)
            act.wait_ge(s["vs_pe"], SB)
            act.activation(OSM[0:SB, :, :].rearrange("p b n -> p (b n)"), ps(0, 4 * 512, SB), ACT.Copy)\
                .then_inc(s["vs_act"], 1)
            high_w(NU)
            high_w(NU + 1)

            def mix_square(i):
                r = rows(i)
                act.wait_ge(s[f"mix_in{i % 2}"], 48 * (i // 2 + 1))
                ge(act, s["mix_sum"], i)
                act.activation(SQM[0:r, :], HOR[0:r, i % 2, :], ACT.Square).then_inc(s["mix_ss"], 1)
                act.wait_ge(s["mix_sum"], i + 1)
                link(act.activation(MN[0:r, 1, i % 2, :], MN[0:r, 0, i % 2, :], ACT.Ln, scale=1.0 / HD, bias=EPSC[0:r, 0:1]))
                act.activation(MN[0:r, 1, i % 2, :], MN[0:r, 1, i % 2, :], ACT.Exp, scale=-0.5).then_inc(s["mix_rs"], 1)

            def mix_high(i):
                if i == 0:
                    act.wait_ge(s["aos_out"], 64)
                for h in range(2):
                    n = 2 * i + h
                    act.wait_ge(s["mt_pe"], n + 1)
                    src = ps(6 + n % 2).rearrange("p (k t) -> p k t", t=P)[:, :, 0:rows(i)]
                    act.activation(XH[:, 4 * h:4 * h + 4, row0(i):row0(i) + rows(i)], src, ACT.Copy)\
                        .then_inc(s["mt_h"], 1)

            mix_square(0)
            for i in range(NT + 1):
                if i < NT:
                    mix_square(i + 1)
                mix_high(i)
            high_w(NU + 2)
            high_w(NU + 3)

        def dve_tail(dve, link):
            dve.wait_ge(s["br_h"], 1)
            dve.tensor_tensor(BL[:, :, :], BRAW[:, :, :], f(BH[:, :, :]), ALU.subtract).then_inc(s["br_l"], 1)

            def build(n):
                i = n // 2
                c = slice(i * P, (i + 1) * P)
                lo, hi = ps(6, 512, HD).rearrange("p (j t) -> p j t", t=P), ps(6, 512, P, HD).rearrange("p (j t) -> p j t", t=P)
                dve.wait_ge(s["b_h"], n + 1)
                if n % 2 == 0:
                    dve.tensor_tensor(KB[0:HD, :, c], lo, f(KA[0:HD, :, c]), ALU.subtract)
                    dve.tensor_tensor(KA[HD:P, :, c], hi, f(KB[HD:P, :, c]), ALU.subtract).then_inc(s["b_l"], 1)
                else:
                    dve.tensor_tensor(QS[HD:P, 0:AH:2, c], lo, f(QS[0:HD, 0:AH:2, c]), ALU.subtract)
                    dve.tensor_tensor(QS[0:HD, 1:AH:2, c], hi, f(QS[HD:P, 1:AH:2, c]), ALU.subtract)\
                        .then_inc(s["b_l"], 1)

            for m in range(NA + 2):
                for n in BUILD.get(m, []):
                    build(n)
                if m < NA:
                    t, h = m // AH, m % AH
                    dve.wait_ge(s["s_pe"], m + 1)
                    link(dve.reduce_max(MX[:, h:h + 1], ps(2 * (m % 2), P * (t + 1)), axis=AX.X))
                    dve.tensor_scalar(NB[:, h:h + 1], MX[:, h:h + 1], -HD ** -0.5, None, ALU.mult).then_inc(s["s_max"], 1)
                m1 = m - 1
                if 0 <= m1 < NA and m1 % 2 == 1:
                    w = P * (m1 // AH + 1)
                    dve.wait_ge(s["p_pe"], m1 + 1)
                    ge(dve, s["v_pe"], m1 - 1)
                    dve.tensor_copy(PTS[:, m1 % 2, :, :].rearrange("p b t -> p (b t)")[:, 0:w], ps(4, w))\
                        .then_inc(s["p_dve"], 1)
                m2 = m - 2
                if m2 >= 0 and m2 % AH == AH - 1:
                    t = m2 // AH
                    dve.wait_ge(s["v_pe"], m2 + 1)
                    dve.wait_ge(s["s_exp"], m2 + 1)
                    link(dve.reciprocal(RI[:, :], RS[:, t % 2, :]))
                    dve.tensor_tensor(AO[:, t, :].rearrange("p (h d) -> p h d", d=HD),
                                      ps(7).rearrange("p (h d) -> p h d", d=HD), bc(RI[:, :], HD), ALU.mult)\
                        .then_inc(s["ao_done"], 1)
            dve.wait_ge(s["ks_pe"], SB)
            link(dve.reduce_max(MX[0:BR, 0:1], ps(0, PAST + 1, BR), axis=AX.X))
            dve.tensor_scalar(NB[0:BR, 0:1], MX[0:BR, 0:1], -HD ** -0.5, None, ALU.mult).then_inc(s["ks_max"], 1)
            dve.wait_ge(s["ks_exp"], 1)
            link(dve.reciprocal(RI[0:BR, 0:1], RS[0:BR, 0, 0:1]))
            dve.tensor_scalar(PSM[0:BR, 0:PAST + 1], PSM[0:BR, 0:PAST + 1], RI[0:BR, 0:1], None, ALU.mult)\
                .then_inc(s["ks_norm"], 1)

            def mix_sum(i):
                r = rows(i)
                dve.wait_ge(s["mix_ss"], i + 1)
                dve.reduce_sum(MN[0:r, 0, i % 2, :], SQM[0:r, :].rearrange("p (h d) -> p h d", d=HD), axis=AX.X)\
                    .then_inc(s["mix_sum"], 1)

            def mix_rows(i):
                r, sl = rows(i), i % 2
                ge(dve, s["mt_pe"], 2 * (i - 1))
                dve.wait_ge(s["mix_rs"], i + 1)
                ho = HOR[0:r, sl, :].rearrange("p (h d) -> p h d", d=HD)
                link(dve.tensor_tensor(ho, ho, bc(MN[0:r, 1, sl, :], HD), ALU.mult))
                dve.wait_ge(s["mix_g"], i + 1)
                link(dve.tensor_tensor(MIX[0:r, sl, 512:1024], HOR[0:r, sl, :], HGR[0:r, sl, :], ALU.mult))
                if i == NT:
                    dve.wait_ge(s["aos_in"], 16)
                dve.tensor_tensor(MIX[0:r, sl, 0:512], AO[0:r, i, :], AGR[0:r, sl, :], ALU.mult)\
                    .then_inc(s["mix_done"], 1)

            def mix_low(i):
                for h in range(2):
                    n = 2 * i + h
                    dve.wait_ge(s["mt_h"], n + 1)
                    src = ps(6 + n % 2).rearrange("p (k t) -> p k t", t=P)[:, :, 0:rows(i)]
                    c = slice(row0(i), row0(i) + rows(i))
                    dve.tensor_tensor(XL[:, 4 * h:4 * h + 4, c], src, f(XH[:, 4 * h:4 * h + 4, c]), ALU.subtract)\
                        .then_inc(s["mt_l"], 1)

            mix_sum(0)
            mix_rows(0)
            for i in range(NT + 1):
                if i < NT:
                    mix_sum(i + 1)
                    mix_rows(i + 1)
                mix_low(i)
            for n in range(NUO * (NT + 1)):
                r = rows(n % (NT + 1))
                dve.wait_ge(s["job_pe"], JOB0[NU] + n + 1)
                dve.wait_ge(s[f"xr_in{n % 2}"], 16 * (n // 2 + 1))
                ge(dve, s[f"y_out{n % 2}"], 16 * (n // 2))
                dve.tensor_tensor(YST[0:r, n % 2, :], ps((JOB0[NU] + n) % PJ, UW, r), XRS[0:r, n % 2, :], ALU.add)\
                    .then_inc(s["y_add"], 1)

        def pe_tail(pe, unit):
            def build(n):
                i, sl = n // 2, (n // 2) % 2
                pe.wait_ge(s[f"qr_in{sl}"], 48 * (i // 2 + 1))
                ge(pe, s["b_l"], n)
                for j in range(4):
                    src = KR[:, sl, j, :, :].rearrange("p a d -> p (a d)") if n % 2 == 0 else QR[:, sl, j * P:(j + 1) * P]
                    last = pe.transpose(ps(6, P, o=j * P), src, IDN[:, :])
                last.then_inc(s["b_pe"], 1)

            def scores(m):
                t, h = m // AH, m % AH
                w = P * (t + 1)
                for n in BUILD.get(m, []):
                    build(n)
                if h == 0:
                    pe.wait_ge(s["b_l"], 2 * (t + 1))
                    if t >= 2:
                        pe.wait_ge(s["masks"], t - 1)
                ge(pe, s["s_exp"], m - 1)
                bank = 2 * (m % 2)
                q = QS[:, h, t * P:(t + 1) * P]
                for c0 in range(0, w, 512):
                    n = min(512, w - c0)
                    pe.matmul(ps(bank, n, o=c0), q, KA[:, h // 2, c0:c0 + n], start=True, stop=False)
                    for kb in (t - 1, t):
                        if kb >= 0 and c0 <= kb * P < c0 + n:
                            for half in (BH, BL):
                                pe.matmul(ps(bank, P, o=kb * P), ANR[:, :], half[:, h, (kb - t + 1) * P:(kb - t + 2) * P],
                                          start=False, stop=False)
                    if t >= 2:
                        pe.matmul(ps(bank, n, o=c0), IDB[:, :], MSK[:, 2 * SC0[t] + c0:2 * SC0[t] + c0 + n],
                                  start=False, stop=False)
                    elif c0 <= t * P < c0 + n:
                        pe.matmul(ps(bank, P, o=t * P), IDB[:, :], TRI[:, :], start=False, stop=False)
                    last = pe.matmul(ps(bank, n, o=c0), q, KB[:, h // 2, c0:c0 + n], start=False, stop=True)
                last.then_inc(s["s_pe"], 1)

            def evacuated(m):
                pe.wait_ge(s["p_dve" if m % 2 else "p_act"], m // 2 + 1)

            def transposes(m):
                pe.wait_ge(s["s_exp"], m + 1)
                if m >= 1:
                    evacuated(m - 1)
                for b in range(m // AH + 1):
                    last = pe.transpose(ps(4, P, o=b * P), PB[:, m % 3, b * P:(b + 1) * P], IDN[:, :])
                last.then_inc(s["p_pe"], 1)

            def values(m):
                t, h = m // AH, m % AH
                evacuated(m)
                if h == 0:
                    ge(pe, s["ao_done"], t)
                for b in range(t + 1):
                    last = pe.matmul(ps(7, HD, o=h * HD), PTS[:, m % 2, b, :], VT[:, b, h // 2 * HD:(h // 2 + 1) * HD],
                                     start=b == 0, stop=b == t)
                last.then_inc(s["v_pe"], 1)

            pe.wait_ge(s["kv_in"], 16)
            scores(0)
            for m in range(NA):
                if m + 1 < NA:
                    scores(m + 1)
                transposes(m)
                if m >= 1:
                    values(m - 1)
            values(NA - 1)
            pe.wait_ge(s["sm_in"], 48)
            for j in range(6):
                last = pe.transpose(ps(6, SB, o=8 * j), SMR[0:SB, j * P:(j + 1) * P], IDN[0:SB, 0:SB])
            last.then_inc(s["sm_pe"], 1)
            pe.wait_ge(s["sm_act"], 1)
            pe.wait_ge(s["masks"], 7)
            for b in range(SB):
                pe.wait_ge(s[f"kc_in{b % 2}"], 128 * (b // 2 + 1))
                for blk in range(2):
                    q = QPD[:, blk, b, :]
                    first, final = b == 0 and blk == 0, b == SB - 1 and blk == 1
                    for c in range(2):
                        pe.matmul(ps(c, 512, BR), q, KS_[:, b % 2, blk, c * 512:(c + 1) * 512], start=first, stop=final)
                    last = pe.matmul(ps(2, 1, BR), q, KNW[:, blk, b:b + 1], start=first, stop=final)
                    if first:
                        for c, w in ((0, 512), (1, 512), (2, 1)):
                            pe.matmul(ps(c, w, BR), E8B[0:8, :], MSKS[0:8, c * 512:c * 512 + w], start=False, stop=False)
                        pe.matmul(ps(1, P, BR, o=512 - P), E8H[0:8, :], UT[0:8, P - 1:2 * P - 1], start=False, stop=False)
                        pe.matmul(ps(2, 1, BR), E8H[0:8, :], UT[0:8, 2 * P - 1:2 * P], start=False, stop=False)
                last.then_inc(s["ks_pe"], 1)
            pe.wait_ge(s["ks_norm"], 1)
            for g in range(NPG):
                pe.transpose(ps(4, BR, o=g * BR), PSM[0:BR, g * P:(g + 1) * P], IDN[0:BR, 0:BR])
            pe.transpose(ps(5, BR, 1), PSM[0:BR, PAST:PAST + 1], IDN[0:BR, 0:BR]).then_inc(s["pt_pe"], 1)
            for n in range(SB * NG):
                last = pe.matmul(ps(6, HD, BR, o=256), QHP[:, n, :], S0T[:, n // NG, n % NG, :], start=n == 0,
                                 stop=n == SB * NG - 1)
            last.then_inc(s["hs_pe"], 1)
            pe.wait_ge(s["pt_act"], 1)
            for b in range(SB):
                pe.wait_ge(s[f"vc_in{b % 2}"], 128 * (b // 2 + 1))
                dst = ps(b // 2, UW, SB, o=b % 2 * UW)
                for g in range(NPG):
                    pe.matmul(dst, PTP[:, g, 8 * b:8 * b + 8], VS_[:, b % 2, g, :], start=g == 0, stop=False)
                pe.matmul(dst, PTN[0:1, 8 * b:8 * b + 8], VN1[0:1, b, :], start=False, stop=True).then_inc(s["vs_pe"], 1)
            pe.wait_ge(s["hs_act"], 1)
            for i in range(NT + 1):
                pe.wait_ge(s["mix_done"], i + 1)
                for h in range(2):
                    n = 2 * i + h
                    ge(pe, s["mt_l"], n - 1)
                    for k in range(4):
                        last = pe.transpose(ps(6 + n % 2, rows(i), o=k * P), MIX[0:rows(i), i % 2, (4 * h + k) * P:(4 * h + k + 1) * P],
                                            IDN[0:rows(i), 0:rows(i)])
                    last.then_inc(s["mt_pe"], 1)
            pe.wait_ge(s["vs_act"], 1)
            for u in range(NU, NU + NUO):
                unit(u)

        @block.sync
        def _(sp):
            for dst, src in ((IDN[:, :], c_ident), (LNG[:, :], ln_g), (LBR[:, :, :], lbs), (BITF[:, :], c_bits),
                             (QG[:, :], q_g), (KG[:, :], k_g), (HNG[:, :], hn_g), (PT_[0:1, :], pages),
                             (E8[0:8, :], c_e8[0]), (E8H[0:8, :], c_e8[1]), (OH[0:32, :], c_oh), (REL[0:32, :], rel),
                             (INM[:, :, :], c_masks[:, 0:256]), (BM[:, :], c_masks[:, 256:384]),
                             (HM[0:BR, :], c_masks[0:BR, 384:400]), (TRF[:, :], c_masks[:, 400:528]), (ANT[:, :], c_masks[:, 528:656])):
                sp.dma_start(dst, src).then_inc(s["const_in"], 16)
            NCONST = 17 * 16

            def load_x(g):
                for i in range(3 * g, 3 * g + 3):
                    if i >= 6:
                        ge(sp, s["xt_t"], 2 * (i - 5))
                    sp.dma_start(XB[0:rows(i), i % 6, :], x_rows(i)).then_inc(s[f"x_in{g}"], 16)

            def load_index_keys(b):
                slot = (b // 2) % 2
                if b >= 4:
                    ge(sp, s["samp_pe"], b // 2 - 1)
                for g in range(NPG):
                    page = sp.value_load(PT_[0:1, b * NPG + g:b * NPG + g + 1], min_val=0, max_val=NPOOL - 1)
                    sp.dma_start(IKT[b % 2 * HD:b % 2 * HD + HD, slot, g * P:(g + 1) * P],
                                 cache_ikt[bass.ds(page, 1)].rearrange("a d k -> (a d) k"))\
                        .then_inc(s[f"ikc_in{slot}"], 16)

            load_x(0)
            load_weights(sp, 0)
            load_x(1)
            load_weights(sp, 1)
            load_x(2)
            ge(sp, s["const_in"], NCONST)
            for b in range(4):
                load_index_keys(b)
            staged = 0
            normed = 0
            for u in range(NU):
                kind, a = UNITS[u]
                if u + 2 < NU + NUO and u + 2 < NU:
                    load_weights(sp, u + 2)
                if u == UIX:
                    ge(sp, s["job_act"], JOB0[u + 1])
                    sp.dma_start(ik_prompt[0, 0].rearrange("(t p) d -> p t d", p=P), IKN[:, 0:NT, 0, :])\
                        .then_inc(s["out_done"], 16)
                    sp.dma_start(ik_sample[0, :, 0, :], IKN[0:SB, NT, 0, :]).then_inc(s["out_done"], 16)
                    for b in range(4, SB):
                        load_index_keys(b)
                    ge(sp, s["tab_act"], 1)
                    sp.dma_start(d_ut.ap(), UT[0:AH, :]).then_inc(s["tab_out"], 16)
                for i in range(NT + 1):
                    n = JOB0[u] + i
                    if kind in STAGED:
                        ge(sp, s["stg_act"], staged + 1)
                        dst = {"gh": d_gh, "ga": d_ga}.get(kind)
                        if kind == "v":
                            dst = v_prompt[0, 0, i * P:(i + 1) * P].rearrange("t h d -> t (h d)") if i < NT \
                                else v_sample[0, :, 0].rearrange("t h d -> t (h d)")
                        else:
                            dst = dst[row0(i):row0(i) + rows(i), a * UW:(a + 1) * UW]
                        sp.dma_start(dst, STG[0:rows(i), staged % 2, :]).then_inc(s[f"stg_out{staged % 2}"], 16)
                        staged += 1
                    if u in NORMED:
                        ge(sp, s["nq_done"], normed + 1)
                        if kind == "k":
                            dst = k_prompt[0, 0, i * P:(i + 1) * P].rearrange("t h d -> t (h d)") if i < NT \
                                else k_sample[0, :, 0].rearrange("t h d -> t (h d)")
                        else:
                            dst = d_q[row0(i):row0(i) + rows(i), a * UW:(a + 1) * UW]
                        sp.dma_start(dst, NQ[0:rows(i), normed % 2, :]).then_inc(s[f"nq_out{normed % 2}"], 16)
                        normed += 1
                if kind == "hv":
                    ge(sp, s["job_act"], JOB0[u + 1])
                    sp.dma_start(d_hv.ap()[:, a * UW:(a + 1) * UW], HV[0:SB, NT, a * UW:(a + 1) * UW])\
                        .then_inc(s["hv_out"], 16)
                if u in HUNIT:
                    j = HUNIT[u]
                    ge(sp, s["o_act"], NT * (j + 1))
                    sp.dma_start(d_ho[0:T, j * P:(j + 1) * P].rearrange("(c s) n -> s c n", s=P), HO[:, :, :])\
                        .then_inc(s["ho_out"], 16)
            ge(sp, s["st_gp"], NT * NG)
            for hh in range(2):
                sp.dma_start(s_prompt[0, 0].rearrange("(j a) k v -> a k j v", a=2)[hh],
                             ST[hh * HD:(hh + 1) * HD, :, hh * HD:(hh + 1) * HD]).then_inc(s["out_done"], 16)
            sp_tail(sp)

        @block.gpsimd
        def _(gp):
            chain = [0]

            def link(ins):
                chain[0] += 1
                ins.then_inc(s["gp_chain"], 1)
                gp.wait_ge(s["gp_chain"], chain[0])

            gp.memset(IQP[:, :, :], 0.0).then_inc(s["init_gp"], 1)
            gp.memset(RM[:, :], 1.0).then_inc(s["init_gp"], 1)
            gp.wait_ge(s["init_gp"], 2)
            gp.memset(RM[:, 0:T:P], 0.0).then_inc(s["init_gp"], 1)
            gp.wait_ge(s["const_in"], NCONST_)

            def prep(j):
                u = HGU[j]
                gp.wait_ge(s["job_act"], JOB0[u + 1])
                if j == 0:
                    gp.wait_ge(s["lb_done"], 1)
                gp.tensor_scalar(FB[:, :], FB[:, :], OML[:, j:j + 1], LB[:, j:j + 1], ALU.mult, ALU.add)\
                    .then_inc(s["f_gp"], 1)
                gp.tensor_scalar(FS[:, j, :], FS[:, j, :], OML[:, j:j + 1], LB[:, j:j + 1], ALU.mult, ALU.add)\
                    .then_inc(s["f_gp"], 1)
                gp.tensor_scalar(QB[:, :], QB[:, :], HD ** -0.5, 0.0, ALU.mult, ALU.add).then_inc(s["f_gp"], 1)
                gp.tensor_scalar(QSS[:, j, :], QSS[:, j, :], HD ** -0.5, 0.0, ALU.mult, ALU.add)\
                    .then_inc(s["f_gp"], 1)
                gp.wait_ge(s["f_gp"], 6 * j + 4)
                gp.tensor_scalar(HK[:, :], FB[:, :], -1.0, 1.0, ALU.mult, ALU.add).then_inc(s["f_gp"], 1)
                gp.tensor_scalar(KSS[:, j, :], FS[:, j, :], -1.0, 1.0, ALU.mult, ALU.add).then_inc(s["f_gp"], 1)
                gp.wait_ge(s["scan_done"], j + 1)
                ge(gp, s["o_pe"], NT * j)
                ge(gp, s["st_gp"], NT * j)
                b4 = FB[:, :].rearrange("p (n t) -> p n t", t=SUB)
                ref = b4[:, :, SUB // 2 - 1]
                for hh in range(2):
                    r = slice(hh * HD, hh * HD + HD)
                    link(gp.tensor_tensor(QT[r, hh, :].rearrange("p (n t) -> p n t", t=SUB), b4[r],
                                          bc(ref[r], SUB), ALU.subtract))
                b8 = FB[:, :].rearrange("p (c t) -> p c t", t=P)
                o = 0
                for i in range(NSUB):
                    w = SUB * (i + 1)
                    gp.tensor_tensor(KT[:, o:o + NT * w].rearrange("p (c t) -> p c t", t=w),
                                     bc(ref[:, i:NT * NSUB:NSUB], w), b8[:, :, 0:w], ALU.subtract)
                    o += NT * w
                gp.tensor_tensor(DE[:, 1, :], b8[:, :, P - 1], ref[:, NSUB - 1:NT * NSUB:NSUB], ALU.subtract)
                gp.tensor_scalar(DE[:, 0, :], b8[:, :, P - 1], 1.0, 0.0, ALU.mult, ALU.add).then_inc(s["d_gp"], 1)
                gp.wait_ge(s["e_act"], j + 1)
                for hh in range(2):
                    r = slice(hh * HD, hh * HD + HD)
                    link(gp.tensor_tensor(QT[r, hh, :], QT[r, hh, :], QB[r, :], ALU.mult))
                gp.tensor_tensor(QI[:, :], QI[:, :], QB[:, :], ALU.mult)
                k8 = HK[:, :].rearrange("p (c t) -> p c t", t=P)
                o = 0
                for i in range(NSUB):
                    w = SUB * (i + 1)
                    kt = KT[:, o:o + NT * w].rearrange("p (c t) -> p c t", t=w)
                    last = gp.tensor_tensor(kt, kt, k8[:, :, 0:w], ALU.mult)
                    o += NT * w
                last.then_inc(s["prep_done"], 1)

            def chunk(j, c):
                n = NT * j + c
                gp.wait_ge(s["at_act"], n + 1)
                gp.tensor_tensor(ATB[:, n % 2], ATB[:, n % 2], INM[:, :, :], ALU.mult).then_inc(s["at_gp"], 1)
                gp.wait_ge(s["u_act"], n + 1)
                gp.tensor_tensor(TMP[:, n % 2, :], TMP[:, n % 2, :], BM[:, :], ALU.mult).then_inc(s["gp_chain"], 1)
                chain[0] += 1
                gp.wait_ge(s["o_pe"], n + 1)
                link(gp.tensor_scalar(ST[:, j, :], ST[:, j, :], DE[:, 0, c:c + 1], 0.0, ALU.mult, ALU.add))
                gp.tensor_tensor(ST[:, j, :], ST[:, j, :], TMP[:, n % 2, :], ALU.add).then_inc(s["st_gp"], 1)

            def norm(r, i, gain):
                gp.wait_ge(s["nq_rs"], r + 1)
                q = NQ[0:rows(i), r % 2, :].rearrange("p (h d) -> p h d", d=HD)
                link(gp.tensor_tensor(q, q, bc(NRM[0:rows(i), 1, r % 2, :], HD), ALU.mult))
                gp.tensor_tensor(q, q, rep(gain[0:rows(i), :], 4), ALU.mult).then_inc(s["nq_done"], 1)

            split_w(gp, 0)
            normed = 0
            for u in range(NU):
                if u + 1 < NU:
                    split_w(gp, u + 1)
                if u == UIX:
                    for t in range(2, NT):
                        gp.wait_ge(s["sc_acc"], IH * (t - 1))
                        diag = SC[:, SC0[t] + P * t:SC0[t] + P * (t + 1)]
                        gp.affine_select(out=diag, in_=diag, compare_op=ALU.is_ge, fill=UNSEEN, base=0,
                                         pattern=[[-1, P]], channel_multiplier=1).then_inc(s["sc_seen"], 1)
                    gp.wait_ge(s["samp_sc"], 1)
                    gp.wait_ge(s["sc_pe"], IH * 6)
                    gp.wait_ge(s["tab_pe"], 1)
                    gp.wait_ge(s["out_done"], 32)
                    gp.memset(ATB[:, :, :, :], 0.0)
                    gp.memset(QT[:, :, :], 0.0)
                    gp.memset(ST[:, :, :], 0.0).then_inc(s["init_gp"], 1)
                    gp.wait_ge(s["init_gp"], 4)
                if u - 1 in HGU:
                    prep(HGU.index(u - 1))
                for i in range(NT + 1):
                    if u in NORMED:
                        norm(normed, i, KG if UNITS[u][0] == "k" else QG)
                        normed += 1
                    if u in HUNIT and i >= 2:
                        chunk(HUNIT[u], i - 2)
                if u in HUNIT:
                    chunk(HUNIT[u], NT - 1)
            gp_tail(gp, link)

        @block.scalar
        def _(act):
            chain = [0]

            def link(ins):
                chain[0] += 1
                ins.then_inc(s["act_chain"], 1)
                act.wait_ge(s["act_chain"], chain[0])

            act.wait_ge(s["const_in"], NCONST_)
            act.wait_ge(s["init_dve"], 2)
            act.activation(ANR[:, :], ANT[:, :], ACT.Copy)
            act.activation(IDB[:, :], IDN[:, :], ACT.Copy)
            act.activation(E8B[0:8, :], E8[0:8, :], ACT.Copy)
            act.activation(TRI[:, :], TRF[:, :], ACT.Copy).then_inc(s["init_act"], 1)
            act.activation(LB[:, :], OML[:, :], ACT.Sigmoid).then_inc(s["lb_act"], 1)

            def squares(g):
                act.wait_ge(s[f"x_in{g}"], 48)
                for i in range(3 * g, 3 * g + 3):
                    r = rows(i)
                    ge(act, s["ss_done"], i)
                    act.activation(JA[0:r, :], XB[0:r, i % 6, :], ACT.Square,
                                   accum_out=STAT[0:r, 0, i:i + 1]).then_inc(s["ss_done"], 1)

            def first_rstd(g):
                c = slice(3 * g, 3 * g + 3)
                act.wait_ge(s["var_done"], g + 1)
                link(act.activation(STAT[:, 2, c], STAT[:, 1, c], ACT.Ln))
                act.activation(STAT[:, 2, c], STAT[:, 2, c], ACT.Exp, scale=-0.5).then_inc(s["r0_done"], 1)

            def high_x(g):
                for i in range(3 * g, 3 * g + 3):
                    for h in range(2):
                        n = 2 * i + h
                        act.wait_ge(s["xt_t"], n + 1)
                        src = ps(6 + n % 2).rearrange("p (k t) -> p k t", t=P)[:, :, 0:rows(i)]
                        act.activation(XH[:, 4 * h:4 * h + 4, row0(i):row0(i) + rows(i)], src, ACT.Copy)\
                            .then_inc(s["xt_h"], 1)

            def high_w(u):
                w = width(u)
                if NU > u >= 2:
                    act.wait_ge(s["unit_pe"], u - 1)
                if u > NU + 1:
                    act.wait_ge(s["unit_pe"], u - 1)
                for h in range(2):
                    if u < NU:
                        act.wait_ge(s["wg_done"], 2 * u + h + 1)
                    else:
                        act.wait_ge(s[f"w_in{h}"], 16 * (u + 1))
                    act.activation(WH[:, u % 2, 4 * h:4 * h + 4, 0:w], WR[:, h, :, 0:w], ACT.Copy)\
                        .then_inc(s["wh_done"], 1)

            def prep_log(j):
                act.wait_ge(s["f_gp"], 6 * (j + 1))
                act.activation(FB[:, :], FB[:, :], ACT.Ln).then_inc(s["f_ln"], 1)

            def prep_exp(j):
                act.wait_ge(s["d_gp"], j + 1)
                for hh in range(2):
                    r = slice(hh * HD, hh * HD + HD)
                    act.activation(QT[r, hh, :], QT[r, hh, :], ACT.Exp)
                act.activation(QI[:, :], FB[:, :], ACT.Exp)
                act.activation(KT[:, :], KT[:, :], ACT.Exp)
                act.activation(DE[:, :, :], DE[:, :, :], ACT.Exp).then_inc(s["e_act"], 1)

            def chunk_a(j, c):
                n = NT * j + c
                act.wait_ge(s["a_pe"], n + 1)
                ge(act, s["o_pe"], n - 1)
                src = ps(6 + n % 2, 256).rearrange("p (i h t) -> p i h t", h=2, t=SUB)
                for i in range(NSUB):
                    w = SUB * (i + 1)
                    act.activation(ATB[0:w, n % 2, :, i * SUB:(i + 1) * SUB], src[0:w, i], ACT.Copy)
                act.activation(KTN[:, n % 2, :], ps(6 + n % 2, P, o=256), ACT.Copy).then_inc(s["at_act"], 1)

            def chunk_b(j, c):
                n = NT * j + c
                act.wait_ge(s["u_pe"], n + 1)
                ge(act, s["st_gp"], n - 1)
                act.activation(TMP[:, n % 2, :], ps(5, P), ACT.Copy, scale=DE[:, 1, c:c + 1])\
                    .then_inc(s["u_act"], 1)
                act.wait_ge(s["o_pe"], n + 1)
                if c == 0:
                    ge(act, s["ho_out"], 16 * j)
                act.activation(HO[:, c, :], ps(4, P), ACT.Copy).then_inc(s["o_act"], 1)

            staged = [0]
            normed = [0]

            def rstd_of(r):
                act.activation(NRM[:, 1, r % 2, :], NRM[:, 0, r % 2, :], ACT.Ln, scale=1.0 / HD, bias=EPSC[:, 0:1])\
                    .then_inc(s["act_chain"], 1)
                chain[0] += 1
                act.wait_ge(s["act_chain"], chain[0])
                act.activation(NRM[:, 1, r % 2, :], NRM[:, 1, r % 2, :], ACT.Exp, scale=-0.5)\
                    .then_inc(s["nq_rs"], 1)

            def evac(u, q):
                kind, a = UNITS[u]
                form, i, c = jobs(u)[q]
                n = JOB0[u] + q
                act.wait_ge(s["job_pe"], n + 1)
                bank = n % PJ
                r = rows(i) if form == "N" else P
                if kind == "iq":
                    t0, cw = CHUNKS[c]
                    lo, hi = max(2 * P - t0, 0), min(T - t0, cw)
                    j = 2 * a + i
                    dst = slice(t0 + lo - 2 * P, t0 + hi - 2 * P)
                    act.activation(IQS[0:HD, 2 * j, dst], ps(bank, hi - lo, HD, o=lo), ACT.Copy)
                    last = act.activation(IQS[HD:P, 2 * j + 1, dst], ps(bank, hi - lo, P, HD, lo), ACT.Copy)
                    if c == 2:
                        act.wait_ge(s["init_gp"], 1)
                        iqp = IQP[:, :, :].rearrange("p a b -> p (a b)")
                        for hh in range(2):
                            for b2 in range(2):
                                last = act.activation(
                                    iqp[b2 * HD:(b2 + 1) * HD, 8 * b2 + 2 * j + hh:4 * BR:BR + 16],
                                    ps(bank, SB, (hh + 1) * HD, hh * HD, 256)[:, b2:SB:2], ACT.Copy)
                elif kind == "ix":
                    act.activation(IW[0:r, i, :], ps(bank, IH, r), ACT.Copy, scale=float(IH ** -0.5 * HD ** -0.5))
                    last = act.activation(IKN[0:r, i, :, :], rep(ps(bank, HD, r, o=IH), 2), ACT.Copy)
                elif kind == "hg":
                    t0, cw = CHUNKS[c]
                    hi = min(T - t0, cw)
                    dst, samp, fn = ((FB, FS, ACT.Sigmoid), (QB, QSS, ACT.Silu))[i]
                    if q == 0 and a > 0:
                        act.wait_ge(s["prep_done"], a)
                    last = act.activation(dst[:, t0:t0 + hi], ps(bank, hi), fn)
                    if c == 2:
                        last = act.activation(samp[:, a, :], ps(bank, SB, o=hi), fn)
                elif kind == "hv":
                    last = act.activation(HV[0:r, i, a * UW:(a + 1) * UW], ps(bank, UW, r), ACT.Copy)
                elif kind in STAGED:
                    g = staged[0]
                    ge(act, s[f"stg_out{g % 2}"], 16 * (g // 2))
                    act.activation(STG[0:r, g % 2, :], ps(bank, UW, r),
                                   ACT.Copy if kind == "v" else ACT.Silu).then_inc(s["stg_act"], 1)
                    act.wait_ge(s["stg_act"], g + 1)
                    last = act.activation(ONE[0:1, 0:1], ONE[0:1, 0:1], ACT.Copy)
                    staged[0] += 1
                else:
                    g = normed[0]
                    ge(act, s[f"nq_out{g % 2}"], 16 * (g // 2))
                    act.activation(NQ[0:r, g % 2, :], ps(bank, UW, r), ACT.Copy)
                    for h in range(4):
                        last = act.activation(SQ[0:r, h * HD:(h + 1) * HD], ps(bank, HD, r, o=h * HD), ACT.Square,
                                              accum_out=NRM[0:r, 0, g % 2, h:h + 1])
                    normed[0] += 1
                last.then_inc(s["job_act"], 1)
                if u in NORMED:
                    act.wait_ge(s["job_act"], n + 1)
                    rstd_of(normed[0] - 1)

            act.wait_ge(s["tab_pe"], 1)
            act.activation(UT[0:AH, :], ps(6, UL, AH), ACT.Copy, scale=8.0).then_inc(s["tab_act"], 1)
            squares(0)
            first_rstd(0)
            high_w(0)
            squares(1)
            first_rstd(1)
            high_x(0)
            squares(2)
            first_rstd(2)
            high_x(1)
            high_x(2)
            for u in range(NU):
                if u + 1 < NU:
                    high_w(u + 1)
                for q in range(len(jobs(u))):
                    evac(u, q)
                    if u - 1 in HGU and q == 1:
                        prep_log(HGU.index(u - 1))
                    if u in HUNIT and 1 <= q:
                        chunk_a(HUNIT[u], q - 1)
                        if q >= 2:
                            chunk_b(HUNIT[u], q - 2)
                if u in HUNIT:
                    chunk_b(HUNIT[u], NT - 1)
                if u - 1 in HGU:
                    prep_exp(HGU.index(u - 1))
                if u == UIX:
                    for g in range(2):
                        act.wait_ge(s["ik_t"], g + 1)
                        c = slice(512 * g, 512 * g + 512)
                        act.activation(IA[0:HD, c], ps(6 + g, 512, HD), ACT.Copy)
                        act.activation(IB[HD:P, c], ps(6 + g, 512, P, HD), ACT.Copy).then_inc(s["ik_h"], 1)
                    act.wait_ge(s["ik_t"], 3)
                    act.activation(IKNEW[0:HD, :], ps(6, SB, HD)[:, 0:SB:2], ACT.Copy)
                    act.activation(IKNEW[HD:P, :], ps(6, SB, P, HD)[:, 1:SB:2], ACT.Copy).then_inc(s["ik_h"], 1)
                    act.wait_ge(s["samp_pe"], 4)
                    act.activation(RSM[0:BR, :], ps(0, PAST + 1, BR), ACT.Relu).then_inc(s["samp_relu"], 1)
                    for m in range(IH * 6):
                        w = P * (m // IH + 3)
                        act.wait_ge(s["sc_pe"], m + 1)
                        ge(act, s["sc_acc"], m - 1)
                        act.activation(RB[:, m % 2, 0:w], ps(2 * (m % 3), w), ACT.Relu).then_inc(s["sc_relu"], 1)
            act_tail(act, link, high_w)

        @block.vector
        def _(dve):
            chain = [0]

            def link(ins):
                chain[0] += 1
                ins.then_inc(s["dve_chain"], 1)
                dve.wait_ge(s["dve_chain"], chain[0])

            dve.memset(STAT[:, 0, :], 1.0)
            dve.memset(EPSC[:, :], EPS)
            dve.memset(ONE[:, :], 1.0)
            dve.memset(NRM[:, :, :, :], 1.0)
            dve.memset(CNT[:, :], 0.0)
            dve.memset(U[:, :], 0).then_inc(s["init_dve"], 1)
            dve.wait_ge(s["init_dve"], 1)
            dve.wait_ge(s["const_in"], NCONST_)
            dve.tensor_copy(BITI[:, :], BITF[:, :])
            dve.tensor_tensor(OML[:, :], LBR[:, 0, :], LBR[:, 1, :], ALU.subtract).then_inc(s["init_dve"], 1)
            dve.wait_ge(s["lb_act"], 1)
            dve.tensor_scalar(OML[:, :], LB[:, :], -1.0, 1.0, ALU.mult, ALU.add).then_inc(s["lb_done"], 1)

            def x_norm(g):
                c = slice(3 * g, 3 * g + 3)
                dve.wait_ge(s["ss_done"], 3 * g + 3)
                dve.tensor_scalar(STAT[:, 1, c], STAT[:, 0, c], 1.0 / D, EPS, ALU.mult, ALU.add)\
                    .then_inc(s["var_done"], 1)
                dve.wait_ge(s["r0_done"], g + 1)
                link(dve.tensor_tensor(STAT[:, 3, c], STAT[:, 2, c], STAT[:, 2, c], ALU.mult))
                link(dve.tensor_tensor(STAT[:, 3, c], STAT[:, 3, c], STAT[:, 1, c], ALU.mult))
                link(dve.tensor_scalar(STAT[:, 3, c], STAT[:, 3, c], -0.5, 1.5, ALU.mult, ALU.add))
                link(dve.tensor_tensor(STAT[:, 3, c], STAT[:, 3, c], STAT[:, 2, c], ALU.mult))
                for i in range(3 * g, 3 * g + 3):
                    r = rows(i)
                    dve.tensor_scalar(XB[0:r, i % 6, :], XB[0:r, i % 6, :], STAT[0:r, 3, i:i + 1], None, ALU.mult)\
                        .then_inc(s["xn_done"], 1)

            def low_x(g):
                for i in range(3 * g, 3 * g + 3):
                    for h in range(2):
                        n = 2 * i + h
                        dve.wait_ge(s["xt_h"], n + 1)
                        src = ps(6 + n % 2).rearrange("p (k t) -> p k t", t=P)[:, :, 0:rows(i)]
                        c = slice(row0(i), row0(i) + rows(i))
                        dve.tensor_tensor(XL[:, 4 * h:4 * h + 4, c], src, f(XH[:, 4 * h:4 * h + 4, c]), ALU.subtract)\
                            .then_inc(s["xt_l"], 1)

            x_norm(0)
            x_norm(1)
            low_x(0)
            x_norm(2)
            low_x(1)
            low_x(2)
            for u in range(UIX):
                for q, (form, i, c) in enumerate(jobs(u)):
                    n = JOB0[u] + q
                    t0, cw = CHUNKS[c]
                    lo, hi = max(2 * P - t0, 0), min(T - t0, cw)
                    j = 2 * UNITS[u][1] + i
                    dst = slice(t0 + lo - 2 * P, t0 + hi - 2 * P)
                    dve.wait_ge(s["job_act"], n + 1)
                    dve.tensor_tensor(IQS[HD:P, 2 * j, dst], ps(n % PJ, hi - lo, HD, o=lo), f(IQS[0:HD, 2 * j, dst]),
                                      ALU.subtract)
                    dve.tensor_tensor(IQS[0:HD, 2 * j + 1, dst], ps(n % PJ, hi - lo, P, HD, lo),
                                      f(IQS[HD:P, 2 * j + 1, dst]), ALU.subtract).then_inc(s["iq_low"], 1)
            for g in range(2):
                c = slice(512 * g, 512 * g + 512)
                dve.wait_ge(s["ik_h"], g + 1)
                dve.tensor_tensor(IB[0:HD, c], ps(6 + g, 512, HD), f(IA[0:HD, c]), ALU.subtract)
                dve.tensor_tensor(IA[HD:P, c], ps(6 + g, 512, P, HD), f(IB[HD:P, c]), ALU.subtract)\
                    .then_inc(s["ik_l"], 1)
            dve.wait_ge(s["iw_pe"], 1)
            link(dve.tensor_tensor(HMT[0:BR, :], ps(7, IH, BR), HM[0:BR, 0:8], ALU.mult))
            link(dve.reduce_sum(IWC[0:BR, :], HMT[0:BR, :], axis=AX.X))
            dve.tensor_scalar(WSEL[0:BR, :], HM[0:BR, 8:16], IWC[0:BR, 0:1], None, ALU.mult).then_inc(s["iw_sel"], 1)
            dve.wait_ge(s["samp_w"], 1)
            dve.tensor_copy(SCS[0:SB, 0:PAST + 1], ps(3, PAST + 1, SB)).then_inc(s["samp_sc"], 1)
            for m in range(IH * 6):
                t, h = m // IH + 2, m % IH
                w = P * (t + 1)
                sc = SC[:, SC0[t]:SC0[t] + w]
                dve.wait_ge(s["sc_relu"], m + 1)
                if h == 0:
                    ins = dve.tensor_scalar(sc, RB[:, m % 2, 0:w], IW[:, t, h:h + 1], None, ALU.mult)
                else:
                    dve.wait_ge(s["sc_acc"], m)
                    ins = dve.scalar_tensor_tensor(sc, RB[:, m % 2, 0:w], IW[:, t, h:h + 1], sc, ALU.mult, ALU.add)
                ins.then_inc(s["sc_acc"], 1)

            dve.wait_ge(s["sc_seen"], 6)
            dve.wait_ge(s["samp_sc"], 1)
            tiles = [(t - 2, P, SC[:, SC0[t]:SC0[t] + P * (t + 1)], P * (t + 1)) for t in range(2, NT)]
            tiles.append((6, SB, SCS[0:SB, 0:PAST + 1], PAST + 1))

            def count(threshold, op, done):
                for k, r, sc, w in tiles:
                    dve.tensor_scalar(JK[0:r, 0:w], sc, threshold(k, r), None, op, ALU.add,
                                      accum_out=CNT[0:r, k:k + 1]).then_inc(s["dve_chain"], 1)
                    dve.wait_ge(s["dve_chain"], done + k + 1)

            count(lambda k, r: 0.0, ALU.is_ge, chain[0])
            chain[0] += 7
            link(dve.tensor_scalar(XM[:, :], CNT[:, :], float(TOPK), -1.0, ALU.is_lt, ALU.mult))
            def rounds(a, b):
                start = chain[0]
                with dve.Fori(a, b) as it:
                    done = (it - a) * 10 + start
                    dve.scalar_tensor_tensor(CAND[:, :], U[:, :], BITI[:, bass.ds(it, 1)], XM[:, :],
                                             ALU.bitwise_or, ALU.bitwise_xor).then_inc(s["dve_chain"], 1)
                    dve.wait_ge(s["dve_chain"], done + 1)
                    count(lambda k, r: CAND[0:r, k:k + 1].bitcast(F32), ALU.is_ge, done + 1)
                    dve.tensor_scalar(HIT[:, :], CNT[:, :], float(TOPK), BITF[:, bass.ds(it, 1)],
                                      ALU.is_ge, ALU.mult).then_inc(s["dve_chain"], 1)
                    dve.wait_ge(s["dve_chain"], done + 9)
                    dve.tensor_tensor(U[:, :], U[:, :], HIT[:, :], ALU.bitwise_or).then_inc(s["dve_chain"], 1)
                    dve.wait_ge(s["dve_chain"], done + 10)
                chain[0] = start + 10 * (b - a)

            def scan(j):
                dve.wait_ge(s["f_ln"], j + 1)
                dve.tensor_tensor_scan(FB[:, :], RM[:, :], FB[:, :], 0.0, ALU.mult, ALU.add)\
                    .then_inc(s["scan_done"], 1)

            def masks():
                link(dve.tensor_tensor(CAND[:, :], U[:, :], XM[:, :], ALU.bitwise_xor))
                count(lambda k, r: CAND[0:r, k:k + 1].bitcast(F32), ALU.is_gt, chain[0])
                chain[0] += 7
                link(dve.tensor_scalar(NEED[:, :], CNT[:, :], -1.0, float(TOPK), ALU.mult, ALU.add))
                for k, r, sc, w in tiles:
                    thr = CAND[0:r, k:k + 1].bitcast(F32)
                    link(dve.tensor_scalar(JK[0:r, 0:w], sc, thr, None, ALU.is_equal))
                    link(dve.tensor_tensor_scan(CU[0:r, 0:w], JK[0:r, 0:w], JK[0:r, 0:w], 0.0, ALU.add, ALU.max))
                    link(dve.scalar_tensor_tensor(CU[0:r, 0:w], CU[0:r, 0:w], NEED[0:r, k:k + 1], JK[0:r, 0:w],
                                                  ALU.is_le, ALU.mult))
                    link(dve.scalar_tensor_tensor(JK[0:r, 0:w], sc, thr, CU[0:r, 0:w], ALU.is_gt, ALU.add))
                    m = MSK[:, 2 * SC0[k + 2]:2 * SC0[k + 2] + w] if k < 6 else MSKS[0:SB, 0:w]
                    dve.tensor_scalar(m, JK[0:r, 0:w], -1.0, -NEG, ALU.add, ALU.mult).then_inc(s["masks"], 1)
                    dve.wait_ge(s["masks"], k + 1)

            rounds(0, 3)
            scan(0)
            rounds(3, 13)
            scan(1)
            rounds(13, 26)
            scan(2)
            rounds(26, ROUNDS)
            masks()
            scan(3)
            dve_tail(dve, link)

        @block.tensor
        def _(pe):
            pe.wait_ge(s["const_in"], NCONST_)
            pe.matmul(ps(6, UL, AH), REL[0:32, :], OH[0:32, :], start=True, stop=True).then_inc(s["tab_pe"], 1)

            def transpose_x(i):
                pe.wait_ge(s["xn_done"], i + 1)
                for h in range(2):
                    n = 2 * i + h
                    ge(pe, s["xt_l"], n - 1)
                    if n == 0:
                        pe.wait_ge(s["tab_act"], 1)
                    for k in range(4):
                        last = pe.transpose(ps(6 + n % 2, rows(i), o=k * P), XB[0:rows(i), i % 6, (4 * h + k) * P:(4 * h + k + 1) * P],
                                            IDN[0:rows(i), 0:rows(i)])
                    last.then_inc(s["xt_t"], 1)

            def chunk_a(j, c):
                n = NT * j + c
                if c == 0:
                    pe.wait_ge(s["prep_done"], j + 1)
                ge(pe, s["at_act"], n - 1)
                bank = 6 + n % 2
                o = 0
                for i in range(NSUB):
                    w = SUB * (i + 1)
                    pe.matmul(ps(bank, 2 * SUB, w, o=2 * SUB * i), KT[:, o + c * w:o + (c + 1) * w],
                              QT[:, :, c * P + i * SUB:c * P + (i + 1) * SUB], start=True, stop=True)
                    o += NT * w
                o -= NT * P
                pe.transpose(ps(bank, P, o=256), KT[:, o + c * P:o + (c + 1) * P], IDN[:, :]).then_inc(s["a_pe"], 1)

            def chunk_b(j, c):
                n = NT * j + c
                pe.wait_ge(s["at_act"], n + 1)
                ge(pe, s["u_act"], n)
                v = HV[:, c, j * P:(j + 1) * P]
                pe.matmul(ps(5, P), KTN[:, n % 2, :], v, start=True, stop=True).then_inc(s["u_pe"], 1)
                ge(pe, s["st_gp"], n)
                ge(pe, s["o_act"], n)
                if n == 0:
                    pe.wait_ge(s["init_gp"], 4)
                pe.matmul(ps(4, P), QI[:, c * P:(c + 1) * P], ST[:, j, :], start=True, stop=False)
                pe.wait_ge(s["at_gp"], n + 1)
                for hh in range(2):
                    last = pe.matmul(ps(4, HD, o=hh * HD), ATB[:, n % 2, hh, :], v[:, hh * HD:(hh + 1) * HD],
                                     start=False, stop=hh == 1)
                last.then_inc(s["o_pe"], 1)

            def unit(u):
                w = width(u)
                sl = u % 2
                pe.wait_ge(s["wl_done"], 2 * u + 2)
                for q, (form, i, c) in enumerate(jobs(u)):
                    n = JOB0[u] + q
                    m = n - PJ
                    if m >= JOB0[NU]:
                        pe.wait_ge(s["y_add"], m - JOB0[NU] + 1)
                    elif m >= 0:
                        pe.wait_ge(s["job_act"], m + 1)
                        if m < JOB0[UIX]:
                            pe.wait_ge(s["iq_low"], m + 1)
                    if u == 0:
                        pe.wait_ge(s["xt_l"], 6 * (c + 1))
                    if u >= NU:
                        pe.wait_ge(s["mt_l"], 2 * (i + 1))
                    for k in range(KC):
                        for x, ww in ((XH, WH), (XL, WH), (XH, WL)):
                            first, final = k == 0 and x is XH and ww is WH, k == KC - 1 and ww is WL
                            if form == "T":
                                t0, cw = CHUNKS[c]
                                last = pe.matmul(ps(n % PJ, cw), ww[:, sl, k, i * P:(i + 1) * P], x[:, k, t0:t0 + cw],
                                                 start=first, stop=final)
                            else:
                                last = pe.matmul(ps(n % PJ, w, rows(i)), x[:, k, row0(i):row0(i) + rows(i)],
                                                 ww[:, sl, k, 0:w], start=first, stop=final)
                    last.then_inc(s["job_pe"], 1)
                    if u in HUNIT and 1 <= q:
                        chunk_a(HUNIT[u], q - 1)
                        if q >= 2:
                            chunk_b(HUNIT[u], q - 2)
                if u in HUNIT:
                    chunk_b(HUNIT[u], NT - 1)
                pe.wait_ge(s["job_pe"], JOB0[u + 1])
                pe.matmul(ps(JUNKB, 2, 2), ANR[:, 0:2], ANR[:, 0:2], start=True, stop=True).then_inc(s["unit_pe"], 1)

            for i in range(NT + 1):
                transpose_x(i)
            pe.wait_ge(s["init_act"], 1)
            for u in range(UIX + 1):
                unit(u)
            pe.wait_ge(s["job_act"], JOB0[UIX + 1])
            for g, (lo, hi) in enumerate(((0, 4), (4, 8), (8, 9))):
                if g == 2:
                    pe.wait_ge(s["ik_l"], 1)
                for i in range(lo, hi):
                    last = pe.transpose(ps(6 + g % 2, rows(i), o=(i - lo) * P), IKN[0:rows(i), i, :, :].rearrange("p a d -> p (a d)"),
                                        IDN[0:rows(i), 0:rows(i)])
                last.then_inc(s["ik_t"], 1)
            pe.wait_ge(s["ik_l"], 2)
            pe.matmul(ps(7, IH, BR), E8[0:8, :], IW[0:8, NT, :], start=True, stop=True).then_inc(s["iw_pe"], 1)
            pe.wait_ge(s["ik_h"], 3)
            for bp in range(4):
                sl = bp % 2
                pe.wait_ge(s[f"ikc_in{sl}"], 256 * (bp // 2 + 1))
                for c in range(2):
                    pe.matmul(ps(c, 512, BR), IQP[:, bp, :], IKT[:, sl, c * 512:(c + 1) * 512], start=bp == 0, stop=bp == 3)
                pe.matmul(ps(2, 1, BR), IQP[:, bp, :], IKNEW[:, bp:bp + 1], start=bp == 0, stop=bp == 3)\
                    .then_inc(s["samp_pe"], 1)
            pe.wait_ge(s["samp_relu"], 1)
            pe.wait_ge(s["iw_sel"], 1)
            for c, w in ((0, 512), (1, 512), (2, 1)):
                last = pe.matmul(ps(3 + c, w, SB), WSEL[0:BR, :], RSM[0:BR, c * 512:c * 512 + w], start=True, stop=True)
            last.then_inc(s["samp_w"], 1)
            pe.wait_ge(s["samp_sc"], 1)
            for m in range(IH * 6):
                t, h = m // IH + 2, m % IH
                ge(pe, s["sc_relu"], m - 2)
                for c0 in range(0, P * (t + 1), 512):
                    w = min(512, P * (t + 1) - c0)
                    for kk, stack in enumerate((IA, IB)):
                        last = pe.matmul(ps(2 * (m % 3) + c0 // 512, w), IQS[:, h, (t - 2) * P:(t - 1) * P],
                                         stack[:, c0:c0 + w], start=kk == 0, stop=kk == 1)
                last.then_inc(s["sc_pe"], 1)
            pe.wait_ge(s["sc_relu"], IH * 6)
            for u in range(UIX + 1, NU):
                unit(u)
            pe_tail(pe, unit)


_OUTS = [(1, T, D), (SB, 1, D), (1, 1, T, KVH, HD), (1, 1, T, KVH, HD), (1, 1, T, HD), (1, 1, HH, HD, HD),
         (1, SB, 1, KVH, HD), (1, SB, 1, KVH, HD), (1, SB, 1, HD), (1, SB, HH, HD, HD)]


def _columns():
    q, k, v, ga, iq, ix, hq, hf, hi, gh = 0, 512, 768, 1024, 1536, 2048, 2120, 2632, 3144, 3656
    part = {"iq": iq, "hv": hi, "q": q, "k": k, "v": v, "gh": gh, "ga": ga}
    out = []
    for kind, a in UNITS:
        if kind == "ix":
            out.append([(ix, XW)])
        elif kind == "hg":
            out.append([(hf + a * P, P), (hq + a * P, P)])
        else:
            out.append([(part[kind] + a * UW, UW)])
    return out


def _bucket(n):
    n = max(n, 0)
    if n < 16:
        return n
    large = 16 + int(np.float32(np.log(np.float32(n) / np.float32(16)) / np.float32(np.log(128 / 16))) * np.float32(16))
    return min(large, 31)


def _constants():
    oh = np.zeros((32, UL), np.float32)
    for m in range(UL):
        oh[_bucket(255 - m), m] += 1
        oh[31, m] -= 1
    bits = np.tile((2.0 ** np.arange(ROUNDS - 1, -1, -1)).astype(np.float32), (P, 1))
    e8 = np.zeros((2, 8, BR), np.float32)
    for b in range(SB):
        for h in range(AH):
            e8[0, b, b * AH + h] = 1
            e8[1, h, b * AH + h] = 1
    masks = np.zeros((P, 656), np.float32)
    sidx = np.arange(P)[:, None]
    masks[:, 0:256] = np.tile(sidx <= np.arange(P)[None], (1, 2))
    masks[:, 256:384] = (sidx // HD == np.arange(P)[None] // HD)
    for b in range(SB):
        for h in range(AH):
            masks[b * AH + h, 384 + h] = 1
            masks[b * AH + h, 392 + b] = 1
    masks[:, 400:528] = np.where(np.arange(P)[None] <= sidx, 0.0, NEG)
    masks[:, 528:656] = np.eye(P)[::-1]
    return {"c_ident": np.eye(P, dtype=np.float32), "c_oh": oh, "c_bits": bits, "c_e8": e8, "c_masks": masks}


def kernel(**inputs):
    import concourse.bacc as _bacc
    from concourse.bass_utils import run_bass_kernel_spmd as _run

    x = {k: np.asarray(v) for k, v in inputs.items()}
    w_in, w_out = x["w_in"][0], x["w_out"][0]

    def unit_layout(w):
        return w.reshape(2, 4, P, -1).transpose(0, 2, 1, 3)

    cols = _columns()
    parts = [np.concatenate([w_in[:, c:c + n] for c, n in cs], axis=1) for cs in cols]
    main = [unit_layout(w) for u, w in enumerate(parts) if u != UIX]
    main += [unit_layout(w_out[:, c * UW:(c + 1) * UW]) for c in range(NUO)]
    data = {
        "x_prompt": x["x_prompt"], "x_sample": x["x_sample"],
        "w_main": np.stack(main), "w_ix": unit_layout(parts[UIX]),
        "cache_kt": x["cache_k"][0].reshape(-1, P, 2, P).transpose(0, 3, 2, 1),
        "cache_v": x["cache_v"][0].reshape(-1, P, UW),
        "cache_ikt": x["cache_ik"][0].transpose(0, 2, 1),
        "state": x["state_hgrn"][0].reshape(SB, NG, 2, HD, HD).transpose(2, 3, 0, 1, 4),
        "pages": x["page_table"].reshape(1, -1),
        "rel": x["rel_bias"],
        "ln_g": x["ln_g"][0].reshape(KC, P).T,
        "q_g": np.broadcast_to(x["q_norm_g"][0], (P, HD)), "k_g": np.broadcast_to(x["k_norm_g"][0], (P, HD)),
        "hn_g": np.broadcast_to(x["hgrn_norm_g"][0], (P, HD)),
        "lbs": x["hgrn_lb"].reshape(2, NG, P).transpose(2, 0, 1),
        **_constants(),
    }
    nc = _bacc.Bacc("TRN2", target_bir_lowering=False, num_devices=1)
    arrays, args = {}, []
    for name, a in data.items():
        a = np.ascontiguousarray(a)
        arrays[f"in_{name}"] = a
        args.append(nc.dram_tensor(f"in_{name}", a.shape, mybir.dt.from_np(a.dtype), kind="ExternalInput").ap())
    for i, shape in enumerate(_OUTS):
        args.append(nc.dram_tensor(f"out_{i}", shape, F32, kind="ExternalOutput").ap())
    hymba_step(nc, *args)
    r = _run(nc, [arrays], core_ids=[0])
    return tuple(r.results[0][f"out_{i}"] for i in range(len(_OUTS)))
```

```python
import numpy as np
import concourse.bass as bass
from concourse import mybir
from contextlib import ExitStack

F32 = mybir.dt.float32
F32R = mybir.dt.float32r
BF16 = mybir.dt.bfloat16
F16 = mybir.dt.float16
I32 = mybir.dt.int32
ACT = mybir.ActivationFunctionType
ALU = mybir.AluOpType
AX = mybir.AxisListType

P = 128
D = 1024
KC = D // P
T = 1024
NT = T // P
SB = 8
TT = T + SB
PAST = 1024
NPG = PAST // P
NPOOL = 80
HD = 64
AH, KVH, IH, HH = 8, 4, 8, 8
NG = HH // 2
SUB = 32
NSUB = P // SUB
TOPK = 256
EPS = 1e-6
NEG = -1e30
UNSEEN = -3e38
UW = 256
NEAR = 2 * P
NCONST_ = 17 * 16
UL = 383
ROUNDS = 31
BR = SB * AH


def rows(i):
    return P if i < NT else SB


CHUNKS = [(0, 384), (384, 384), (768, 264)]
UNITS = [("iq", 0), ("iq", 1), ("ix", 0), ("hg", 0), ("hv", 0), ("hv", 1),
         ("hg", 1), ("gh", 0), ("k", 0), ("hg", 2), ("gh", 1), ("q", 0),
         ("hg", 3), ("ga", 0), ("q", 1), ("ga", 1), ("v", 0)]
NU = len(UNITS)
NUO = D // UW
UIX = UNITS.index(("ix", 0))
XW = IH + HD
def width(u):
    return XW if u == UIX else UW


def jobs(u):
    kind = UNITS[u][0] if u < NU else "out"
    if kind == "iq":
        return [("T", b, c) for c in range(3) for b in range(2)]
    if kind == "ix":
        return [("T", 0, c) for c in range(3)]
    if kind == "hg":
        return [("T", b, c) for b in range(2) for c in range(3)]
    return [("N", i, 0) for i in range(NT + 1)]


JOB0 = [0]
for _u in range(NU + NUO):
    JOB0.append(JOB0[-1] + len(jobs(_u)))
PJ = 4
STAGED = ("v", "gh", "ga", "q", "k")
HGU = [UNITS.index(("hg", j)) for j in range(NG)]
STG_UNITS = [u for u in range(NU) if UNITS[u][0] in STAGED]
CHUNK0 = [JOB0[u + 2] + 4 for u in HGU]
EVENTS = {}
for _lag, _kind in ((2, "out"), (0, "intra"), (1, "keys")):
    for _j in range(NG):
        for _c in range(NT):
            EVENTS.setdefault(CHUNK0[_j] + _c + _lag, []).append((_kind, _j, _c))

SC0 = {t: sum(P * (x + 1) for x in range(2, t)) for t in range(2, NT)}
SCW = sum(P * (x + 1) for x in range(2, NT))


def hymba_step(nc, x_prompt, x_sample, w_main, w_ix, cache_kt, cache_v, cache_ikt, state, pages,
               rel, ln_g, q_g, k_g, hn_g, lbs, c_ident, c_oh, c_bits, c_e8, c_masks,
               y_prompt, y_sample, k_prompt, v_prompt, ik_prompt, s_prompt,
               k_sample, v_sample, ik_sample, s_sample):
    with ExitStack() as ctx:
        cur = [16512]

        def at(name, shape, dt, off):
            return nc.alloc_sbuf_tensor_at(name, [P] + shape, dt, offset=off)

        def size(shape, dt):
            return int(np.prod(shape)) * {F32: 4, F32R: 4, I32: 4, BF16: 2, F16: 2}[dt]

        def sb(name, shape, dt=F32):
            off = cur[0]
            cur[0] += (size(shape, dt) + 31) // 32 * 32
            assert cur[0] <= 229344, (name, cur[0])
            return at(name, shape, dt, off)

        def over(start, *parts):
            out = []
            for name, shape, dt in parts:
                out.append(at(name, shape, dt, start))
                start += (size(shape, dt) + 31) // 32 * 32
            out.append(start)
            return out

        def sem(name):
            return ctx.enter_context(nc.semaphore(name))

        def ge(eng, s, v):
            if v > 0:
                eng.wait_ge(s, v)

        IDN = sb("ident", [P])
        ANR = sb("antidiagonal_r", [P], F32R)
        IDB = sb("ident_b", [P], BF16)
        LNG = sb("ln_gain", [KC])
        QG = sb("q_gain", [HD])
        KG = sb("k_gain", [HD])
        HNG = sb("hgrn_gain", [HD])
        IW = sb("index_weight", [NT + 1, IH])
        STAT = sb("x_stats", [4, NT + 1])
        LBR = sb("lb_rows", [2, NG])
        LB = sb("lb", [NG])
        OML = sb("one_minus_lb", [NG])
        TRI = sb("causal_add", [P], BF16)
        FS = sb("f_sample", [NG, SB])
        QSS = sb("q_sample", [NG, SB])
        KSS = sb("k_sample_h", [NG, SB])
        IKNEW = sb("ik_new", [4])
        BITF = sb("bit_value", [ROUNDS])
        BITI = sb("bit", [ROUNDS], I32)
        CNT = sb("count", [7])
        NEED = sb("need", [7])
        U = sb("bits_so_far", [7], I32)
        XM = sb("sign_flip", [7], I32)
        CAND = sb("candidate", [7], I32)
        HIT = sb("bit_kept", [7], I32)
        SQK = sb("qk_square_sums", [3, NT + 1, 12])
        SHO = sb("ho_square_sums", [3, NT, 8])
        DE = sb("chunk_decay", [2, NT])
        PT_ = sb("page_table", [SB * NPG], I32)
        E8 = sb("row_select", [BR])
        E8H = sb("head_select", [BR])
        HM = sb("head_mask", [2 * SB])
        E8B = sb("row_select_b", [BR], BF16)
        IWC = sb("index_weight_col", [1])
        WSEL = sb("index_weight_sel", [SB])
        HMT = sb("head_mask_tmp", [SB])
        MX = sb("row_max", [8])
        NB = sb("neg_max", [8])
        RS = sb("row_sum", [2, 8])
        RI = sb("row_sum_inv", [8])
        MN = sb("ho_sample_stats", [3])
        UT = sb("bias_by_distance", [UL])
        EPSC = sb("eps", [1])
        ONE = sb("one", [1])

        XR0 = cur[0]
        XH = sb("xT_high", [KC, TT], F32R)
        XL = sb("xT_low", [KC, TT], F32R)
        QS, KA, KB, _ = over(XR0, ("qT_stack", [AH, T], F32R), ("kT_high_low", [KVH, T], F32R),
                             ("kT_low_high", [KVH, T], F32R))
        KS_, VS_, _ = over(XR0, ("keys_T", [2, 2, PAST], F32), ("values", [2, NPG, UW], F32))
        WR = sb("w_raw", [2, 4, UW])
        W0 = cur[0]
        WH = sb("w_high", [2, KC, UW], F32R)
        WL = sb("w_low", [2, KC, UW], F32R)
        BL, BH, VT, QR, KR, _e = over(W0, ("bias_low", [AH, NEAR], F32R), ("bias_high", [AH, NEAR], F32R),
                                      ("values_T", [NT, UW], F32), ("q_rows", [2, 512], F32),
                                      ("k_rows", [2, KVH, 2, HD], F32))
        assert _e <= cur[0]
        S0 = cur[0]
        SC = sb("scores", [SCW])
        SCS = sb("scores_sample", [PAST + 32])
        R0_ = cur[0]
        RB = sb("relu", [2, T])
        XB, _e = over(S0, ("x_rows", [6, D], F32))
        assert _e <= cur[0]
        MSK, = over(S0, ("mask", [2 * SCW], BF16))[:1]
        MSKS, = over(S0 + SCW * 4, ("mask_sample", [2 * PAST + 64], BF16))[:1]
        FB, QB, _ = over(R0_, ("decay_log", [T], F32), ("hq", [T], F32))
        PTS, _ = over(R0_, ("pT", [2, NT, P], F32))
        JK = sb("flag", [PAST + 8], F16)
        CU = sb("flag_count", [PAST + 8], F16)
        I0 = cur[0]
        IQS = sb("iqT_stack", [IH, T - 2 * P], F32R)
        IA = sb("ikT_high_low", [T], F32R)
        IB = sb("ikT_low_high", [T], F32R)
        HV, HK, QI, ATB, HO, _e = over(I0, ("hv", [NT + 1, 512], F32), ("hk", [T], F32), ("q_decayed", [T], F32),
                               ("intra", [2, 2, P], F32), ("ho_rows", [NT, P], F32))
        assert _e <= cur[0], (_e, cur[0])
        AO, PB, SQ, _e = over(I0, ("attn_out", [NT + 1, 512], F32), ("prob", [3, T], F32), ("square", [512], F32))
        assert _e <= cur[0]
        TRF, ANT, _ = over(cur[0], ("causal_add_f", [P], F32), ("antidiagonal", [P], F32))
        STG = sb("stage", [4, UW])
        H0 = cur[0]
        QT = sb("q_ref", [2, T])
        KT = sb("k_ref", [NT * SUB * 10])
        KTN = sb("k_rows_h", [2, P])
        INM = sb("intra_mask", [2, P])
        BM = sb("pair_mask", [P])
        ST_OFF = cur[0]
        ST = sb("hgrn_state", [NG, P])
        TMP = sb("state_add", [2, P])
        RM = sb("scan_keep", [T], BF16)
        IXT, IKN, _e = over(H0, ("ix_T", [TT], F32), ("ik_rows", [NT + 1, HD], F32))
        JA, _ = over(H0, ("square_junk", [D], F32))
        IK0 = _e
        IKT, IQP, _e = over(IK0, ("index_keys_T", [2, PAST], F32), ("iq_padded", [4, BR], F32))
        assert _e <= H0 + 8192 + 10240
        RSM, _e = over(H0, ("relu_sample", [PAST + 1], F32))
        BRAW, _e = over(R0_, ("bias_raw", [AH, NEAR], F32))

        A0 = XR0 + 33024
        QPD, KNW, PSM, PTP, PTN, VN1, OSM, _e = over(
            A0, ("q_padded", [2, SB, BR], F32), ("k_new_T", [2, SB], F32), ("prob_sample", [PAST + 8], F32),
            ("prob_T", [NPG, BR], F32), ("prob_new", [BR], F32), ("v_new", [SB, UW], F32),
            ("out_by_head", [SB, UW], F32))
        assert _e <= XR0 + 66048
        S0T, VBT, QHP, _e = over(H0, ("state_in", [SB, NG, HD], F32), ("v_spread", [SB, NG, HD], F32),
                                 ("hq_padded", [SB * NG, BR], F32))
        HOSM, _e = over(_e, ("ho_sample", [HD], F32))
        assert _e <= cur[0], (_e, cur[0])
        HOR, HGR, AGR, MIX, _e = over(S0, ("ho_in", [2, 512], F32), ("hgate_in", [2, 512], F32),
                                      ("agate_in", [2, 512], F32), ("mix", [2, D], F32))
        XRS, YST, _e = over(_e, ("x_res", [2, UW], F32), ("y_rows", [2, UW], F32))
        assert _e <= R0_ + 8192, (_e, R0_)

        PSA = ctx.enter_context(nc.psum_tensor("psum", [P, 8 * 512], F32))

        def ps(bank, n=512, r=P, r0=0, o=0):
            return PSA[r0:r, bank * 512 + o:bank * 512 + o + n]

        d_q = nc.dram_tensor("q_spill", [TT, 512], F32).ap()
        d_k = nc.dram_tensor("k_spill", [TT, UW], F32).ap()
        d_ho = nc.dram_tensor("ho_spill", [TT, 512], F32).ap()
        d_gh = nc.dram_tensor("hgate_spill", [TT, 512], F32).ap()
        d_ga = nc.dram_tensor("agate_spill", [TT, 512], F32).ap()
        d_hv = nc.dram_tensor("hv_spill", [SB, 512], F32)
        d_ut = nc.dram_tensor("bias_spill", [AH, UL], F32)
        d_ao = nc.dram_tensor("attn_sample_spill", [SB, 512], F32).ap()

        s = {}

        class Sems(dict):
            def __missing__(self, name):
                self[name] = sem(name)
                return self[name]

        s = Sems()

        block = ctx.enter_context(nc.Block())

        def dup(ap):
            return bass.AP(ap.tensor, ap.offset, [ap.ap[0], [0, 2], ap.ap[1]])

        def bc(ap, n):
            return bass.AP(ap.tensor, ap.offset, list(ap.ap) + [[0, n]])

        def rep(ap, n):
            return bass.AP(ap.tensor, ap.offset, [ap.ap[0], [0, n]] + list(ap.ap[1:]))

        def f(ap):
            return ap.bitcast(F32)

        def x_rows(i):
            return x_prompt[0, i * P:(i + 1) * P, :] if i < NT else x_sample[:, 0, :]


        OH, REL, _ = over(ST_OFF, ("bucket_of_distance", [UL], F32), ("rel_bias", [AH], F32))

        def row0(i):
            return min(i, NT) * P

        ALLS = [sum(1 for g in range((NT + 1) * len(STG_UNITS)) if g % 4 == x) * 16 for x in range(4)]
        QOUT = [sum(1 for g in range((NT + 1) * (STG_UNITS.index(UNITS.index(("q", 1))) + 1)) if g % 4 == x) * 16
                for x in range(4)]
        NA = NT * AH
        BUILD = {0: [0, 1], **{2 * (n - 1): [n] for n in range(2, 2 * NT)}}

        def inverse_root(eng, link, out, x, tmp):
            link(eng.tensor_scalar(out.bitcast(I32), x.bitcast(I32), -0.5, 1597463007.0, ALU.mult, ALU.add))
            for _ in range(3):
                link(eng.tensor_tensor(tmp, out, out, ALU.mult))
                link(eng.tensor_tensor(tmp, tmp, x, ALU.mult))
                link(eng.tensor_scalar(tmp, tmp, -0.5, 1.5, ALU.mult, ALU.add))
                link(eng.tensor_tensor(out, out, tmp, ALU.mult))

        def load_weights(sp, u):
            w = width(u)
            for h in range(2):
                n = 2 * u + h
                ge(sp, s["wl_done"], n - 1)
                src = w_ix[h] if u == UIX else w_main[u if u < UIX else u - 1, h]
                sp.dma_start(WR[:, h, :, 0:w], src).then_inc(s[f"w_in{h}"], 16)


        def split_w(gp, u):
            w = width(u)
            for h in range(2):
                gp.wait_ge(s[f"w_in{h}"], 16 * (u + 1))
                if u < NU:
                    for k in range(4):
                        last = gp.tensor_scalar(WR[:, h, k, 0:w], WR[:, h, k, 0:w],
                                                LNG[:, 4 * h + k:4 * h + k + 1], 1.0, ALU.mult, ALU.mult)
                    last.then_inc(s["wg_done"], 1)
            if u < NU:
                gp.wait_ge(s["wg_done"], 2 * u + 2)
            for h in range(2):
                gp.wait_ge(s["wh_done"], 2 * u + h + 1)
                gp.tensor_tensor(WL[:, u % 2, 4 * h:4 * h + 4, 0:w], WR[:, h, :, 0:w],
                                 f(WH[:, u % 2, 4 * h:4 * h + 4, 0:w]), ALU.subtract)\
                    .then_inc(s["wl_done"], 1)


        def load_rows(sp, i):
            sl, r = i % 2, rows(i)
            if i < 2:
                for x in range(4):
                    sp.wait_ge(s[f"stg_out{x}"], QOUT[x])
                sp.wait_ge(s["job_pe"], JOB0[NU - 1])
            ge(sp, s["b_pe"], 2 * (i - 1))
            ge(sp, s[f"k_out{sl}"], 16 * (i // 2))
            for x in range(2):
                sp.dma_start(KR[0:r, sl, :, x, :], d_k[row0(i):row0(i) + r, :].rearrange("t (h d) -> t h d", d=HD))\
                    .then_inc(s[f"qr_in{sl}"], 16)
            sp.dma_start(QR[0:r, sl, :], d_q[row0(i):row0(i) + r, :]).then_inc(s[f"qr_in{sl}"], 16)

        def sp_tail(sp):
            def store_keys(i):
                sp.wait_ge(s["qk_done"], i + 1)
                sp.dma_start(k_prompt[0, 0, i * P:(i + 1) * P] if i < NT else k_sample[0, :, 0],
                             KR[0:rows(i), i % 2, :, 0, :]).then_inc(s[f"k_out{i % 2}"], 16)

            for x in range(4):
                sp.wait_ge(s[f"stg_out{x}"], ALLS[x])
            sp.wait_ge(s["job_pe"], JOB0[NU])
            sp.dma_start(VT[:, :, :], v_prompt[0, 0].rearrange("(t p) h d -> p t (h d)", p=P)).then_inc(s["kv_in"], 16)
            store_keys(0)
            load_rows(sp, 2)
            sp.wait_ge(s["out_done"], 64)
            sp.dma_start(S0T[:, :, :, :], state.rearrange("a k b j v -> (a k) b j v")).then_inc(s["h0_in"], 16)
            sp.wait_ge(s["hv_out"], 32)
            for hh in range(2):
                for b in range(SB):
                    sp.dma_start(VBT[hh * HD:(hh + 1) * HD, b, :, :],
                                 bass.AP(d_hv, b * 512 + hh * HD, [[0, HD], [P, NG], [1, HD]])).then_inc(s["h0_in"], 16)
            for i in range(3, NT + 1):
                store_keys(i - 2)
                load_rows(sp, i)
            store_keys(NT - 1)
            store_keys(NT)
            sp.wait_ge(s["hs_gp"], 1)
            for hh in range(2):
                for b in range(SB):
                    sp.dma_start(s_sample[0, b].rearrange("(j a) k v -> a k j v", a=2)[hh],
                                 S0T[hh * HD:(hh + 1) * HD, b, :, :]).then_inc(s["hso_out"], 16)
            sp.wait_ge(s["s_pe"], NA)
            sp.dma_start(VN1[0:1, :, :], v_sample[:, :, 0].rearrange("a b h d -> a b (h d)")).then_inc(s["sm_in"], 16)

            def load_pages(b, dst, src, name, done):
                if b >= 2:
                    sp.wait_ge(s[done], b - 1)
                for g in range(NPG):
                    page = sp.value_load(PT_[0:1, b * NPG + g:b * NPG + g + 1], min_val=0, max_val=NPOOL - 1)
                    if name == "kc_in":
                        sp.dma_start(dst[:, b % 2, :, g * P:(g + 1) * P],
                                     src[bass.ds(page, 1)].rearrange("a d j k -> (a d) j k")).then_inc(s[f"{name}{b % 2}"], 16)
                    else:
                        sp.dma_start(dst[:, b % 2, g, :], src[bass.ds(page, 1)].rearrange("a k n -> (a k) n"))\
                            .then_inc(s[f"{name}{b % 2}"], 16)

            for b in range(2):
                load_pages(b, KS_, cache_kt, "kc_in", "ks_pe")
            for b in range(2):
                load_pages(b, VS_, cache_v, "vc_in", "vs_pe")
            for b in range(2, SB):
                load_pages(b, KS_, cache_kt, "kc_in", "ks_pe")
            for b in range(2, SB):
                load_pages(b, VS_, cache_v, "vc_in", "vs_pe")
            for u in (NU, NU + 1):
                load_weights(sp, u)

            def load_mix(i):
                ge(sp, s["mix_done"], i - 1)
                for dst, src in ((HOR, d_ho), (HGR, d_gh), (AGR, d_ga)):
                    sp.dma_start(dst[0:rows(i), i % 2, :], src[row0(i):row0(i) + rows(i), :])\
                        .then_inc(s[f"mix_in{i % 2}"], 16)

            sp.wait_ge(s["ks_pe"], SB)
            sp.wait_ge(s["ho_out"], 16 * NG)
            load_mix(0)
            load_mix(1)
            sp.wait_ge(s["vs_act"], 1)
            for kv in range(KVH):
                sp.dma_start(d_ao.rearrange("b (k g d) -> k g b d", g=2, d=HD)[kv],
                             OSM[2 * kv:2 * kv + 2, :, kv * HD:(kv + 1) * HD]).then_inc(s["aos_out"], 16)
            sp.wait_ge(s["aos_out"], 64)
            sp.dma_start(AO[0:SB, NT, :], d_ao).then_inc(s["aos_in"], 16)
            sp.wait_ge(s["hs_norm"], 1)
            sp.dma_start(d_ho[T:TT, :].rearrange("b (h v) -> (b h) v", v=HD), HOSM[0:BR, :]).then_inc(s["ho_out"], 16)
            sp.wait_ge(s["ho_out"], 16 * (NG + 1))
            NY = NUO * (NT + 1)

            def y_part(n, a, b):
                u, i = n // (NT + 1), n % (NT + 1)
                c = slice(u * UW, (u + 1) * UW)
                return a[0, i * P:(i + 1) * P, c] if i < NT else b[:, 0, c]

            def load_res(n):
                ge(sp, s["y_add"], n - 1)
                sp.dma_start(XRS[0:rows(n % (NT + 1)), n % 2, :], y_part(n, x_prompt, x_sample))\
                    .then_inc(s[f"xr_in{n % 2}"], 16)

            load_res(0)
            load_res(1)

            def store_y(n):
                if n % (NT + 1) == 4 and n // (NT + 1) + 2 < NUO:
                    load_weights(sp, NU + n // (NT + 1) + 2)
                sp.wait_ge(s["y_add"], n + 1)
                sp.dma_start(y_part(n, y_prompt, y_sample), YST[0:rows(n % (NT + 1)), n % 2, :])\
                    .then_inc(s[f"y_out{n % 2}"], 16)
                if n + 2 < NY:
                    load_res(n + 2)

            for i in range(2, NT + 1):
                load_mix(i)
                if i >= 3:
                    store_y(i - 3)
            for n in range(NT - 2, NY):
                store_y(n)
            sp.wait_ge(s["k_out0"], 16 * 5)
            sp.wait_ge(s["k_out1"], 16 * 4)
            sp.wait_ge(s["y_out0"], NY * 8)
            sp.wait_ge(s["y_out1"], NY * 8)
            sp.wait_ge(s["hso_out"], 16 * 2 * SB)

        def gp_tail(gp, link):
            def roots(t):
                x, out, tmp = (t[:, k, :, :].rearrange("p i h -> p (i h)") for k in (0, 1, 2))
                link(gp.tensor_scalar(x, x, 1.0 / HD, EPS, ALU.mult, ALU.add))
                inverse_root(gp, link, out, x, tmp)

            def norm(i):
                r, sl = rows(i), i % 2
                gp.wait_ge(s[f"qr_in{sl}"], 48 * (i // 2 + 1))
                q = QR[0:r, sl, :].rearrange("p (h d) -> p h d", d=HD)
                k = KR[0:r, sl, :, :, :].rearrange("p h x d -> p h (x d)")
                link(gp.tensor_tensor(q, q, bc(SQK[0:r, 1, i, 0:AH], HD), ALU.mult))
                link(gp.tensor_tensor(q, q, rep(QG[0:r, :], AH), ALU.mult))
                link(gp.tensor_tensor(k, k, bc(SQK[0:r, 1, i, AH:12], 2 * HD), ALU.mult))
                k = KR[0:r, sl, :, :, :].rearrange("p h x d -> p (h x) d")
                ins = gp.tensor_tensor(k, k, rep(KG[0:r, :], 2 * KVH), ALU.mult)
                if i == NT:
                    link(ins)
                    ins = gp.tensor_copy(SQ[0:r, 0:UW].rearrange("p (h d) -> p h d", d=HD), KR[0:r, sl, :, 0, :])
                ins.then_inc(s["qk_done"], 1)

            gp.wait_ge(s["job_act"], JOB0[UNITS.index(("q", 1)) + 1])
            roots(SQK)
            for i in range(NT + 1):
                norm(i)
            gp.wait_ge(s["o_act"], NT * NG)
            roots(SHO)
            gp.wait_ge(s["h0_in"], 16 * (1 + 2 * SB))

            def spread(x):
                return bass.AP(x, 0, [[NG * SB, P], [1, SB], [SB, NG], [0, HD]])

            link(gp.tensor_tensor(S0T[:, :, :, :], S0T[:, :, :, :], spread(FS), ALU.mult))
            link(gp.tensor_tensor(VBT[:, :, :, :], VBT[:, :, :, :], spread(KSS), ALU.mult))
            gp.tensor_tensor(S0T[:, :, :, :], S0T[:, :, :, :], VBT[:, :, :, :], ALU.add).then_inc(s["hs_gp"], 1)
            link(gp.memset(QHP[:, :, :], 0.0))
            w = SB * NG * BR
            for hh in range(2):
                link(gp.tensor_scalar(bass.AP(QHP, hh * HD * w + hh, [[w, HD], [NG * BR + 8, SB], [BR + 2, NG]]),
                                      bass.AP(QSS, hh * HD * NG * SB, [[NG * SB, HD], [1, SB], [SB, NG]]),
                                      1.0, 0.0, ALU.mult, ALU.add))
            gp.wait_ge(s["hs_gp"], 1)
            gp.wait_ge(s["s_pe"], NA)
            gp.wait_ge(s["sm_pe"], 1)
            gp.memset(QPD[:, :, :, :], 0.0).then_inc(s["hs_gp"], 1)

            def gain(i):
                r, sl = rows(i), i % 2
                gp.wait_ge(s[f"mix_in{i % 2}"], 48 * (i // 2 + 1))
                hg = HGR[0:r, i % 2, :].rearrange("p (h d) -> p h d", d=HD)
                gp.tensor_tensor(hg, hg, rep(HNG[0:r, :], HH), ALU.mult).then_inc(s["mix_g"], 1)

            gp.wait_ge(s["hs_act"], 1)
            link(gp.tensor_scalar(MN[0:BR, 0:1], MN[0:BR, 0:1], 1.0 / HD, EPS, ALU.mult, ALU.add))
            inverse_root(gp, link, MN[0:BR, 1:2], MN[0:BR, 0:1], MN[0:BR, 2:3])
            gp.tensor_scalar(HOSM[0:BR, :], HOSM[0:BR, :], MN[0:BR, 1:2], 0.0, ALU.mult, ALU.add).then_inc(s["hs_norm"], 1)
            split_w(gp, NU)
            split_w(gp, NU + 1)
            for i in range(NT + 1):
                gain(i)
            split_w(gp, NU + 2)
            split_w(gp, NU + 3)

        def act_tail(act, link, high_w):
            act.wait_ge(s["job_pe"], JOB0[NU - 1])
            act.wait_ge(s["braw_in"], 16)
            act.activation(BH[:, :, :], BRAW[:, :, :], ACT.Copy).then_inc(s["br_h"], 1)

            def build(n):
                i = n // 2
                c = slice(i * P, (i + 1) * P)
                lo, hi = ps(5, 512, HD).rearrange("p (j t) -> p j t", t=P), ps(5, 512, P, HD).rearrange("p (j t) -> p j t", t=P)
                if n == 0:
                    act.wait_ge(s["br_l"], 1)
                act.wait_ge(s["b_pe"], n + 1)
                if n % 2 == 0:
                    act.activation(KA[0:HD, :, c], lo, ACT.Copy)
                    act.activation(KB[HD:P, :, c], hi, ACT.Copy).then_inc(s["b_h"], 1)
                else:
                    act.activation(QS[0:HD, 0:AH:2, c], lo, ACT.Copy)
                    act.activation(QS[HD:P, 1:AH:2, c], hi, ACT.Copy).then_inc(s["b_h"], 1)

            for m in range(NA + 1):
                for n in BUILD.get(m, []):
                    build(n)
                if m < NA:
                    t, h = m // AH, m % AH
                    w = P * (t + 1)
                    act.wait_ge(s["s_max"], m + 1)
                    ge(act, s["p_pe"], m - 2)
                    act.activation(PB[:, m % 3, 0:w], ps(2 * (m % 2), w), ACT.Exp, scale=HD ** -0.5, bias=NB[:, h:h + 1],
                                   accum_out=RS[:, t % 2, h:h + 1]).then_inc(s["s_exp"], 1)
                m1 = m - 1
                if m1 >= 0 and m1 % 2 == 0:
                    w = P * (m1 // AH + 1)
                    act.wait_ge(s["p_pe"], m1 + 1)
                    ge(act, s["v_pe"], m1 - 1)
                    act.activation(PTS[:, m1 % 2, :, :].rearrange("p b t -> p (b t)")[:, 0:w], ps(4, w), ACT.Copy)\
                        .then_inc(s["p_act"], 1)
            act.wait_ge(s["sm_pe"], 1)
            act.wait_ge(s["hs_gp"], 2)
            qpd = QPD[:, :, :, :].rearrange("p a b n -> p (a b n)")
            for blk in range(2):
                act.activation(KNW[:, blk, :], ps(6, SB, o=32 + 8 * blk), ACT.Copy)
                for kv2 in range(2):
                    for g in range(2):
                        o = 512 * blk + 4 * blk + 2 * kv2 + g
                        last = act.activation(qpd[kv2 * HD:(kv2 + 1) * HD, o:512 * (blk + 1):BR + 8],
                                              ps(6, SB, (g + 1) * HD, g * HD, 8 * (2 * blk + kv2)), ACT.Copy)
            last.then_inc(s["sm_act"], 1)
            act.wait_ge(s["ks_max"], 1)
            act.activation(PSM[0:BR, 0:PAST + 1], ps(0, PAST + 1, BR), ACT.Exp, scale=HD ** -0.5, bias=NB[0:BR, 0:1],
                           accum_out=RS[0:BR, 0, 0:1]).then_inc(s["ks_exp"], 1)
            act.wait_ge(s["pt_pe"], 1)
            act.activation(PTP[:, :, :], ps(4, 512).rearrange("p (g n) -> p g n", n=BR), ACT.Copy)
            act.activation(PTN[0:1, :], ps(5, BR, 1), ACT.Copy).then_inc(s["pt_act"], 1)
            act.wait_ge(s["hs_pe"], 1)
            act.activation(ps(6, HD, BR, o=320), ps(6, HD, BR, o=256), ACT.Square, accum_out=MN[0:BR, 0:1])
            act.activation(HOSM[0:BR, :], ps(6, HD, BR, o=256), ACT.Copy).then_inc(s["hs_act"], 1)
            act.wait_ge(s["vs_pe"], SB)
            act.activation(OSM[0:SB, :, :].rearrange("p b n -> p (b n)"), ps(0, 4 * 512, SB), ACT.Copy)\
                .then_inc(s["vs_act"], 1)
            high_w(NU)
            high_w(NU + 1)

            def mix_high(i):
                if i == 0:
                    act.wait_ge(s["aos_out"], 64)
                for h in range(2):
                    n = 2 * i + h
                    act.wait_ge(s["mt_pe"], n + 1)
                    src = ps(6 + n % 2).rearrange("p (k t) -> p k t", t=P)[:, :, 0:rows(i)]
                    act.activation(XH[:, 4 * h:4 * h + 4, row0(i):row0(i) + rows(i)], src, ACT.Copy)\
                        .then_inc(s["mt_h"], 1)

            for i in range(NT + 1):
                mix_high(i)
            high_w(NU + 2)
            high_w(NU + 3)

        def dve_tail(dve, link):
            dve.wait_ge(s["br_h"], 1)
            dve.wait_ge(s["job_pe"], JOB0[NU])
            dve.tensor_tensor(BL[:, :, :], BRAW[:, :, :], f(BH[:, :, :]), ALU.subtract).then_inc(s["br_l"], 1)

            def build(n):
                i = n // 2
                c = slice(i * P, (i + 1) * P)
                lo, hi = ps(5, 512, HD).rearrange("p (j t) -> p j t", t=P), ps(5, 512, P, HD).rearrange("p (j t) -> p j t", t=P)
                dve.wait_ge(s["b_h"], n + 1)
                if n % 2 == 0:
                    dve.tensor_tensor(KB[0:HD, :, c], lo, f(KA[0:HD, :, c]), ALU.subtract)
                    dve.tensor_tensor(KA[HD:P, :, c], hi, f(KB[HD:P, :, c]), ALU.subtract).then_inc(s["b_l"], 1)
                else:
                    dve.tensor_tensor(QS[HD:P, 0:AH:2, c], lo, f(QS[0:HD, 0:AH:2, c]), ALU.subtract)
                    dve.tensor_tensor(QS[0:HD, 1:AH:2, c], hi, f(QS[HD:P, 1:AH:2, c]), ALU.subtract)\
                        .then_inc(s["b_l"], 1)

            for m in range(NA + 2):
                for n in BUILD.get(m, []):
                    build(n)
                if m < NA:
                    t, h = m // AH, m % AH
                    dve.wait_ge(s["s_pe"], m + 1)
                    link(dve.reduce_max(MX[:, h:h + 1], ps(2 * (m % 2), P * (t + 1)), axis=AX.X))
                    dve.tensor_scalar(NB[:, h:h + 1], MX[:, h:h + 1], -HD ** -0.5, None, ALU.mult).then_inc(s["s_max"], 1)
                m1 = m - 1
                if 0 <= m1 < NA and m1 % 2 == 1:
                    w = P * (m1 // AH + 1)
                    dve.wait_ge(s["p_pe"], m1 + 1)
                    ge(dve, s["v_pe"], m1 - 1)
                    dve.tensor_copy(PTS[:, m1 % 2, :, :].rearrange("p b t -> p (b t)")[:, 0:w], ps(4, w))\
                        .then_inc(s["p_dve"], 1)
                m2 = m - 2
                if m2 >= 0 and m2 % AH == AH - 1:
                    t = m2 // AH
                    dve.wait_ge(s["v_pe"], m2 + 1)
                    dve.wait_ge(s["s_exp"], m2 + 1)
                    link(dve.reciprocal(RI[:, :], RS[:, t % 2, :]))
                    dve.tensor_tensor(AO[:, t, :].rearrange("p (h d) -> p h d", d=HD),
                                      ps(7).rearrange("p (h d) -> p h d", d=HD), bc(RI[:, :], HD), ALU.mult)\
                        .then_inc(s["ao_done"], 1)
            dve.wait_ge(s["ks_pe"], SB)
            link(dve.reduce_max(MX[0:BR, 0:1], ps(0, PAST + 1, BR), axis=AX.X))
            dve.tensor_scalar(NB[0:BR, 0:1], MX[0:BR, 0:1], -HD ** -0.5, None, ALU.mult).then_inc(s["ks_max"], 1)
            dve.wait_ge(s["ks_exp"], 1)
            link(dve.reciprocal(RI[0:BR, 0:1], RS[0:BR, 0, 0:1]))
            dve.tensor_scalar(PSM[0:BR, 0:PAST + 1], PSM[0:BR, 0:PAST + 1], RI[0:BR, 0:1], None, ALU.mult)\
                .then_inc(s["ks_norm"], 1)

            def mix_rows(i):
                r, sl = rows(i), i % 2
                ge(dve, s["mt_pe"], 2 * (i - 1))
                dve.wait_ge(s["mix_g"], i + 1)
                if i < NT:
                    ho = HOR[0:r, sl, :].rearrange("p (h d) -> p h d", d=HD)
                    link(dve.tensor_tensor(ho, ho, bc(SHO[0:r, 1, i, :], HD), ALU.mult))
                link(dve.tensor_tensor(MIX[0:r, sl, 512:1024], HOR[0:r, sl, :], HGR[0:r, sl, :], ALU.mult))
                if i == NT:
                    dve.wait_ge(s["aos_in"], 16)
                dve.tensor_tensor(MIX[0:r, sl, 0:512], AO[0:r, i, :], AGR[0:r, sl, :], ALU.mult)\
                    .then_inc(s["mix_done"], 1)

            def mix_low(i):
                for h in range(2):
                    n = 2 * i + h
                    dve.wait_ge(s["mt_h"], n + 1)
                    src = ps(6 + n % 2).rearrange("p (k t) -> p k t", t=P)[:, :, 0:rows(i)]
                    c = slice(row0(i), row0(i) + rows(i))
                    dve.tensor_tensor(XL[:, 4 * h:4 * h + 4, c], src, f(XH[:, 4 * h:4 * h + 4, c]), ALU.subtract)\
                        .then_inc(s["mt_l"], 1)

            def add_residual(n):
                r = rows(n % (NT + 1))
                dve.wait_ge(s["job_pe"], JOB0[NU] + n + 1)
                dve.wait_ge(s[f"xr_in{n % 2}"], 16 * (n // 2 + 1))
                ge(dve, s[f"y_out{n % 2}"], 16 * (n // 2))
                dve.tensor_tensor(YST[0:r, n % 2, :], ps((JOB0[NU] + n) % PJ, UW, r), XRS[0:r, n % 2, :], ALU.add)\
                    .then_inc(s["y_add"], 1)

            mix_rows(0)
            for i in range(NT + 1):
                if i < NT:
                        mix_rows(i + 1)
                mix_low(i)
                if i >= 1:
                    add_residual(i - 1)
            for n in range(NT, NUO * (NT + 1)):
                add_residual(n)

        def pe_tail(pe, unit):
            def build(n):
                i, sl = n // 2, (n // 2) % 2
                pe.wait_ge(s["qk_done"], i + 1)
                ge(pe, s["b_l"], n)
                for j in range(4):
                    src = KR[:, sl, j, :, :].rearrange("p a d -> p (a d)") if n % 2 == 0 else QR[:, sl, j * P:(j + 1) * P]
                    last = pe.transpose(ps(5, P, o=j * P), src, IDN[:, :])
                last.then_inc(s["b_pe"], 1)

            def scores(m):
                t, h = m // AH, m % AH
                w = P * (t + 1)
                for n in BUILD.get(m, []):
                    build(n)
                if h == 0:
                    pe.wait_ge(s["b_l"], 2 * (t + 1))
                    if t >= 2:
                        pe.wait_ge(s["masks"], t - 1)
                ge(pe, s["s_exp"], m - 1)
                bank = 2 * (m % 2)
                q = QS[:, h, t * P:(t + 1) * P]
                for c0 in range(0, w, 512):
                    n = min(512, w - c0)
                    pe.matmul(ps(bank, n, o=c0), q, KA[:, h // 2, c0:c0 + n], start=True, stop=False)
                    for kb in (t - 1, t):
                        if kb >= 0 and c0 <= kb * P < c0 + n:
                            for half in (BH, BL):
                                pe.matmul(ps(bank, P, o=kb * P), ANR[:, :], half[:, h, (kb - t + 1) * P:(kb - t + 2) * P],
                                          start=False, stop=False)
                    if t >= 2:
                        pe.matmul(ps(bank, n, o=c0), IDB[:, :], MSK[:, 2 * SC0[t] + c0:2 * SC0[t] + c0 + n],
                                  start=False, stop=False)
                    elif c0 <= t * P < c0 + n:
                        pe.matmul(ps(bank, P, o=t * P), IDB[:, :], TRI[:, :], start=False, stop=False)
                    last = pe.matmul(ps(bank, n, o=c0), q, KB[:, h // 2, c0:c0 + n], start=False, stop=True)
                last.then_inc(s["s_pe"], 1)

            def evacuated(m):
                pe.wait_ge(s["p_dve" if m % 2 else "p_act"], m // 2 + 1)

            def transposes(m):
                pe.wait_ge(s["s_exp"], m + 1)
                if m >= 1:
                    evacuated(m - 1)
                if m == NA // 2:
                    pe.wait_ge(s["b_l"], 2 * NT)
                for b in range(m // AH + 1):
                    last = pe.transpose(ps(4, P, o=b * P), PB[:, m % 3, b * P:(b + 1) * P], IDN[:, :])
                last.then_inc(s["p_pe"], 1)

            def values(m):
                t, h = m // AH, m % AH
                evacuated(m)
                if h == 0:
                    ge(pe, s["ao_done"], t)
                for b in range(t + 1):
                    last = pe.matmul(ps(7, HD, o=h * HD), PTS[:, m % 2, b, :], VT[:, b, h // 2 * HD:(h // 2 + 1) * HD],
                                     start=b == 0, stop=b == t)
                last.then_inc(s["v_pe"], 1)

            pe.wait_ge(s["kv_in"], 16)
            scores(0)
            for m in range(NA):
                if m + 1 < NA:
                    scores(m + 1)
                if m >= 1:
                    values(m - 1)
                transposes(m)
            values(NA - 1)
            pe.wait_ge(s["sm_in"], 16)
            pe.wait_ge(s["qk_done"], NT + 1)
            for j in range(6):
                rows_ = QR[0:SB, 0, j * P:(j + 1) * P] if j < 4 else SQ[0:SB, (j - 4) * P:(j - 3) * P]
                last = pe.transpose(ps(6, SB, o=8 * j), rows_, IDN[0:SB, 0:SB])
            last.then_inc(s["sm_pe"], 1)
            pe.wait_ge(s["sm_act"], 1)
            pe.wait_ge(s["masks"], 7)
            for b in range(SB):
                pe.wait_ge(s[f"kc_in{b % 2}"], 128 * (b // 2 + 1))
                for blk in range(2):
                    q = QPD[:, blk, b, :]
                    first, final = b == 0 and blk == 0, b == SB - 1 and blk == 1
                    for c in range(2):
                        pe.matmul(ps(c, 512, BR), q, KS_[:, b % 2, blk, c * 512:(c + 1) * 512], start=first, stop=final)
                    last = pe.matmul(ps(2, 1, BR), q, KNW[:, blk, b:b + 1], start=first, stop=final)
                    if first:
                        for c, w in ((0, 512), (1, 512), (2, 1)):
                            pe.matmul(ps(c, w, BR), E8B[0:8, :], MSKS[0:8, c * 512:c * 512 + w], start=False, stop=False)
                        pe.matmul(ps(1, P, BR, o=512 - P), E8H[0:8, :], UT[0:8, P - 1:2 * P - 1], start=False, stop=False)
                        pe.matmul(ps(2, 1, BR), E8H[0:8, :], UT[0:8, 2 * P - 1:2 * P], start=False, stop=False)
                last.then_inc(s["ks_pe"], 1)
            pe.wait_ge(s["ks_norm"], 1)
            for g in range(NPG):
                pe.transpose(ps(4, BR, o=g * BR), PSM[0:BR, g * P:(g + 1) * P], IDN[0:BR, 0:BR])
            pe.transpose(ps(5, BR, 1), PSM[0:BR, PAST:PAST + 1], IDN[0:BR, 0:BR]).then_inc(s["pt_pe"], 1)
            for n in range(SB * NG):
                last = pe.matmul(ps(6, HD, BR, o=256), QHP[:, n, :], S0T[:, n // NG, n % NG, :], start=n == 0,
                                 stop=n == SB * NG - 1)
            last.then_inc(s["hs_pe"], 1)
            pe.wait_ge(s["pt_act"], 1)
            for b in range(SB):
                pe.wait_ge(s[f"vc_in{b % 2}"], 128 * (b // 2 + 1))
                dst = ps(b // 2, UW, SB, o=b % 2 * UW)
                for g in range(NPG):
                    pe.matmul(dst, PTP[:, g, 8 * b:8 * b + 8], VS_[:, b % 2, g, :], start=g == 0, stop=False)
                pe.matmul(dst, PTN[0:1, 8 * b:8 * b + 8], VN1[0:1, b, :], start=False, stop=True).then_inc(s["vs_pe"], 1)
            pe.wait_ge(s["hs_act"], 1)
            pe.wait_ge(s["vs_act"], 1)

            def transpose_mix(i):
                pe.wait_ge(s["mix_done"], i + 1)
                for h in range(2):
                    n = 2 * i + h
                    ge(pe, s["mt_l"], n - 1)
                    for k in range(4):
                        last = pe.transpose(ps(6 + n % 2, rows(i), o=k * P), MIX[0:rows(i), i % 2, (4 * h + k) * P:(4 * h + k + 1) * P],
                                            IDN[0:rows(i), 0:rows(i)])
                    last.then_inc(s["mt_pe"], 1)

            transpose_mix(0)
            for u in range(NU, NU + NUO):
                unit(u, transpose_mix)

        @block.sync
        def _(sp):
            for dst, src in ((IDN[:, :], c_ident), (LNG[:, :], ln_g), (LBR[:, :, :], lbs), (BITF[:, :], c_bits),
                             (QG[:, :], q_g), (KG[:, :], k_g), (HNG[:, :], hn_g), (PT_[0:1, :], pages),
                             (E8[0:8, :], c_e8[0]), (E8H[0:8, :], c_e8[1]), (OH[0:32, :], c_oh), (REL[0:32, :], rel),
                             (INM[:, :, :], c_masks[:, 0:256]), (BM[:, :], c_masks[:, 256:384]),
                             (HM[0:BR, :], c_masks[0:BR, 384:400]), (TRF[:, :], c_masks[:, 400:528]), (ANT[:, :], c_masks[:, 528:656])):
                sp.dma_start(dst, src).then_inc(s["const_in"], 16)
            NCONST = 17 * 16

            def load_x(g):
                for i in range(3 * g, 3 * g + 3):
                    if i >= 6:
                        ge(sp, s["xt_t"], 2 * (i - 5))
                    sp.dma_start(XB[0:rows(i), i % 6, :], x_rows(i)).then_inc(s[f"x_in{g}"], 16)

            def load_index_keys(b):
                slot = (b // 2) % 2
                if b >= 4:
                    ge(sp, s["samp_pe"], b // 2 - 1)
                for g in range(NPG):
                    page = sp.value_load(PT_[0:1, b * NPG + g:b * NPG + g + 1], min_val=0, max_val=NPOOL - 1)
                    sp.dma_start(IKT[b % 2 * HD:b % 2 * HD + HD, slot, g * P:(g + 1) * P],
                                 cache_ikt[bass.ds(page, 1)].rearrange("a d k -> (a d) k"))\
                        .then_inc(s[f"ikc_in{slot}"], 16)

            load_x(0)
            load_weights(sp, 0)
            load_x(1)
            load_weights(sp, 1)
            load_x(2)
            ge(sp, s["const_in"], NCONST)
            staged = 0
            for u in range(NU):
                kind, a = UNITS[u]
                if u + 2 < NU:
                    load_weights(sp, u + 2)
                if u == 0:
                    for b in range(4):
                        load_index_keys(b)
                if u == UIX:
                    sp.wait_ge(s["ik_rows"], 3)
                    sp.dma_start(ik_prompt[0, 0].rearrange("(t p) d -> p t d", p=P), IKN[:, 0:NT, :])\
                        .then_inc(s["out_done"], 16)
                    sp.dma_start(ik_sample[0, :, 0, :], IKN[0:SB, NT, :]).then_inc(s["out_done"], 16)
                    for b in range(4, SB):
                        load_index_keys(b)
                    ge(sp, s["tab_act"], 1)
                    sp.dma_start(d_ut.ap(), UT[0:AH, :]).then_inc(s["tab_out"], 16)
                if u == NU - 1:
                    sp.wait_ge(s["tab_out"], 16)
                    sp.wait_ge(s["prep_done"], NG)
                    sp.dma_start(BRAW[:, :, :], bass.AP(d_ut, 0, [[1, P], [UL, AH], [1, NEAR]])).then_inc(s["braw_in"], 16)
                    load_rows(sp, 0)
                    load_rows(sp, 1)
                for i in range(NT + 1):
                    n = JOB0[u] + i
                    if kind in STAGED:
                        ge(sp, s["job_act"], n + 1)
                        dst = {"gh": d_gh, "ga": d_ga, "q": d_q, "k": d_k}.get(kind)
                        if kind == "v":
                            dst = v_prompt[0, 0, i * P:(i + 1) * P].rearrange("t h d -> t (h d)") if i < NT \
                                else v_sample[0, :, 0].rearrange("t h d -> t (h d)")
                        else:
                            dst = dst[row0(i):row0(i) + rows(i), a * UW:(a + 1) * UW]
                        sp.dma_start(dst, STG[0:rows(i), staged % 4, :]).then_inc(s[f"stg_out{staged % 4}"], 16)
                        staged += 1
                if kind == "hv":
                    ge(sp, s["job_act"], JOB0[u + 1])
                    sp.dma_start(d_hv.ap()[:, a * UW:(a + 1) * UW], HV[0:SB, NT, a * UW:(a + 1) * UW])\
                        .then_inc(s["hv_out"], 16)
                if u - 3 in HGU:
                    j = HGU.index(u - 3)
                    ge(sp, s["o_act"], NT * (j + 1))
                    sp.dma_start(d_ho[0:T, j * P:(j + 1) * P].rearrange("(c s) n -> s c n", s=P), HO[:, :, :])\
                        .then_inc(s["ho_out"], 16)
            ge(sp, s["st_gp"], NT * NG)
            for hh in range(2):
                sp.dma_start(s_prompt[0, 0].rearrange("(j a) k v -> a k j v", a=2)[hh],
                             ST[hh * HD:(hh + 1) * HD, :, hh * HD:(hh + 1) * HD]).then_inc(s["out_done"], 16)
            sp_tail(sp)

        @block.gpsimd
        def _(gp):
            chain = [0]

            def link(ins):
                chain[0] += 1
                ins.then_inc(s["gp_chain"], 1)
                gp.wait_ge(s["gp_chain"], chain[0])

            gp.memset(IQP[:, :, :], 0.0).then_inc(s["init_gp"], 1)
            gp.memset(RM[:, :], 1.0).then_inc(s["init_gp"], 1)
            gp.wait_ge(s["init_gp"], 2)
            gp.memset(RM[:, 0:T:P], 0.0).then_inc(s["init_gp"], 1)
            gp.wait_ge(s["const_in"], NCONST_)

            def prep(j):
                u = HGU[j]
                gp.wait_ge(s["job_act"], JOB0[u + 1])
                if j == 0:
                    gp.wait_ge(s["lb_done"], 1)
                gp.tensor_scalar(FB[:, :], FB[:, :], OML[:, j:j + 1], LB[:, j:j + 1], ALU.mult, ALU.add)\
                    .then_inc(s["f_gp"], 1)
                gp.tensor_scalar(FS[:, j, :], FS[:, j, :], OML[:, j:j + 1], LB[:, j:j + 1], ALU.mult, ALU.add)\
                    .then_inc(s["f_gp"], 1)
                gp.tensor_scalar(QB[:, :], QB[:, :], HD ** -0.5, 0.0, ALU.mult, ALU.add).then_inc(s["f_gp"], 1)
                gp.tensor_scalar(QSS[:, j, :], QSS[:, j, :], HD ** -0.5, 0.0, ALU.mult, ALU.add)\
                    .then_inc(s["f_gp"], 1)
                gp.wait_ge(s["f_gp"], 6 * j + 4)
                gp.tensor_scalar(HK[:, :], FB[:, :], -1.0, 1.0, ALU.mult, ALU.add).then_inc(s["f_gp"], 1)
                gp.tensor_scalar(KSS[:, j, :], FS[:, j, :], -1.0, 1.0, ALU.mult, ALU.add).then_inc(s["f_gp"], 1)
                gp.wait_ge(s["scan_done"], j + 1)
                ge(gp, s["o_pe"], NT * j)
                ge(gp, s["st_gp"], NT * j)
                b4 = FB[:, :].rearrange("p (n t) -> p n t", t=SUB)
                ref = b4[:, :, SUB // 2 - 1]
                for hh in range(2):
                    r = slice(hh * HD, hh * HD + HD)
                    link(gp.tensor_tensor(QT[r, hh, :].rearrange("p (n t) -> p n t", t=SUB), b4[r],
                                          bc(ref[r], SUB), ALU.subtract))
                b8 = FB[:, :].rearrange("p (c t) -> p c t", t=P)
                o = 0
                for i in range(NSUB):
                    w = SUB * (i + 1)
                    gp.tensor_tensor(KT[:, o:o + NT * w].rearrange("p (c t) -> p c t", t=w),
                                     bc(ref[:, i:NT * NSUB:NSUB], w), b8[:, :, 0:w], ALU.subtract)
                    o += NT * w
                gp.tensor_tensor(DE[:, 1, :], b8[:, :, P - 1], ref[:, NSUB - 1:NT * NSUB:NSUB], ALU.subtract)
                gp.tensor_scalar(DE[:, 0, :], b8[:, :, P - 1], 1.0, 0.0, ALU.mult, ALU.add).then_inc(s["d_gp"], 1)
                gp.wait_ge(s["e_act"], j + 1)
                for hh in range(2):
                    r = slice(hh * HD, hh * HD + HD)
                    link(gp.tensor_tensor(QT[r, hh, :], QT[r, hh, :], QB[r, :], ALU.mult))
                gp.tensor_tensor(QI[:, :], QI[:, :], QB[:, :], ALU.mult)
                k8 = HK[:, :].rearrange("p (c t) -> p c t", t=P)
                o = 0
                for i in range(NSUB):
                    w = SUB * (i + 1)
                    kt = KT[:, o:o + NT * w].rearrange("p (c t) -> p c t", t=w)
                    last = gp.tensor_tensor(kt, kt, k8[:, :, 0:w], ALU.mult)
                    o += NT * w
                last.then_inc(s["prep_done"], 1)

            def chunk(kind, j, c):
                n = NT * j + c
                if kind == "intra":
                    gp.wait_ge(s["at_act"], n + 1)
                    gp.tensor_tensor(ATB[:, n % 2], ATB[:, n % 2], INM[:, :, :], ALU.mult).then_inc(s["at_gp"], 1)
                elif kind == "keys":
                    gp.wait_ge(s["u_act"], n + 1)
                    gp.tensor_tensor(TMP[:, n % 2, :], TMP[:, n % 2, :], BM[:, :], ALU.mult).then_inc(s["tmp_gp"], 1)
                else:
                    gp.wait_ge(s["o_pe"], n + 1)
                    gp.wait_ge(s["tmp_gp"], n + 1)
                    link(gp.tensor_scalar(ST[:, j, :], ST[:, j, :], DE[:, 0, c:c + 1], 0.0, ALU.mult, ALU.add))
                    gp.tensor_tensor(ST[:, j, :], ST[:, j, :], TMP[:, n % 2, :], ALU.add).then_inc(s["st_gp"], 1)

            split_w(gp, 0)
            for u in range(NU):
                if u + 1 < NU:
                    split_w(gp, u + 1)
                if u == UIX:
                    for t in range(2, NT):
                        gp.wait_ge(s["sc_acc"], IH * (t - 1))
                        diag = SC[:, SC0[t] + P * t:SC0[t] + P * (t + 1)]
                        gp.affine_select(out=diag, in_=diag, compare_op=ALU.is_ge, fill=UNSEEN, base=0,
                                         pattern=[[-1, P]], channel_multiplier=1).then_inc(s["sc_seen"], 1)
                    gp.wait_ge(s["samp_sc"], 1)
                    gp.wait_ge(s["sc_pe"], IH * 6)
                    gp.wait_ge(s["tab_pe"], 1)
                    gp.wait_ge(s["out_done"], 32)
                    gp.memset(ATB[:, :, :, :], 0.0)
                    gp.memset(QT[:, :, :], 0.0)
                    gp.memset(ST[:, :, :], 0.0).then_inc(s["init_gp"], 1)
                    gp.wait_ge(s["init_gp"], 4)
                if u - 1 in HGU:
                    prep(HGU.index(u - 1))
                for n in range(JOB0[u], JOB0[u + 1]):
                    for event in EVENTS.get(n, ()):
                        chunk(*event)
            gp_tail(gp, link)

        @block.scalar
        def _(act):
            chain = [0]

            def link(ins):
                chain[0] += 1
                ins.then_inc(s["act_chain"], 1)
                act.wait_ge(s["act_chain"], chain[0])

            act.wait_ge(s["const_in"], NCONST_)
            act.wait_ge(s["init_dve"], 2)
            act.activation(ANR[:, :], ANT[:, :], ACT.Copy)
            act.activation(IDB[:, :], IDN[:, :], ACT.Copy)
            act.activation(E8B[0:8, :], E8[0:8, :], ACT.Copy)
            act.activation(TRI[:, :], TRF[:, :], ACT.Copy).then_inc(s["init_act"], 1)
            act.activation(LB[:, :], OML[:, :], ACT.Sigmoid).then_inc(s["lb_act"], 1)

            def squares(g):
                act.wait_ge(s[f"x_in{g}"], 48)
                for i in range(3 * g, 3 * g + 3):
                    r = rows(i)
                    ge(act, s["ss_done"], i)
                    act.activation(JA[0:r, :], XB[0:r, i % 6, :], ACT.Square,
                                   accum_out=STAT[0:r, 0, i:i + 1]).then_inc(s["ss_done"], 1)

            def high_x(g):
                for i in range(3 * g, 3 * g + 3):
                    for h in range(2):
                        n = 2 * i + h
                        act.wait_ge(s["xt_t"], n + 1)
                        src = ps(6 + n % 2).rearrange("p (k t) -> p k t", t=P)[:, :, 0:rows(i)]
                        act.activation(XH[:, 4 * h:4 * h + 4, row0(i):row0(i) + rows(i)], src, ACT.Copy)\
                            .then_inc(s["xt_h"], 1)

            def high_w(u):
                w = width(u)
                if NU > u >= 2:
                    act.wait_ge(s["job_pe"], JOB0[u - 1])
                if u > NU + 1:
                    act.wait_ge(s["job_pe"], JOB0[u - 1])
                for h in range(2):
                    if u < NU:
                        act.wait_ge(s["wg_done"], 2 * u + h + 1)
                    else:
                        act.wait_ge(s[f"w_in{h}"], 16 * (u + 1))
                    act.activation(WH[:, u % 2, 4 * h:4 * h + 4, 0:w], WR[:, h, :, 0:w], ACT.Copy)\
                        .then_inc(s["wh_done"], 1)

            def prep_log(j):
                act.wait_ge(s["f_gp"], 6 * (j + 1))
                act.activation(FB[:, :], FB[:, :], ACT.Ln).then_inc(s["f_ln"], 1)

            def prep_exp(j):
                act.wait_ge(s["d_gp"], j + 1)
                for hh in range(2):
                    r = slice(hh * HD, hh * HD + HD)
                    act.activation(QT[r, hh, :], QT[r, hh, :], ACT.Exp)
                act.activation(QI[:, :], FB[:, :], ACT.Exp)
                act.activation(KT[:, :], KT[:, :], ACT.Exp)
                act.activation(DE[:, :, :], DE[:, :, :], ACT.Exp).then_inc(s["e_act"], 1)

            def chunk(kind, j, c):
                n = NT * j + c
                if kind == "intra":
                    act.wait_ge(s["a_pe"], n + 1)
                    ge(act, s["o_pe"], n - 1)
                    src = ps(6 + n % 2, 256).rearrange("p (i h t) -> p i h t", h=2, t=SUB)
                    for i in range(NSUB):
                        w = SUB * (i + 1)
                        act.activation(ATB[0:w, n % 2, :, i * SUB:(i + 1) * SUB], src[0:w, i], ACT.Copy)
                    act.activation(KTN[:, n % 2, :], ps(6 + n % 2, P, o=256), ACT.Copy).then_inc(s["at_act"], 1)
                elif kind == "keys":
                    act.wait_ge(s["u_pe"], n + 1)
                    ge(act, s["st_gp"], n - 1)
                    act.activation(TMP[:, n % 2, :], ps(5, P), ACT.Copy, scale=DE[:, 1, c:c + 1])\
                        .then_inc(s["u_act"], 1)
                else:
                    act.wait_ge(s["o_pe"], n + 1)
                    if c == 0:
                        ge(act, s["ho_out"], 16 * j)
                    for hh in range(2):
                        act.activation(ps(4, HD, o=P + hh * HD), ps(4, HD, o=hh * HD), ACT.Square,
                                       accum_out=SHO[:, 0, c, 2 * j + hh:2 * j + hh + 1])
                    act.activation(HO[:, c, :], ps(4, P), ACT.Copy).then_inc(s["o_act"], 1)

            staged = [0]

            def evac(u, q):
                kind, a = UNITS[u]
                form, i, c = jobs(u)[q]
                n = JOB0[u] + q
                act.wait_ge(s["job_pe"], n + 1)
                bank = n % PJ
                r = rows(i) if form == "N" else P
                if kind == "iq":
                    t0, cw = CHUNKS[c]
                    lo, hi = max(2 * P - t0, 0), min(T - t0, cw)
                    j = 2 * a + i
                    dst = slice(t0 + lo - 2 * P, t0 + hi - 2 * P)
                    act.activation(IQS[0:HD, 2 * j, dst], ps(bank, hi - lo, HD, o=lo), ACT.Copy)
                    last = act.activation(IQS[HD:P, 2 * j + 1, dst], ps(bank, hi - lo, P, HD, lo), ACT.Copy)
                    if c == 2:
                        act.wait_ge(s["init_gp"], 1)
                        iqp = IQP[:, :, :].rearrange("p a b -> p (a b)")
                        for hh in range(2):
                            for b2 in range(2):
                                last = act.activation(
                                    iqp[b2 * HD:(b2 + 1) * HD, 8 * b2 + 2 * j + hh:4 * BR:BR + 16],
                                    ps(bank, SB, (hh + 1) * HD, hh * HD, 256)[:, b2:SB:2], ACT.Copy)
                elif kind == "ix":
                    t0, cw = CHUNKS[c]
                    hi = min(T - t0, cw)
                    act.activation(IXT[0:XW, t0:t0 + cw], ps(bank, cw, XW), ACT.Copy)
                    act.activation(IA[0:HD, t0:t0 + hi], ps(bank, hi, HD), ACT.Copy)
                    last = act.activation(IB[HD:P, t0:t0 + hi], ps(bank, hi, HD), ACT.Copy)
                elif kind == "hg":
                    t0, cw = CHUNKS[c]
                    hi = min(T - t0, cw)
                    dst, samp, fn = ((FB, FS, ACT.Sigmoid), (QB, QSS, ACT.Silu))[i]
                    if q == 0 and a > 0:
                        act.wait_ge(s["prep_done"], a)
                    last = act.activation(dst[:, t0:t0 + hi], ps(bank, hi), fn)
                    if c == 2:
                        last = act.activation(samp[:, a, :], ps(bank, SB, o=hi), fn)
                elif kind == "hv":
                    last = act.activation(HV[0:r, i, a * UW:(a + 1) * UW], ps(bank, UW, r), ACT.Copy)
                elif kind in STAGED:
                    g = staged[0]
                    ge(act, s[f"stg_out{g % 4}"], 16 * (g // 4))
                    last = act.activation(STG[0:r, g % 4, :], ps(bank, UW, r),
                                          ACT.Silu if kind in ("gh", "ga") else ACT.Copy)
                    if kind in ("q", "k"):
                        h0 = AH if kind == "k" else a * 4
                        for h in range(4):
                            last = act.activation(ps(bank, HD, r, o=UW + h * HD), ps(bank, HD, r, o=h * HD), ACT.Square,
                                                  accum_out=SQK[0:r, 0, i, h0 + h:h0 + h + 1])
                    staged[0] += 1
                last.then_inc(s["job_act"], 1)

            act.wait_ge(s["tab_pe"], 1)
            act.activation(UT[0:AH, :], ps(6, UL, AH), ACT.Copy, scale=8.0).then_inc(s["tab_act"], 1)
            squares(0)
            high_w(0)
            squares(1)
            high_x(0)
            squares(2)
            high_x(1)
            high_x(2)
            for u in range(NU):
                if u + 1 < NU:
                    high_w(u + 1)
                for q in range(len(jobs(u))):
                    evac(u, q)
                    if u - 1 in HGU and q == 1:
                        prep_log(HGU.index(u - 1))
                    for event in EVENTS.get(JOB0[u] + q, ()):
                        chunk(*event)
                if u - 1 in HGU:
                    prep_exp(HGU.index(u - 1))
                if u == UIX:
                    act.wait_ge(s["job_act"], JOB0[UIX + 1])
                    act.activation(IKNEW[0:HD, :], IXT[0:HD, T:TT:2], ACT.Copy)
                    act.activation(IKNEW[HD:P, :], IXT[0:HD, T + 1:TT:2], ACT.Copy).then_inc(s["ik_h"], 1)
                    for g, (lo, hi) in enumerate(((0, 5), (5, NT), (NT, NT + 1))):
                        act.wait_ge(s["ik_t"], min(g, 1) + 1)
                        r = rows(lo)
                        src = ps(6 + min(g, 1), 512, r)[:, (lo - 5 * min(g, 1)) * XW:(hi - 5 * min(g, 1)) * XW]\
                            .rearrange("p (i n) -> p i n", n=XW)
                        act.activation(IW[0:r, lo:hi, :], src[:, :, HD:XW], ACT.Copy, scale=float(IH ** -0.5 * HD ** -0.5))
                        act.activation(IKN[0:r, lo:hi, :], src[:, :, 0:HD], ACT.Copy).then_inc(s["ik_rows"], 1)
                    for m in range(IH * 6):
                        w = P * (m // IH + 3)
                        act.wait_ge(s["sc_pe"], m + 1)
                        ge(act, s["sc_acc"], m - 1)
                        act.activation(RB[:, m % 2, 0:w], ps(2 * (m % 2), w), ACT.Relu).then_inc(s["sc_relu"], 1)
                    act.wait_ge(s["out_done"], 32)
                    act.wait_ge(s["samp_pe"], 4)
                    act.activation(RSM[0:BR, :], ps(4, PAST + 1, BR), ACT.Relu).then_inc(s["samp_relu"], 1)
            act_tail(act, link, high_w)

        @block.vector
        def _(dve):
            chain = [0]

            def link(ins):
                chain[0] += 1
                ins.then_inc(s["dve_chain"], 1)
                dve.wait_ge(s["dve_chain"], chain[0])

            dve.memset(STAT[:, 0, :], 1.0)
            dve.memset(EPSC[:, :], EPS)
            dve.memset(ONE[:, :], 1.0)
            dve.memset(SQK[:, 0, :, :], 1.0)
            dve.memset(CNT[:, :], 0.0)
            dve.memset(U[:, :], 0).then_inc(s["init_dve"], 1)
            dve.wait_ge(s["init_dve"], 1)
            dve.wait_ge(s["const_in"], NCONST_)
            dve.tensor_copy(BITI[:, :], BITF[:, :])
            dve.tensor_tensor(OML[:, :], LBR[:, 0, :], LBR[:, 1, :], ALU.subtract).then_inc(s["init_dve"], 1)
            dve.wait_ge(s["lb_act"], 1)
            dve.tensor_scalar(OML[:, :], LB[:, :], -1.0, 1.0, ALU.mult, ALU.add).then_inc(s["lb_done"], 1)

            def x_norm(g):
                c = slice(3 * g, 3 * g + 3)
                dve.wait_ge(s["ss_done"], 3 * g + 3)
                link(dve.tensor_scalar(STAT[:, 1, c], STAT[:, 0, c], 1.0 / D, EPS, ALU.mult, ALU.add))
                inverse_root(dve, link, STAT[:, 3, c], STAT[:, 1, c], STAT[:, 2, c])
                for i in range(3 * g, 3 * g + 3):
                    r = rows(i)
                    dve.tensor_scalar(XB[0:r, i % 6, :], XB[0:r, i % 6, :], STAT[0:r, 3, i:i + 1], None, ALU.mult)\
                        .then_inc(s["xn_done"], 1)

            def low_x(g):
                for i in range(3 * g, 3 * g + 3):
                    for h in range(2):
                        n = 2 * i + h
                        dve.wait_ge(s["xt_h"], n + 1)
                        src = ps(6 + n % 2).rearrange("p (k t) -> p k t", t=P)[:, :, 0:rows(i)]
                        c = slice(row0(i), row0(i) + rows(i))
                        dve.tensor_tensor(XL[:, 4 * h:4 * h + 4, c], src, f(XH[:, 4 * h:4 * h + 4, c]), ALU.subtract)\
                            .then_inc(s["xt_l"], 1)

            x_norm(0)
            x_norm(1)
            low_x(0)
            x_norm(2)
            low_x(1)
            low_x(2)
            for u in range(UIX):
                for q, (form, i, c) in enumerate(jobs(u)):
                    n = JOB0[u] + q
                    t0, cw = CHUNKS[c]
                    lo, hi = max(2 * P - t0, 0), min(T - t0, cw)
                    j = 2 * UNITS[u][1] + i
                    dst = slice(t0 + lo - 2 * P, t0 + hi - 2 * P)
                    dve.wait_ge(s["job_act"], n + 1)
                    dve.tensor_tensor(IQS[HD:P, 2 * j, dst], ps(n % PJ, hi - lo, HD, o=lo), f(IQS[0:HD, 2 * j, dst]),
                                      ALU.subtract)
                    dve.tensor_tensor(IQS[0:HD, 2 * j + 1, dst], ps(n % PJ, hi - lo, P, HD, lo),
                                      f(IQS[HD:P, 2 * j + 1, dst]), ALU.subtract).then_inc(s["iq_low"], 1)
            for c, (t0, cw) in enumerate(CHUNKS):
                n = JOB0[UIX] + c
                hi = min(T - t0, cw)
                dve.wait_ge(s["job_act"], n + 1)
                for stack in (IB[0:HD, t0:t0 + hi], IA[HD:P, t0:t0 + hi]):
                    ins = dve.tensor_tensor(stack, ps(n % PJ, hi, HD), f(IA[0:HD, t0:t0 + hi]), ALU.subtract)
                ins.then_inc(s["ik_l"], 1)
            dve.wait_ge(s["iw_pe"], 1)
            link(dve.tensor_tensor(HMT[0:BR, :], ps(7, IH, BR), HM[0:BR, 0:8], ALU.mult))
            link(dve.reduce_sum(IWC[0:BR, :], HMT[0:BR, :], axis=AX.X))
            dve.tensor_scalar(WSEL[0:BR, :], HM[0:BR, 8:16], IWC[0:BR, 0:1], None, ALU.mult).then_inc(s["iw_sel"], 1)
            for m in range(IH * 6):
                t, h = m // IH + 2, m % IH
                w = P * (t + 1)
                sc = SC[:, SC0[t]:SC0[t] + w]
                dve.wait_ge(s["sc_relu"], m + 1)
                if h == 0:
                    ins = dve.tensor_scalar(sc, RB[:, m % 2, 0:w], IW[:, t, h:h + 1], None, ALU.mult)
                else:
                    dve.wait_ge(s["sc_acc"], m)
                    ins = dve.scalar_tensor_tensor(sc, RB[:, m % 2, 0:w], IW[:, t, h:h + 1], sc, ALU.mult, ALU.add)
                ins.then_inc(s["sc_acc"], 1)

            dve.wait_ge(s["samp_w"], 1)
            dve.tensor_copy(SCS[0:SB, 0:PAST + 1], ps(0, PAST + 1, SB)).then_inc(s["samp_sc"], 1)
            dve.wait_ge(s["sc_seen"], 6)
            dve.wait_ge(s["samp_sc"], 1)
            tiles = [(t - 2, P, SC[:, SC0[t]:SC0[t] + P * (t + 1)], P * (t + 1)) for t in range(2, NT)]
            tiles.append((6, SB, SCS[0:SB, 0:PAST + 1], PAST + 1))

            def count(threshold, op, done):
                for k, r, sc, w in tiles:
                    dve.tensor_scalar(JK[0:r, 0:w], sc, threshold(k, r), None, op, ALU.add,
                                      accum_out=CNT[0:r, k:k + 1]).then_inc(s["dve_chain"], 1)
                    dve.wait_ge(s["dve_chain"], done + k + 1)

            count(lambda k, r: 0.0, ALU.is_ge, chain[0])
            chain[0] += 7
            link(dve.tensor_scalar(XM[:, :], CNT[:, :], float(TOPK), -1.0, ALU.is_lt, ALU.mult))
            def rounds(a, b):
                start = chain[0]
                with dve.Fori(a, b) as it:
                    done = (it - a) * 10 + start
                    dve.scalar_tensor_tensor(CAND[:, :], U[:, :], BITI[:, bass.ds(it, 1)], XM[:, :],
                                             ALU.bitwise_or, ALU.bitwise_xor).then_inc(s["dve_chain"], 1)
                    dve.wait_ge(s["dve_chain"], done + 1)
                    count(lambda k, r: CAND[0:r, k:k + 1].bitcast(F32), ALU.is_ge, done + 1)
                    dve.tensor_scalar(HIT[:, :], CNT[:, :], float(TOPK), BITF[:, bass.ds(it, 1)],
                                      ALU.is_ge, ALU.mult).then_inc(s["dve_chain"], 1)
                    dve.wait_ge(s["dve_chain"], done + 9)
                    dve.tensor_tensor(U[:, :], U[:, :], HIT[:, :], ALU.bitwise_or).then_inc(s["dve_chain"], 1)
                    dve.wait_ge(s["dve_chain"], done + 10)
                chain[0] = start + 10 * (b - a)

            def scan(j):
                dve.wait_ge(s["f_ln"], j + 1)
                dve.tensor_tensor_scan(FB[:, :], RM[:, :], FB[:, :], 0.0, ALU.mult, ALU.add)\
                    .then_inc(s["scan_done"], 1)

            def masks():
                link(dve.tensor_tensor(CAND[:, :], U[:, :], XM[:, :], ALU.bitwise_xor))
                count(lambda k, r: CAND[0:r, k:k + 1].bitcast(F32), ALU.is_gt, chain[0])
                chain[0] += 7
                link(dve.tensor_scalar(NEED[:, :], CNT[:, :], -1.0, float(TOPK), ALU.mult, ALU.add))
                for k, r, sc, w in tiles:
                    thr = CAND[0:r, k:k + 1].bitcast(F32)
                    link(dve.tensor_scalar(JK[0:r, 0:w], sc, thr, None, ALU.is_equal))
                    link(dve.tensor_tensor_scan(CU[0:r, 0:w], JK[0:r, 0:w], JK[0:r, 0:w], 0.0, ALU.add, ALU.max))
                    link(dve.scalar_tensor_tensor(CU[0:r, 0:w], CU[0:r, 0:w], NEED[0:r, k:k + 1], JK[0:r, 0:w],
                                                  ALU.is_le, ALU.mult))
                    link(dve.scalar_tensor_tensor(JK[0:r, 0:w], sc, thr, CU[0:r, 0:w], ALU.is_gt, ALU.add))
                    m = MSK[:, 2 * SC0[k + 2]:2 * SC0[k + 2] + w] if k < 6 else MSKS[0:SB, 0:w]
                    dve.tensor_scalar(m, JK[0:r, 0:w], -1.0, -NEG, ALU.add, ALU.mult).then_inc(s["masks"], 1)
                    dve.wait_ge(s["masks"], k + 1)

            rounds(0, 4)
            scan(0)
            rounds(4, 13)
            scan(1)
            rounds(13, 22)
            scan(2)
            rounds(22, ROUNDS)
            masks()
            scan(3)
            dve_tail(dve, link)

        @block.tensor
        def _(pe):
            pe.wait_ge(s["const_in"], NCONST_)
            pe.matmul(ps(6, UL, AH), REL[0:32, :], OH[0:32, :], start=True, stop=True).then_inc(s["tab_pe"], 1)

            def transpose_x(i):
                pe.wait_ge(s["xn_done"], i + 1)
                for h in range(2):
                    n = 2 * i + h
                    ge(pe, s["xt_l"], n - 1)
                    if n == 0:
                        pe.wait_ge(s["tab_act"], 1)
                    for k in range(4):
                        last = pe.transpose(ps(6 + n % 2, rows(i), o=k * P), XB[0:rows(i), i % 6, (4 * h + k) * P:(4 * h + k + 1) * P],
                                            IDN[0:rows(i), 0:rows(i)])
                    last.then_inc(s["xt_t"], 1)

            def chunk(kind, j, c):
                n = NT * j + c
                bank = 6 + n % 2
                v = HV[:, c, j * P:(j + 1) * P]
                if kind == "intra":
                    if c == 0:
                        pe.wait_ge(s["prep_done"], j + 1)
                    ge(pe, s["at_act"], n - 1)
                    o = 0
                    for i in range(NSUB):
                        w = SUB * (i + 1)
                        pe.matmul(ps(bank, 2 * SUB, w, o=2 * SUB * i), KT[:, o + c * w:o + (c + 1) * w],
                                  QT[:, :, c * P + i * SUB:c * P + (i + 1) * SUB], start=True, stop=True)
                        o += NT * w
                    o -= NT * P
                    pe.transpose(ps(bank, P, o=256), KT[:, o + c * P:o + (c + 1) * P], IDN[:, :]).then_inc(s["a_pe"], 1)
                elif kind == "keys":
                    pe.wait_ge(s["at_act"], n + 1)
                    ge(pe, s["u_act"], n)
                    pe.matmul(ps(5, P), KTN[:, n % 2, :], v, start=True, stop=True).then_inc(s["u_pe"], 1)
                else:
                    ge(pe, s["st_gp"], n)
                    ge(pe, s["o_act"], n)
                    if n == 0:
                        pe.wait_ge(s["init_gp"], 4)
                    pe.matmul(ps(4, P), QI[:, c * P:(c + 1) * P], ST[:, j, :], start=True, stop=False)
                    pe.wait_ge(s["at_gp"], n + 1)
                    for hh in range(2):
                        last = pe.matmul(ps(4, HD, o=hh * HD), ATB[:, n % 2, hh, :], v[:, hh * HD:(hh + 1) * HD],
                                         start=False, stop=hh == 1)
                    last.then_inc(s["o_pe"], 1)

            def unit(u, transpose_mix=None):
                w = width(u)
                sl = u % 2
                pe.wait_ge(s["wl_done"], 2 * u + 2)
                for q, (form, i, c) in enumerate(jobs(u)):
                    n = JOB0[u] + q
                    m = n - PJ
                    if u == NU and q < NT:
                        transpose_mix(q + 1)
                    if m >= JOB0[NU]:
                        pe.wait_ge(s["y_add"], m - JOB0[NU] + 1)
                    elif m >= 0:
                        pe.wait_ge(s["job_act"], m + 1)
                        if m < JOB0[UIX]:
                            pe.wait_ge(s["iq_low"], m + 1)
                    if u == 0:
                        pe.wait_ge(s["xt_l"], 6 * (c + 1))
                    if u >= NU:
                        pe.wait_ge(s["mt_l"], 2 * (i + 1))
                    for k in range(KC):
                        for x, ww in ((XH, WH), (XL, WH), (XH, WL)):
                            first, final = k == 0 and x is XH and ww is WH, k == KC - 1 and ww is WL
                            if form == "T":
                                t0, cw = CHUNKS[c]
                                m_ = XW if u == UIX else P
                                last = pe.matmul(ps(n % PJ, cw, m_), ww[:, sl, k, i * P:i * P + m_], x[:, k, t0:t0 + cw],
                                                 start=first, stop=final)
                            else:
                                last = pe.matmul(ps(n % PJ, w, rows(i)), x[:, k, row0(i):row0(i) + rows(i)],
                                                 ww[:, sl, k, 0:w], start=first, stop=final)
                    last.then_inc(s["job_pe"], 1)
                    for event in EVENTS.get(n, ()):
                        chunk(*event)

            for i in range(NT + 1):
                transpose_x(i)
            pe.wait_ge(s["init_act"], 1)
            for u in range(UIX + 1):
                unit(u)
            pe.wait_ge(s["job_act"], JOB0[UIX + 1])
            for g, (lo, hi) in enumerate(((0, 5), (5, NT + 1))):
                for i in range(lo, hi):
                    last = pe.transpose(ps(6 + g, XW, rows(i), o=(i - lo) * XW), IXT[0:XW, row0(i):row0(i) + rows(i)],
                                        IDN[0:XW, 0:XW])
                last.then_inc(s["ik_t"], 1)
            pe.wait_ge(s["ik_l"], 3)
            pe.wait_ge(s["ik_rows"], 3)
            pe.matmul(ps(7, IH, BR), E8[0:8, :], IW[0:8, NT, :], start=True, stop=True).then_inc(s["iw_pe"], 1)

            def sample_products(bp):
                sl = bp % 2
                pe.wait_ge(s[f"ikc_in{sl}"], 256 * (bp // 2 + 1))
                for c in range(2):
                    pe.matmul(ps(4 + c, 512, BR), IQP[:, bp, :], IKT[:, sl, c * 512:(c + 1) * 512], start=bp == 0, stop=bp == 3)
                pe.matmul(ps(6, 1, BR), IQP[:, bp, :], IKNEW[:, bp:bp + 1], start=bp == 0, stop=bp == 3)\
                    .then_inc(s["samp_pe"], 1)

            pe.wait_ge(s["ik_h"], 1)
            for bp in (0, 1):
                sample_products(bp)
            for m in range(IH * 6):
                t, h = m // IH + 2, m % IH
                ge(pe, s["sc_relu"], m - 1)
                for c0 in range(0, P * (t + 1), 512):
                    w = min(512, P * (t + 1) - c0)
                    for kk, stack in enumerate((IA, IB)):
                        last = pe.matmul(ps(2 * (m % 2) + c0 // 512, w), IQS[:, h, (t - 2) * P:(t - 1) * P],
                                         stack[:, c0:c0 + w], start=kk == 0, stop=kk == 1)
                last.then_inc(s["sc_pe"], 1)
            pe.wait_ge(s["sc_relu"], IH * 6)
            for bp in (2, 3):
                sample_products(bp)
            pe.wait_ge(s["samp_relu"], 1)
            pe.wait_ge(s["iw_sel"], 1)
            for c, w in ((0, 512), (1, 512), (2, 1)):
                last = pe.matmul(ps(c, w, SB), WSEL[0:BR, :], RSM[0:BR, c * 512:c * 512 + w], start=True, stop=True)
            last.then_inc(s["samp_w"], 1)
            pe.wait_ge(s["samp_sc"], 1)
            for u in range(UIX + 1, NU):
                unit(u)
            pe_tail(pe, unit)


_OUTS = [(1, T, D), (SB, 1, D), (1, 1, T, KVH, HD), (1, 1, T, KVH, HD), (1, 1, T, HD), (1, 1, HH, HD, HD),
         (1, SB, 1, KVH, HD), (1, SB, 1, KVH, HD), (1, SB, 1, HD), (1, SB, HH, HD, HD)]


def _columns():
    q, k, v, ga, iq, ix, hq, hf, hi, gh = 0, 512, 768, 1024, 1536, 2048, 2120, 2632, 3144, 3656
    part = {"iq": iq, "hv": hi, "q": q, "k": k, "v": v, "gh": gh, "ga": ga}
    out = []
    for kind, a in UNITS:
        if kind == "ix":
            out.append([(ix + IH, HD), (ix, IH)])
        elif kind == "hg":
            out.append([(hf + a * P, P), (hq + a * P, P)])
        else:
            out.append([(part[kind] + a * UW, UW)])
    return out


def _bucket(n):
    n = max(n, 0)
    if n < 16:
        return n
    large = 16 + int(np.float32(np.log(np.float32(n) / np.float32(16)) / np.float32(np.log(128 / 16))) * np.float32(16))
    return min(large, 31)


def _constants():
    oh = np.zeros((32, UL), np.float32)
    for m in range(UL):
        oh[_bucket(255 - m), m] += 1
        oh[31, m] -= 1
    bits = np.tile((2.0 ** np.arange(ROUNDS - 1, -1, -1)).astype(np.float32), (P, 1))
    e8 = np.zeros((2, 8, BR), np.float32)
    for b in range(SB):
        for h in range(AH):
            e8[0, b, b * AH + h] = 1
            e8[1, h, b * AH + h] = 1
    masks = np.zeros((P, 656), np.float32)
    sidx = np.arange(P)[:, None]
    masks[:, 0:256] = np.tile(sidx <= np.arange(P)[None], (1, 2))
    masks[:, 256:384] = (sidx // HD == np.arange(P)[None] // HD)
    for b in range(SB):
        for h in range(AH):
            masks[b * AH + h, 384 + h] = 1
            masks[b * AH + h, 392 + b] = 1
    masks[:, 400:528] = np.where(np.arange(P)[None] <= sidx, 0.0, NEG)
    masks[:, 528:656] = np.eye(P)[::-1]
    return {"c_ident": np.eye(P, dtype=np.float32), "c_oh": oh, "c_bits": bits, "c_e8": e8, "c_masks": masks}


def kernel(**inputs):
    import concourse.bacc as _bacc
    from concourse.bass_utils import run_bass_kernel_spmd as _run

    x = {k: np.asarray(v) for k, v in inputs.items()}
    w_in, w_out = x["w_in"][0], x["w_out"][0]

    def unit_layout(w):
        return w.reshape(2, 4, P, -1).transpose(0, 2, 1, 3)

    cols = _columns()
    parts = [np.concatenate([w_in[:, c:c + n] for c, n in cs], axis=1) for cs in cols]
    main = [unit_layout(w) for u, w in enumerate(parts) if u != UIX]
    main += [unit_layout(w_out[:, c * UW:(c + 1) * UW]) for c in range(NUO)]
    data = {
        "x_prompt": x["x_prompt"], "x_sample": x["x_sample"],
        "w_main": np.stack(main), "w_ix": unit_layout(parts[UIX]),
        "cache_kt": x["cache_k"][0].reshape(-1, P, 2, P).transpose(0, 3, 2, 1),
        "cache_v": x["cache_v"][0].reshape(-1, P, UW),
        "cache_ikt": x["cache_ik"][0].transpose(0, 2, 1),
        "state": x["state_hgrn"][0].reshape(SB, NG, 2, HD, HD).transpose(2, 3, 0, 1, 4),
        "pages": x["page_table"].reshape(1, -1),
        "rel": x["rel_bias"],
        "ln_g": x["ln_g"][0].reshape(KC, P).T,
        "q_g": np.broadcast_to(x["q_norm_g"][0], (P, HD)), "k_g": np.broadcast_to(x["k_norm_g"][0], (P, HD)),
        "hn_g": np.broadcast_to(x["hgrn_norm_g"][0], (P, HD)),
        "lbs": x["hgrn_lb"].reshape(2, NG, P).transpose(2, 0, 1),
        **_constants(),
    }
    nc = _bacc.Bacc("TRN2", target_bir_lowering=False, num_devices=1)
    arrays, args = {}, []
    for name, a in data.items():
        a = np.ascontiguousarray(a)
        arrays[f"in_{name}"] = a
        args.append(nc.dram_tensor(f"in_{name}", a.shape, mybir.dt.from_np(a.dtype), kind="ExternalInput").ap())
    for i, shape in enumerate(_OUTS):
        args.append(nc.dram_tensor(f"out_{i}", shape, F32, kind="ExternalOutput").ap())
    hymba_step(nc, *args)
    r = _run(nc, [arrays], core_ids=[0])
    return tuple(r.results[0][f"out_{i}"] for i in range(len(_OUTS)))
```

```python
import numpy as np
import concourse.bass as bass
from concourse import mybir
from contextlib import ExitStack

F32 = mybir.dt.float32
F32R = mybir.dt.float32r
BF16 = mybir.dt.bfloat16
F16 = mybir.dt.float16
I32 = mybir.dt.int32
ACT = mybir.ActivationFunctionType
ALU = mybir.AluOpType
AX = mybir.AxisListType

P = 128
D = 1024
KC = D // P
T = 1024
NT = T // P
SB = 8
TT = T + SB
PAST = 1024
NPG = PAST // P
NPOOL = 80
HD = 64
AH, KVH, IH, HH = 8, 4, 8, 8
NG = HH // 2
SUB = 32
NSUB = P // SUB
TOPK = 256
EPS = 1e-6
NEG = -1e30
UNSEEN = -3e38
UW = 256
NEAR = 2 * P
CONSTS_IN = 15 * 16
UL = 383
ROUNDS = 31
BR = SB * AH


def rows(i):
    return P if i < NT else SB


CHUNKS = [(0, 384), (384, 384), (768, 264)]
UNITS = [("iq", 0), ("iq", 1), ("ix", 0), ("hg", 0), ("hv", 0), ("hv", 1),
         ("hg", 1), ("gh", 0), ("k", 0), ("hg", 2), ("gh", 1), ("q", 0),
         ("hg", 3), ("ga", 0), ("q", 1), ("ga", 1), ("v", 0)]
NU = len(UNITS)
LATE = 6
NUO = D // UW
UIX = UNITS.index(("ix", 0))
XW = IH + HD
KEYS_AT = [4 + 3 * b for b in range(SB)]
LOGITS_AT = KEYS_AT[-1] + 1
VALUES_AT = [LOGITS_AT + 9 + int(3.5 * b) for b in range(SB)]
assert LOGITS_AT + 1 < NT * AH // 2 and VALUES_AT[-1] < NT * AH


def width(u):
    return XW if u == UIX else UW


def jobs(u):
    kind = UNITS[u][0] if u < NU else "out"
    if kind == "iq":
        return [("T", b, c) for c in range(3) for b in range(2)]
    if kind == "ix":
        return [("T", 0, c) for c in range(3)]
    if kind == "hg":
        return [("T", b, c) for b in range(2) for c in range(3)]
    return [("N", i, 0) for i in range(NT + 1)]


JOB0 = [0]
for _u in range(NU + NUO):
    JOB0.append(JOB0[-1] + len(jobs(_u)))
PJ = 4
STAGED = ("v", "gh", "ga", "q", "k")
HGU = [UNITS.index(("hg", j)) for j in range(NG)]
STG_UNITS = [u for u in range(NU) if UNITS[u][0] in STAGED]
CHUNK0 = [JOB0[u + 2] + 4 for u in HGU]
EVENTS = {}
for _lag, _kind in ((2, "out"), (0, "intra"), (1, "keys")):
    for _j in range(NG):
        for _c in range(NT):
            EVENTS.setdefault(CHUNK0[_j] + _c + _lag, []).append((_kind, _j, _c))

SC0 = {t: sum(P * (x + 1) for x in range(2, t)) for t in range(2, NT)}
SCW = sum(P * (x + 1) for x in range(2, NT))


def hymba_step(nc, x_prompt, x_sample, w_main, w_ix, cache_kt, cache_v, cache_ikt, state, pages,
               rel, ln_g, q_g, k_g, hn_g, lbs, c_ident, c_oh, c_bits, c_e8, c_masks,
               y_prompt, y_sample, k_prompt, v_prompt, ik_prompt, s_prompt,
               k_sample, v_sample, ik_sample, s_sample):
    with ExitStack() as ctx:
        cur = [16512]

        def at(name, shape, dt, off):
            return nc.alloc_sbuf_tensor_at(name, [P] + shape, dt, offset=off)

        def size(shape, dt):
            return int(np.prod(shape)) * {F32: 4, F32R: 4, I32: 4, BF16: 2, F16: 2}[dt]

        def sb(name, shape, dt=F32):
            off = cur[0]
            cur[0] += (size(shape, dt) + 31) // 32 * 32
            assert cur[0] <= 229344, (name, cur[0])
            return at(name, shape, dt, off)

        def over(start, *parts):
            out = []
            for name, shape, dt in parts:
                out.append(at(name, shape, dt, start))
                start += (size(shape, dt) + 31) // 32 * 32
            out.append(start)
            return out

        def sem(name):
            return ctx.enter_context(nc.semaphore(name))

        def ge(eng, s, v):
            if v > 0:
                eng.wait_ge(s, v)

        IDN = sb("ident", [P])
        ANR = sb("antidiagonal_r", [P], F32R)
        IDB = sb("ident_b", [P], BF16)
        QG = sb("q_gain", [HD])
        KG = sb("k_gain", [HD])
        HNG = sb("hgrn_gain", [HD])
        IW = sb("index_weight", [NT + 1, IH])
        STAT = sb("x_stats", [4, NT + 1])
        LBR = sb("lb_rows", [2, NG])
        LB = sb("lb", [NG])
        OML = sb("one_minus_lb", [NG])
        NOML = sb("lb_minus_one", [NG])
        TRI = sb("causal_add", [P], BF16)
        FS = sb("f_sample", [NG, SB])
        QSS = sb("q_sample", [NG, SB])
        KSS = sb("k_sample_h", [NG, SB])
        IKNEW = sb("ik_new", [4])
        BITF = sb("bit_value", [ROUNDS])
        BITI = sb("bit", [ROUNDS], I32)
        CNT = sb("count", [7])
        NEED = sb("need", [7])
        U = sb("bits_so_far", [7], I32)
        XM = sb("sign_flip", [7], I32)
        CAND = sb("candidate", [7], I32)
        HIT = sb("bit_kept", [7], I32)
        SQK = sb("qk_square_sums", [3, NT + 1, 12])
        SHO = sb("ho_square_sums", [3, NT, 8])
        DE = sb("chunk_decay", [2, NT])
        PT_ = sb("page_table", [SB * NPG], I32)
        E8 = sb("row_select", [BR])
        E8H = sb("head_select", [BR])
        HM = sb("head_mask", [2 * SB + 2])
        E8B = sb("row_select_b", [BR], BF16)
        IWC = sb("index_weight_col", [1])
        WSEL = sb("index_weight_sel", [SB])
        HMT = sb("head_mask_tmp", [SB])
        MX = sb("row_max", [8])
        NB = sb("neg_max", [8])
        RS = sb("row_sum", [2, 8])
        RI = sb("row_sum_inv", [8])
        MN = sb("ho_sample_stats", [3])
        SMS = sb("softmax_sample", [4])
        SN = sb("new_key_scores", [AH])
        UT = sb("bias_by_distance", [UL])

        XR0 = cur[0]
        XH = sb("xT_high", [KC, TT], F32R)
        XL = sb("xT_low", [KC, TT], F32R)
        QS, KA, KB, _ = over(XR0, ("qT_stack", [AH, T], F32R), ("kT_high_low", [KVH, T], F32R),
                             ("kT_low_high", [KVH, T], F32R))
        WR = sb("w_raw", [2, 4, UW])
        W0 = cur[0]
        KP0, _ = over(W0 - 8192, ("page_keys_0", [2, PAST], F32))
        VP0, _ = over(W0 - 8192, ("page_values_0", [NPG, UW], F32))
        WH = sb("w_high", [2, KC, UW], F32R)
        WL = sb("w_low", [2, KC, UW], F32R)
        BL, BH, VT, QR, KR, _e = over(W0, ("bias_low", [AH, NEAR], F32R), ("bias_high", [AH, NEAR], F32R),
                                      ("values_T", [NT, UW], F32), ("q_rows", [2, 512], F32),
                                      ("k_rows", [2, KVH, 2, HD], F32))
        assert _e <= cur[0]
        S0 = cur[0]
        SC = sb("scores", [SCW])
        SCS = sb("scores_sample", [PAST + 32])
        R0_ = cur[0]
        RB = sb("relu", [2, T])
        XB, _e = over(S0, ("x_rows", [6, D], F32))
        assert _e <= cur[0]
        MSK, = over(S0, ("mask", [SCW], BF16))[:1]
        KP1, _e = over(S0 + SCW * 2, ("page_keys_1", [2, PAST], F32))
        assert _e <= S0 + SCW * 4
        VP1, _ = over(S0 + SCW * 2, ("page_values_1", [NPG, UW], F32))
        MSKS, PTP, _e = over(S0 + SCW * 4, ("mask_sample", [PAST + 16], BF16), ("prob_T", [NPG, BR], F32))
        assert _e <= R0_, (_e, R0_)
        LNG, _e = over(S0 + 6 * D * 4, ("ln_gain", [D], F32))
        assert _e <= R0_ + 8192
        FB, QB, _ = over(R0_, ("decay_log", [T], F32), ("hq", [T], F32))
        PTS, _ = over(R0_, ("pT", [2, NT, P], F32))
        PSM, _ = over(cur[0], ("prob_sample", [PAST + 4], F32))
        JK = sb("flag", [PAST + 8], F16)
        CU = sb("flag_count", [PAST + 8], F16)
        I0 = cur[0]
        IQS = sb("iqT_stack", [IH, T - 2 * P], F32R)
        IA = sb("ikT_high_low", [T], F32R)
        IB = sb("ikT_low_high", [T], F32R)
        XB2, _ = over(I0 + IH // 2 * (T - 2 * P) * 4, ("x_rows_2", [3, D], F32))

        def x_buf(i):
            return XB[:, i, :] if i < 6 else XB2[:, i - 6, :]

        HV, HK, QI, ATB, HO, _e = over(I0, ("hv", [NT + 1, 512], F32), ("hk", [T], F32), ("q_decayed", [T], F32),
                               ("intra", [2, 2, P], F32), ("ho_rows", [NT, P], F32))
        QD, _ = over(_e - NT * P * 4, ("q_decayed_ref", [T], F32))
        assert _e <= cur[0], (_e, cur[0])
        AO, PB, SQ, _e = over(I0, ("attn_out", [NT + 1, 512], F32), ("prob", [3, T], F32), ("square", [512], F32))
        QPD, _ = over(I0 + 4 * 2048, ("q_padded", [2, SB, BR], F32))
        assert _e <= cur[0]
        TRF, ANT, _ = over(cur[0], ("causal_add_f", [P], F32), ("antidiagonal", [P], F32))
        VN, PN, DG, _e = over(cur[0], ("v_new", [UW], F32), ("prob_new", [BR], F32), ("diag", [BR], F32))
        STG = sb("stage", [4, UW])
        H0 = cur[0]
        QT = sb("q_ref", [2, T])
        KT = sb("k_ref", [NT * SUB * 10])
        KTN = sb("k_rows_h", [2, P])
        INM = sb("intra_mask", [2, P])
        BM = sb("pair_mask", [P])
        ST_OFF = cur[0]
        ST = sb("hgrn_state", [NG, P])
        TMP = sb("state_add", [2, P])
        RM = sb("scan_keep", [T], BF16)
        IXT, IKN, _e = over(H0, ("ix_T", [TT], F32), ("ik_rows", [NT + 1, HD], F32))
        JA, _ = over(H0, ("square_junk", [D], F32))
        IK0 = _e
        IKT, IQP, _e = over(IK0, ("index_keys_T", [2, PAST], F32), ("iq_padded", [4, BR], F32))
        assert _e <= H0 + 8192 + 10240
        RSM, _e = over(H0, ("relu_sample", [PAST + 1], F32))
        BRAW, _e = over(R0_, ("bias_raw", [AH, NEAR], F32))

        S0T, VBT, QHP, _e = over(H0, ("state_in", [SB, NG, HD], F32), ("v_spread", [SB, NG, HD], F32),
                                 ("hq_padded", [SB * NG, BR], F32))
        OSM, _ = over(H0 + 8192, ("out_by_head", [SB, UW], F32))
        HOSM, _e = over(_e, ("ho_sample", [HD], F32))
        assert _e <= cur[0], (_e, cur[0])
        MIX, _ = over(S0, ("mix", [2, D], F32))
        HOR, HGR, _ = over(H0, ("ho_in", [2, 512], F32), ("hgate_in", [2, 512], F32))
        AGR, XRS, YST, _ = over(H0 + 16384, ("agate_in", [2, 512], F32), ("x_res", [2, UW], F32),
                                ("y_rows", [2, UW], F32))

        PSA = ctx.enter_context(nc.psum_tensor("psum", [P, 8 * 512], F32))

        def ps(bank, n=512, r=P, r0=0, o=0):
            return PSA[r0:r, bank * 512 + o:bank * 512 + o + n]

        d_q = nc.dram_tensor("q_spill", [TT, 512], F32).ap()
        d_k = nc.dram_tensor("k_spill", [TT, UW], F32).ap()
        d_ho = nc.dram_tensor("ho_spill", [TT, 512], F32).ap()
        d_gh = nc.dram_tensor("hgate_spill", [TT, 512], F32).ap()
        d_ga = nc.dram_tensor("agate_spill", [TT, 512], F32).ap()
        d_hv = nc.dram_tensor("hv_spill", [SB, 512], F32)
        d_ut = nc.dram_tensor("bias_spill", [AH, UL], F32)
        d_ao = nc.dram_tensor("attn_sample_spill", [SB, 512], F32).ap()

        class Sems(dict):
            def __missing__(self, name):
                self[name] = sem(name)
                return self[name]

        s = Sems()

        block = ctx.enter_context(nc.Block())

        def bc(ap, n):
            return bass.AP(ap.tensor, ap.offset, list(ap.ap) + [[0, n]])

        def rep(ap, n):
            return bass.AP(ap.tensor, ap.offset, [ap.ap[0], [0, n]] + list(ap.ap[1:]))

        def f(ap):
            return ap.bitcast(F32)

        def x_rows(i):
            return x_prompt[0, i * P:(i + 1) * P, :] if i < NT else x_sample[:, 0, :]


        OH, REL, _ = over(ST_OFF, ("bucket_of_distance", [UL], F32), ("rel_bias", [AH], F32))

        def row0(i):
            return min(i, NT) * P

        ALLS = [sum(1 for g in range((NT + 1) * len(STG_UNITS)) if g % 4 == x) * 16 for x in range(4)]
        QOUT = [sum(1 for g in range((NT + 1) * (STG_UNITS.index(UNITS.index(("q", 1))) + 1)) if g % 4 == x) * 16
                for x in range(4)]
        NA = NT * AH
        BUILD = {0: [0, 1], **{2 * (n - 1): [n] for n in range(2, 2 * NT)}}

        SIDE = {1: [("new_key", 0)], LOGITS_AT: [("logits", 0)], LOGITS_AT + 4: [("probs_T", 0)],
                LOGITS_AT + 6: [("prob_new", 0)], LOGITS_AT + 8: [("hgrn", 0)]}
        for b in range(SB):
            SIDE.setdefault(KEYS_AT[b], []).append(("keys", b))
            SIDE.setdefault(VALUES_AT[b], []).append(("values", b))
        KP, VP = (KP0, KP1), (VP0, VP1)

        def place(i):
            return 0 if i == NT else i + 1

        def inverse_root(eng, link, out, x, tmp, done=None):
            link(eng.tensor_scalar(out.bitcast(I32), x.bitcast(I32), -0.5, 1597463007.0, ALU.mult, ALU.add))
            for n in range(3):
                link(eng.tensor_tensor(tmp, out, out, ALU.mult))
                link(eng.tensor_tensor(tmp, tmp, x, ALU.mult))
                link(eng.tensor_scalar(tmp, tmp, -0.5, 1.5, ALU.mult, ALU.add))
                last = eng.tensor_tensor(out, out, tmp, ALU.mult)
                if n < 2 or done is None:
                    link(last)
                else:
                    last.then_inc(done, 1)

        def load_weights(sp, u):
            w = width(u)
            for h in range(2):
                n = 2 * u + h
                ge(sp, s["weights_low_ready"], n - 1)
                src = w_ix[h] if u == UIX else w_main[u if u < UIX else u - 1, h]
                sp.dma_start(WR[:, h, :, 0:w], src).then_inc(s[f"weights_in{h}"], 16)


        def split_w(gp, u):
            w = width(u)
            for h in range(2):
                gp.wait_ge(s["weights_high_ready"], 2 * u + h + 1)
                gp.tensor_tensor(WL[:, u % 2, 4 * h:4 * h + 4, 0:w], WR[:, h, :, 0:w],
                                 f(WH[:, u % 2, 4 * h:4 * h + 4, 0:w]), ALU.subtract)\
                    .then_inc(s["weights_low_ready"], 1)


        def load_rows(sp, i):
            p, r = place(i), rows(i)
            sl = p % 2
            if p < 2:
                for x in range(4):
                    sp.wait_ge(s[f"rows_out{x}"], QOUT[x])
                sp.wait_ge(s["job_done"], JOB0[NU - 1])
            elif p == 2:
                sp.wait_ge(s["sample_q_transposed"], 1)
                sp.wait_ge(s["new_key_products_ready"], 1)
            else:
                sp.wait_ge(s["attn_rows_transposed"], 2 * (p - 2))
            ge(sp, s[f"k_out{sl}"], 16 * (p // 2))
            for x in range(2):
                sp.dma_start(KR[0:r, sl, :, x, :], d_k[row0(i):row0(i) + r, :].rearrange("t (h d) -> t h d", d=HD))\
                    .then_inc(s[f"qk_rows_in{sl}"], 16)
            sp.dma_start(QR[0:r, sl, :], d_q[row0(i):row0(i) + r, :]).then_inc(s[f"qk_rows_in{sl}"], 16)

        def load_states(sp):
            sp.dma_start(S0T[:, :, :, :], state.rearrange("a k b j v -> (a k) b j v")).then_inc(s["states_in"], 16)
            sp.wait_ge(s["hv_out"], 32)
            for hh in range(2):
                sp.dma_start(VBT[hh * HD:(hh + 1) * HD, :, :, :].rearrange("p b j v -> p (b j) v"),
                             bass.AP(d_hv, hh * HD, [[0, HD], [P, SB * NG], [1, HD]])).then_inc(s["states_in"], 16)

        def sp_tail(sp):
            def store_keys(i):
                sp.wait_ge(s["qk_normed"], place(i) + 1)
                sp.dma_start(k_prompt[0, 0, i * P:(i + 1) * P] if i < NT else k_sample[0, :, 0],
                             KR[0:rows(i), place(i) % 2, :, 0, :]).then_inc(s[f"k_out{place(i) % 2}"], 16)

            def load_pages(b, values):
                n = SB * values + b
                if n >= 2:
                    ge(sp, s["sample_keys_done"], min(n - 1, SB))
                    ge(sp, s["sample_values_done"], n - 1 - SB)
                elif n == 1:
                    sp.wait_ge(s["masks_ready"], 7)
                pages_ = [sp.value_load(PT_[0:1, b * NPG + g:b * NPG + g + 1], min_val=0, max_val=NPOOL - 1)
                          for g in range(NPG)]
                for g, page in enumerate(pages_):
                    if values:
                        sp.dma_start(VP[b % 2][:, g, :], cache_v[bass.ds(page, 1)].rearrange("a k n -> (a k) n"))\
                            .then_inc(s[f"pages_in{b % 2}"], 16)
                    else:
                        sp.dma_start(KP[b % 2][:, :, g * P:(g + 1) * P],
                                     cache_kt[bass.ds(page, 1)].rearrange("a d j k -> (a d) j k"))\
                            .then_inc(s[f"pages_in{b % 2}"], 16)

            store_keys(NT)
            load_rows(sp, 1)
            for x in range(4):
                sp.wait_ge(s[f"rows_out{x}"], ALLS[x])
            sp.wait_ge(s["job_done"], JOB0[NU])
            sp.dma_start(VT[:, :, :], v_prompt[0, 0].rearrange("(t p) h d -> p t (h d)", p=P)).then_inc(s["values_in"], 16)
            sp.dma_start(VN[0:SB, :], v_sample[:, :, 0].rearrange("a b h d -> (a b) (h d)")).then_inc(s["new_values_in"], 16)
            load_pages(0, 0)
            store_keys(0)
            load_rows(sp, 2)
            load_pages(1, 0)
            for i, b in ((3, 2), (4, 3), (5, 4), (6, 5), (None, 6), (7, 7)):
                if i is not None:
                    store_keys(i - 2)
                    load_rows(sp, i)
                load_pages(b, 0)
            store_keys(NT - 2)
            store_keys(NT - 1)
            sp.wait_ge(s["sample_state_ready"], 1)
            for hh in range(2):
                sp.dma_start(s_sample[0].rearrange("b (j a) k v -> a k (b j) v", a=2)[hh],
                             S0T[hh * HD:(hh + 1) * HD, :, :, :].rearrange("p b j v -> p (b j) v")).then_inc(s["sample_state_out"], 16)
            for b in range(SB):
                load_pages(b, 1)
            def load_mix(i):
                ge(sp, s["mix_hgrn_ready"], i - 1)
                ge(sp, s["mix_attn_ready"], i - 1)
                for dst, src in ((HOR, d_ho), (HGR, d_gh), (AGR, d_ga)):
                    sp.dma_start(dst[0:rows(i), i % 2, :], src[row0(i):row0(i) + rows(i), :])\
                        .then_inc(s[f"mix_in{i % 2}"], 16)

            NY = NUO * (NT + 1)

            def y_part(n, a, b):
                u, i = n // (NT + 1), n % (NT + 1)
                c = slice(u * UW, (u + 1) * UW)
                return a[0, i * P:(i + 1) * P, c] if i < NT else b[:, 0, c]

            def load_res(n):
                ge(sp, s["y_ready"], n - 1)
                sp.dma_start(XRS[0:rows(n % (NT + 1)), n % 2, :], y_part(n, x_prompt, x_sample))\
                    .then_inc(s[f"residual_in{n % 2}"], 16)

            sp.wait_ge(s["sample_hgrn_ready"], 1)
            sp.wait_ge(s["sample_state_out"], 32)
            sp.wait_ge(s["ho_out"], 16 * NG)
            load_mix(0)
            load_mix(1)
            load_res(0)
            load_res(1)
            sp.wait_ge(s["sample_values_done"], SB - 1)
            load_weights(sp, NU)
            sp.wait_ge(s["sample_out_copied"], SB)
            for kv in range(KVH):
                sp.dma_start(d_ao.rearrange("b (k g d) -> k g b d", g=2, d=HD)[kv],
                             OSM[2 * kv:2 * kv + 2, :, kv * HD:(kv + 1) * HD]).then_inc(s["sample_attn_out"], 16)
            sp.wait_ge(s["sample_hgrn_normed"], 1)
            sp.dma_start(d_ho[T:TT, :].rearrange("b (h v) -> (b h) v", v=HD), HOSM[0:BR, :]).then_inc(s["ho_out"], 16)
            sp.wait_ge(s["sample_attn_out"], 16 * KVH)
            sp.dma_start(AO[0:SB, NT, :], d_ao).then_inc(s["sample_attn_in"], 16)
            load_mix(2)
            load_weights(sp, NU + 1)
            sp.wait_ge(s["ho_out"], 16 * (NG + 1))

            def store_y(n):
                if n % (NT + 1) == 4 and n // (NT + 1) + 2 < NUO:
                    load_weights(sp, NU + n // (NT + 1) + 2)
                sp.wait_ge(s["y_ready"], n + 1)
                sp.dma_start(y_part(n, y_prompt, y_sample), YST[0:rows(n % (NT + 1)), n % 2, :])\
                    .then_inc(s[f"y_out{n % 2}"], 16)
                if n + 2 < NY:
                    load_res(n + 2)

            for i in range(3, NT + 1):
                load_mix(i)
                if i >= 3:
                    store_y(i - 3)
            for n in range(NT - 2, NY):
                store_y(n)
            sp.wait_ge(s["k_out0"], 16 * 5)
            sp.wait_ge(s["k_out1"], 16 * 4)
            sp.wait_ge(s["y_out0"], NY * 8)
            sp.wait_ge(s["y_out1"], NY * 8)
            sp.wait_ge(s["sample_state_out"], 32)

        def gp_tail(gp, link):
            def roots(t):
                x, out, tmp = (t[:, k, :, :].rearrange("p i h -> p (i h)") for k in (0, 1, 2))
                link(gp.tensor_scalar(x, x, 1.0 / HD, EPS, ALU.mult, ALU.add))
                inverse_root(gp, link, out, x, tmp)

            def norm(i):
                r, sl = rows(i), place(i) % 2
                gp.wait_ge(s[f"qk_rows_in{sl}"], 48 * (place(i) // 2 + 1))
                q = QR[0:r, sl, :].rearrange("p (h d) -> p h d", d=HD)
                k = KR[0:r, sl, :, :, :].rearrange("p h x d -> p h (x d)")
                link(gp.tensor_tensor(q, q, bc(SQK[0:r, 1, i, 0:AH], HD), ALU.mult))
                link(gp.tensor_tensor(q, q, rep(QG[0:r, :], AH), ALU.mult))
                link(gp.tensor_tensor(k, k, bc(SQK[0:r, 1, i, AH:12], 2 * HD), ALU.mult))
                k = KR[0:r, sl, :, :, :].rearrange("p h x d -> p (h x) d")
                gp.tensor_tensor(k, k, rep(KG[0:r, :], 2 * KVH), ALU.mult).then_inc(s["qk_normed"], 1)

            def sample_state():
                gp.wait_ge(s["states_in"], 48)

                def spread(x):
                    return bass.AP(x, 0, [[NG * SB, P], [1, SB], [SB, NG], [0, HD]])

                link(gp.tensor_tensor(S0T[:, :, :, :], S0T[:, :, :, :], spread(FS), ALU.mult))
                link(gp.tensor_tensor(VBT[:, :, :, :], VBT[:, :, :, :], spread(KSS), ALU.mult))
                gp.tensor_tensor(S0T[:, :, :, :], S0T[:, :, :, :], VBT[:, :, :, :], ALU.add).then_inc(s["sample_state_ready"], 1)
                link(gp.memset(QHP[:, :, :], 0.0))
                w = SB * NG * BR
                for hh in range(2):
                    ins = gp.tensor_scalar(bass.AP(QHP, hh * HD * w + hh, [[w, HD], [NG * BR + 8, SB], [BR + 2, NG]]),
                                           bass.AP(QSS, hh * HD * NG * SB, [[NG * SB, HD], [1, SB], [SB, NG]]),
                                           HD ** -0.5, 0.0, ALU.mult, ALU.add)
                    ins.then_inc(s["sample_hq_padded"], 1)
                    gp.wait_ge(s["sample_hq_padded"], hh + 1)

            gp.wait_ge(s["job_copied"], JOB0[UNITS.index(("q", 1)) + 1])
            roots(SQK)
            norm(NT)
            gp.wait_ge(s["chunk_output_ready"], NT * NG)
            gp.memset(QPD[:, :, :, :], 0.0).then_inc(s["sample_q_cleared"], 1)
            norm(0)
            norm(1)
            for i in range(2, NT):
                norm(i)
            sample_state()
            gp.wait_ge(s["chunk_output_copied"], NT * NG)
            roots(SHO)
            def gain(i):
                r, sl = rows(i), i % 2
                gp.wait_ge(s[f"mix_in{i % 2}"], 48 * (i // 2 + 1))
                hg = HGR[0:r, i % 2, :].rearrange("p (h d) -> p h d", d=HD)
                gp.tensor_tensor(hg, hg, rep(HNG[0:r, :], HH), ALU.mult).then_inc(s["gate_ready"], 1)

            gp.wait_ge(s["sample_hgrn_copied"], 1)
            link(gp.tensor_scalar(MN[0:BR, 0:1], MN[0:BR, 0:1], 1.0 / HD, EPS, ALU.mult, ALU.add))
            inverse_root(gp, link, MN[0:BR, 1:2], MN[0:BR, 0:1], MN[0:BR, 2:3])
            gp.tensor_scalar(HOSM[0:BR, :], HOSM[0:BR, :], MN[0:BR, 1:2], 0.0, ALU.mult, ALU.add).then_inc(s["sample_hgrn_normed"], 1)
            def gated(i):
                r, sl = rows(i), i % 2
                ge(gp, s["mix_transposed"], 2 * (i - 1))
                if i == NT:
                    gp.wait_ge(s["sample_attn_in"], 16)
                else:
                    gp.wait_ge(s["attn_out_ready"], i + 1)
                gp.tensor_tensor(MIX[0:r, sl, 0:512], AO[0:r, i, :], AGR[0:r, sl, :], ALU.mult).then_inc(s["mix_attn_ready"], 1)

            gain(0)
            gain(1)
            gp.wait_ge(s["attn_values_done"], NA)
            gated(0)
            split_w(gp, NU)
            gated(1)
            for i in range(2, NT + 1):
                gain(i)
                gated(i)
                if i == 3:
                    split_w(gp, NU + 1)
            split_w(gp, NU + 2)
            split_w(gp, NU + 3)

        def act_tail(act, link, high_w):
            act.wait_ge(s["job_done"], JOB0[NU - 1])
            act.wait_ge(s["bias_in"], 16)
            act.activation(BH[:, :, :], BRAW[:, :, :], ACT.Copy).then_inc(s["bias_high_ready"], 1)

            def build(n):
                i = n // 2
                c = slice(i * P, (i + 1) * P)
                lo, hi = ps(5, 512, HD).rearrange("p (j t) -> p j t", t=P), ps(5, 512, P, HD).rearrange("p (j t) -> p j t", t=P)
                act.wait_ge(s["attn_rows_transposed"], n + 1)
                if n % 2 == 0:
                    act.activation(KA[0:HD, :, c], lo, ACT.Copy)
                    act.activation(KB[HD:P, :, c], hi, ACT.Copy).then_inc(s["attn_high_ready"], 1)
                else:
                    act.activation(QS[0:HD, 0:AH:2, c], lo, ACT.Copy)
                    act.activation(QS[HD:P, 1:AH:2, c], hi, ACT.Copy).then_inc(s["attn_high_ready"], 1)

            def sample(kind, b):
                if kind == "queries":
                    act.wait_ge(s["sample_q_transposed"], 1)
                    act.wait_ge(s["sample_q_cleared"], 1)
                    qpd = QPD[:, :, :, :].rearrange("p a b n -> p (a b n)")
                    for blk in range(2):
                        for kv2 in range(2):
                            for g in range(2):
                                o = 512 * blk + 4 * blk + 2 * kv2 + g
                                last = act.activation(qpd[kv2 * HD:(kv2 + 1) * HD, o:512 * (blk + 1):BR + 8],
                                                      ps(6, SB, (g + 1) * HD, g * HD, 8 * (2 * blk + kv2)), ACT.Copy)
                    last.then_inc(s["sample_q_ready"], 1)
                elif kind == "hgrn":
                    act.wait_ge(s["sample_hgrn_ready"], 1)
                    act.activation(ps(6, HD, BR, o=320), ps(6, HD, BR, o=256), ACT.Square, accum_out=MN[0:BR, 0:1])
                    act.activation(HOSM[0:BR, :], ps(6, HD, BR, o=256), ACT.Copy).then_inc(s["sample_hgrn_copied"], 1)
                elif kind == "values":
                    act.wait_ge(s["sample_values_done"], b + 1)
                    act.activation(OSM[0:SB, b, :], ps(6, UW, SB, o=b % 2 * UW), ACT.Copy).then_inc(s["sample_out_copied"], 1)
                elif kind == "logits":
                    act.wait_ge(s["sample_max_ready"], 1)
                    act.activation(PSM[0:BR, 0:PAST + 1], PSM[0:BR, 0:PAST + 1], ACT.Exp, scale=HD ** -0.5,
                                   bias=SMS[0:BR, 1:2], accum_out=SMS[0:BR, 2:3]).then_inc(s["sample_exp_ready"], 1)

            for m in range(NA + 1):
                for n in BUILD.get(m, []):
                    build(n)
                if m == 0:
                    sample("queries", 0)
                if m < NA:
                    t, h = m // AH, m % AH
                    w = P * (t + 1)
                    act.wait_ge(s["max_ready"], m + 1)
                    ge(act, s["probs_transposed"], m - 2)
                    act.activation(PB[:, m % 3, 0:w], ps(2 * (m % 2), w), ACT.Exp, scale=HD ** -0.5, bias=NB[:, h:h + 1],
                                   accum_out=RS[:, t % 2, h:h + 1]).then_inc(s["probs_ready"], 1)
                m1 = m - 1
                if m1 >= 0 and m1 % 2 == 0:
                    w = P * (m1 // AH + 1)
                    act.wait_ge(s["probs_transposed"], m1 + 1)
                    ge(act, s["attn_values_done"], m1 - 1)
                    act.activation(PTS[:, m1 % 2, :, :].rearrange("p b t -> p (b t)")[:, 0:w], ps(4, w), ACT.Copy)\
                        .then_inc(s["probs_T_act_ready"], 1)
                for side in SIDE.get(m1, ()):
                    sample(*side)
            act.wait_ge(s["scores_ready"], NA)
            high_w(NU)

            def mix_high(i):
                for h in range(2):
                    n = 2 * i + h
                    act.wait_ge(s["mix_transposed"], n + 1)
                    src = ps(6 + n % 2).rearrange("p (k t) -> p k t", t=P)[:, :, 0:rows(i)]
                    act.activation(XH[:, 4 * h:4 * h + 4, row0(i):row0(i) + rows(i)], src, ACT.Copy)\
                        .then_inc(s["mix_high_ready"], 1)

            for i in range(3):
                mix_high(i)
            high_w(NU + 1)
            for i in range(3, NT + 1):
                mix_high(i)
            high_w(NU + 2)
            high_w(NU + 3)

        def dve_tail(dve, link):
            def build(n):
                i = n // 2
                c = slice(i * P, (i + 1) * P)
                lo, hi = ps(5, 512, HD).rearrange("p (j t) -> p j t", t=P), ps(5, 512, P, HD).rearrange("p (j t) -> p j t", t=P)
                dve.wait_ge(s["attn_high_ready"], n + 1)
                if n % 2 == 0:
                    dve.tensor_tensor(KB[0:HD, :, c], lo, f(KA[0:HD, :, c]), ALU.subtract)
                    dve.tensor_tensor(KA[HD:P, :, c], hi, f(KB[HD:P, :, c]), ALU.subtract).then_inc(s["attn_low_ready"], 1)
                else:
                    dve.tensor_tensor(QS[HD:P, 0:AH:2, c], lo, f(QS[0:HD, 0:AH:2, c]), ALU.subtract)
                    dve.tensor_tensor(QS[0:HD, 1:AH:2, c], hi, f(QS[HD:P, 1:AH:2, c]), ALU.subtract)\
                        .then_inc(s["attn_low_ready"], 1)

            def sample(kind, b):
                if kind == "queries":
                    dve.wait_ge(s["qk_normed"], 1)
                    q = QR[0:SB, 0, :].rearrange("p (n g d) -> p n g d", g=2, d=HD)
                    k = KR[0:SB, 0, :, :, :]
                    link(dve.tensor_tensor(SQ[0:SB, :].rearrange("p (n g d) -> p n g d", g=2, d=HD), q, k, ALU.mult))
                    dve.reduce_sum(SN[0:SB, :], SQ[0:SB, :].rearrange("p (h d) -> p h d", d=HD), axis=AX.X)\
                        .then_inc(s["new_key_products_ready"], 1)
                elif kind == "new_key":
                    dve.wait_ge(s["new_key_spread"], 1)
                    link(dve.tensor_tensor(HMT[0:BR, :], ps(6, AH, BR), HM[0:BR, 0:8], ALU.mult))
                    link(dve.reduce_sum(IWC[0:BR, :], HMT[0:BR, :], axis=AX.X))
                    dve.tensor_tensor(SMS[0:BR, 3:4], IWC[0:BR, :], ps(6, 1, BR, o=8), ALU.add).then_inc(s["new_key_score_ready"], 1)
                elif kind == "logits":
                    dve.wait_ge(s["sample_logits_ready"], 1)
                    for c in range(2):
                        link(dve.tensor_copy(PSM[0:BR, c * 512:(c + 1) * 512], ps(1 + 2 * c, 512, BR)))
                    dve.wait_ge(s["new_key_score_ready"], 1)
                    link(dve.tensor_copy(PSM[0:BR, PAST:PAST + 1], SMS[0:BR, 3:4]))
                    link(dve.reduce_max(SMS[0:BR, 0:1], PSM[0:BR, 0:PAST + 1], axis=AX.X))
                    dve.tensor_scalar(SMS[0:BR, 1:2], SMS[0:BR, 0:1], -HD ** -0.5, None, ALU.mult)\
                        .then_inc(s["sample_max_ready"], 1)
                elif kind == "probs_T":
                    dve.wait_ge(s["sample_probs_transposed"], 1)
                    dve.tensor_copy(PTP[:, :, :].rearrange("p g n -> p (g n)"), ps(6)).then_inc(s["sample_probs_T_ready"], 1)
                    dve.tensor_scalar(DG[0:BR, :], IDN[0:BR, 0:BR], PSM[0:BR, PAST:PAST + 1], None, ALU.mult)\
                        .then_inc(s["new_prob_diag_ready"], 1)
                elif kind == "prob_new":
                    dve.wait_ge(s["new_prob_spread"], 1)
                    dve.tensor_copy(PN[0:SB, :], ps(6, BR, SB)).then_inc(s["new_prob_ready"], 1)

            sample("queries", 0)
            for m in range(NA + 3):
                if m - 3 == LOGITS_AT:
                    dve.wait_ge(s["sample_exp_ready"], 1)
                    link(dve.reciprocal(SMS[0:BR, 3:4], SMS[0:BR, 2:3]))
                    dve.tensor_scalar(PSM[0:BR, 0:PAST + 1], PSM[0:BR, 0:PAST + 1], SMS[0:BR, 3:4], None, ALU.mult)\
                        .then_inc(s["sample_probs_ready"], 1)
                for n in BUILD.get(m, []):
                    build(n)
                if m == 0:
                    dve.wait_ge(s["bias_high_ready"], 1)
                    dve.wait_ge(s["job_done"], JOB0[NU])
                    dve.tensor_tensor(BL[:, :, :], BRAW[:, :, :], f(BH[:, :, :]), ALU.subtract).then_inc(s["bias_low_ready"], 1)
                if m < NA:
                    t, h = m // AH, m % AH
                    dve.wait_ge(s["scores_ready"], m + 1)
                    link(dve.reduce_max(MX[:, h:h + 1], ps(2 * (m % 2), P * (t + 1)), axis=AX.X))
                    dve.tensor_scalar(NB[:, h:h + 1], MX[:, h:h + 1], -HD ** -0.5, None, ALU.mult).then_inc(s["max_ready"], 1)
                m1 = m - 1
                if 0 <= m1 < NA and m1 % 2 == 1:
                    w = P * (m1 // AH + 1)
                    dve.wait_ge(s["probs_transposed"], m1 + 1)
                    ge(dve, s["attn_values_done"], m1 - 1)
                    dve.tensor_copy(PTS[:, m1 % 2, :, :].rearrange("p b t -> p (b t)")[:, 0:w], ps(4, w))\
                        .then_inc(s["probs_T_dve_ready"], 1)
                for side in SIDE.get(m1, ()):
                    sample(*side)
                m2 = m - 3
                if m2 >= 0 and m2 % AH == AH - 1:
                    t = m2 // AH
                    dve.wait_ge(s["attn_values_done"], m2 + 1)
                    dve.wait_ge(s["probs_ready"], m2 + 1)
                    link(dve.reciprocal(RI[:, :], RS[:, t % 2, :]))
                    dve.tensor_tensor(AO[:, t, :].rearrange("p (h d) -> p h d", d=HD),
                                      ps(7).rearrange("p (h d) -> p h d", d=HD), bc(RI[:, :], HD), ALU.mult)\
                        .then_inc(s["attn_out_ready"], 1)
            def mix_rows(i):
                r, sl = rows(i), i % 2
                ge(dve, s["mix_transposed"], 2 * (i - 1))
                dve.wait_ge(s["gate_ready"], i + 1)
                if i < NT:
                    ho = HOR[0:r, sl, :].rearrange("p (h d) -> p h d", d=HD)
                    link(dve.tensor_tensor(ho, ho, bc(SHO[0:r, 1, i, :], HD), ALU.mult))
                dve.tensor_tensor(MIX[0:r, sl, 512:1024], HOR[0:r, sl, :], HGR[0:r, sl, :], ALU.mult)\
                    .then_inc(s["mix_hgrn_ready"], 1)

            def mix_low(i):
                for h in range(2):
                    n = 2 * i + h
                    dve.wait_ge(s["mix_high_ready"], n + 1)
                    src = ps(6 + n % 2).rearrange("p (k t) -> p k t", t=P)[:, :, 0:rows(i)]
                    c = slice(row0(i), row0(i) + rows(i))
                    dve.tensor_tensor(XL[:, 4 * h:4 * h + 4, c], src, f(XH[:, 4 * h:4 * h + 4, c]), ALU.subtract)\
                        .then_inc(s["mix_low_ready"], 1)

            def add_residual(n):
                r = rows(n % (NT + 1))
                dve.wait_ge(s["job_done"], JOB0[NU] + n + 1)
                dve.wait_ge(s[f"residual_in{n % 2}"], 16 * (n // 2 + 1))
                ge(dve, s[f"y_out{n % 2}"], 16 * (n // 2))
                dve.tensor_tensor(YST[0:r, n % 2, :], ps((JOB0[NU] + n) % PJ, UW, r), XRS[0:r, n % 2, :], ALU.add)\
                    .then_inc(s["y_ready"], 1)

            mix_rows(0)
            for i in range(NT + 1):
                if i < NT:
                        mix_rows(i + 1)
                mix_low(i)
                if i >= 1:
                    add_residual(i - 1)
            for n in range(NT, NUO * (NT + 1)):
                add_residual(n)

        def pe_tail(pe, unit):
            def build(n):
                i = n // 2
                sl = place(i) % 2
                pe.wait_ge(s["qk_normed"], place(i) + 1)
                ge(pe, s["attn_low_ready"], n)
                for j in range(4):
                    src = KR[:, sl, j, :, :].rearrange("p a d -> p (a d)") if n % 2 == 0 else QR[:, sl, j * P:(j + 1) * P]
                    last = pe.transpose(ps(5, P, o=j * P), src, IDN[:, :])
                last.then_inc(s["attn_rows_transposed"], 1)

            def scores(m):
                t, h = m // AH, m % AH
                w = P * (t + 1)
                for n in BUILD.get(m, []):
                    build(n)
                if m == NA // 2:
                    pe.wait_ge(s["sample_max_ready"], 1)
                if m == 0:
                    pe.wait_ge(s["bias_low_ready"], 1)
                if h == 0:
                    pe.wait_ge(s["attn_low_ready"], 2 * (t + 1))
                    if t >= 2:
                        pe.wait_ge(s["masks_ready"], t - 1)
                ge(pe, s["probs_ready"], m - 1)
                bank = 2 * (m % 2)
                q = QS[:, h, t * P:(t + 1) * P]
                for c0 in range(0, w, 512):
                    n = min(512, w - c0)
                    pe.matmul(ps(bank, n, o=c0), q, KA[:, h // 2, c0:c0 + n], start=True, stop=False)
                    k0, k1 = max(c0, (t - 1) * P), min(c0 + n, (t + 1) * P)
                    if k0 < k1:
                        for half in (BH, BL):
                            pe.matmul(ps(bank, k1 - k0, o=k0), ANR[:, :],
                                      half[:, h, k0 - (t - 1) * P:k1 - (t - 1) * P], start=False, stop=False)
                    if t >= 2:
                        pe.matmul(ps(bank, n, o=c0), IDB[:, :], MSK[:, SC0[t] + c0:SC0[t] + c0 + n],
                                  start=False, stop=False)
                    elif c0 <= t * P < c0 + n:
                        pe.matmul(ps(bank, P, o=t * P), IDB[:, :], TRI[:, :], start=False, stop=False)
                    last = pe.matmul(ps(bank, n, o=c0), q, KB[:, h // 2, c0:c0 + n], start=False, stop=True)
                last.then_inc(s["scores_ready"], 1)

            def evacuated(m):
                pe.wait_ge(s["probs_T_dve_ready" if m % 2 else "probs_T_act_ready"], m // 2 + 1)

            def transposes(m):
                pe.wait_ge(s["probs_ready"], m + 1)
                if m >= 1:
                    evacuated(m - 1)
                if m == NA // 2:
                    pe.wait_ge(s["attn_low_ready"], 2 * NT)
                for b in range(m // AH + 1):
                    last = pe.transpose(ps(4, P, o=b * P), PB[:, m % 3, b * P:(b + 1) * P], IDN[:, :])
                last.then_inc(s["probs_transposed"], 1)

            def values(m):
                t, h = m // AH, m % AH
                evacuated(m)
                if m == 0:
                    pe.wait_ge(s["values_in"], 16)
                if h == 0:
                    ge(pe, s["attn_out_ready"], t)
                for b in range(t + 1):
                    last = pe.matmul(ps(7, HD, o=h * HD), PTS[:, m % 2, b, :], VT[:, b, h // 2 * HD:(h // 2 + 1) * HD],
                                     start=b == 0, stop=b == t)
                last.then_inc(s["attn_values_done"], 1)

            def sample(kind, b):
                if kind == "queries":
                    pe.wait_ge(s["qk_normed"], 1)
                    for j in range(4):
                        last = pe.transpose(ps(6, SB, o=8 * j), QR[0:SB, 0, j * P:(j + 1) * P], IDN[0:SB, 0:SB])
                    last.then_inc(s["sample_q_transposed"], 1)
                elif kind == "new_key":
                    pe.wait_ge(s["new_key_products_ready"], 1)
                    pe.wait_ge(s["sample_q_ready"], 1)
                    pe.wait_ge(s["masks_ready"], 7)
                    pe.matmul(ps(6, AH, BR), E8[0:8, :], SN[0:SB, :], start=True, stop=True)
                    pe.matmul(ps(6, 1, BR, o=8), E8B[0:8, :], MSKS[0:8, PAST:PAST + 1], start=True, stop=False)
                    pe.matmul(ps(6, 1, BR, o=8), E8H[0:8, :], UT[0:8, 2 * P - 1:2 * P], start=False, stop=True)\
                        .then_inc(s["new_key_spread"], 1)
                elif kind == "keys":
                    if b == 0:
                        pe.wait_ge(s["new_key_score_ready"], 1)
                    pe.wait_ge(s[f"pages_in{b % 2}"], 128 * (b // 2 + 1))
                    for blk in range(2):
                        for c in range(2):
                            last = pe.matmul(ps(1 + 2 * c, 512, BR), QPD[:, blk, b, :],
                                             KP[b % 2][:, blk, c * 512:(c + 1) * 512],
                                             start=b == 0 and blk == 0, stop=False)
                    last.then_inc(s["sample_keys_done"], 1)
                elif kind == "logits":
                    pe.matmul(ps(3, P, BR, o=512 - P), E8H[0:8, :], UT[0:8, P - 1:2 * P - 1], start=False, stop=False)
                    for c in range(2):
                        last = pe.matmul(ps(1 + 2 * c, 512, BR), E8B[0:8, :], MSKS[0:8, c * 512:(c + 1) * 512],
                                         start=False, stop=True)
                    last.then_inc(s["sample_logits_ready"], 1)
                elif kind == "probs_T":
                    pe.wait_ge(s["sample_probs_ready"], 1)
                    for g in range(NPG):
                        last = pe.transpose(ps(6, BR, o=g * BR), PSM[0:BR, g * P:(g + 1) * P], IDN[0:BR, 0:BR])
                    last.then_inc(s["sample_probs_transposed"], 1)
                elif kind == "prob_new":
                    pe.wait_ge(s["sample_probs_T_ready"], 1)
                    pe.wait_ge(s["new_prob_diag_ready"], 1)
                    pe.matmul(ps(6, BR, SB), HM[0:BR, 8:16], DG[0:BR, :], start=True, stop=True).then_inc(s["new_prob_spread"], 1)
                elif kind == "hgrn":
                    pe.wait_ge(s["new_prob_ready"], 1)
                    pe.wait_ge(s["sample_state_ready"], 1)
                    pe.wait_ge(s["sample_hq_padded"], 2)
                    for n in range(SB * NG):
                        last = pe.matmul(ps(6, HD, BR, o=256), QHP[:, n, :], S0T[:, n // NG, n % NG, :], start=n == 0,
                                         stop=n == SB * NG - 1)
                    last.then_inc(s["sample_hgrn_ready"], 1)
                elif kind == "values":
                    pe.wait_ge(s[f"pages_in{b % 2}"], 128 * (SB // 2 + b // 2 + 1))
                    if b == 0:
                        pe.wait_ge(s["new_values_in"], 16)
                        pe.wait_ge(s["sample_hgrn_copied"], 1)
                    ge(pe, s["sample_out_copied"], b)
                    dst = ps(6, UW, SB, o=b % 2 * UW)
                    for g in range(NPG):
                        pe.matmul(dst, PTP[:, g, AH * b:AH * (b + 1)], VP[b % 2][:, g, :], start=g == 0, stop=False)
                    pe.matmul(dst, PN[0:SB, AH * b:AH * (b + 1)], VN[0:SB, :], start=False, stop=True)\
                        .then_inc(s["sample_values_done"], 1)

            sample("queries", 0)
            scores(0)
            for m in range(NA):
                if m + 1 < NA:
                    scores(m + 1)
                if m >= 2:
                    values(m - 2)
                transposes(m)
                for side in SIDE.get(m, ()):
                    sample(*side)
            values(NA - 2)
            values(NA - 1)

            def transpose_mix(i):
                pe.wait_ge(s["mix_hgrn_ready"], i + 1)
                pe.wait_ge(s["mix_attn_ready"], i + 1)
                for h in range(2):
                    n = 2 * i + h
                    ge(pe, s["mix_low_ready"], n - 1)
                    for k in range(4):
                        last = pe.transpose(ps(6 + n % 2, rows(i), o=k * P), MIX[0:rows(i), i % 2, (4 * h + k) * P:(4 * h + k + 1) * P],
                                            IDN[0:rows(i), 0:rows(i)])
                    last.then_inc(s["mix_transposed"], 1)

            transpose_mix(0)
            for u in range(NU, NU + NUO):
                unit(u, transpose_mix)

        @block.sync
        def _(sp):
            def load_x(g):
                for i in range(3 * g, 3 * g + 3):
                    sp.dma_start(x_buf(i)[0:rows(i)], x_rows(i)).then_inc(s[f"x_in{g}"], 16)

            def load_index_keys(b):
                slot = (b // 2) % 2
                if b >= 4:
                    ge(sp, s["sample_index_done"], b // 2 - 1)
                pages_ = [sp.value_load(PT_[0:1, b * NPG + g:b * NPG + g + 1], min_val=0, max_val=NPOOL - 1)
                          for g in range(NPG)]
                for g, page in enumerate(pages_):
                    sp.dma_start(IKT[b % 2 * HD:b % 2 * HD + HD, slot, g * P:(g + 1) * P],
                                 cache_ikt[bass.ds(page, 1)].rearrange("a d k -> (a d) k"))\
                        .then_inc(s[f"index_pages_in{slot}"], 16)

            load_x(0)
            sp.dma_start(IDN[:, :], c_ident).then_inc(s["ident_in"], 16)
            sp.dma_start(LNG[:, :], ln_g).then_inc(s["gain_in"], 16)
            load_weights(sp, 0)
            load_x(1)
            load_x(2)
            for dst, src in ((LBR[:, :, :], lbs), (BITF[:, :], c_bits),
                             (QG[:, :], q_g), (KG[:, :], k_g), (HNG[:, :], hn_g), (PT_[0:1, :], pages),
                             (E8[0:8, :], c_e8[0]), (E8H[0:8, :], c_e8[1]), (OH[0:32, :], c_oh), (REL[0:32, :], rel),
                             (INM[:, :, :], c_masks[:, 0:256]), (BM[:, :], c_masks[:, 256:384]),
                             (HM[0:BR, :], c_masks[0:BR, 656:674]), (TRF[:, :], c_masks[:, 400:528]), (ANT[:, :], c_masks[:, 528:656])):
                sp.dma_start(dst, src).then_inc(s["const_in"], 16)
            load_weights(sp, 1)
            sp.wait_ge(s["const_in"], CONSTS_IN)
            staged = 0
            for u in range(NU):
                kind, a = UNITS[u]
                late = LATE if u - 2 in HGU else -1
                if u + 2 < NU and late < 0:
                    load_weights(sp, u + 2)
                if u == 1:
                    for b in range(4):
                        load_index_keys(b)
                if u == UIX:
                    sp.wait_ge(s["index_rows_copied"], 3)
                    sp.dma_start(ik_prompt[0, 0].rearrange("(t p) d -> p t d", p=P), IKN[:, 0:NT, :])\
                        .then_inc(s["early_outputs_stored"], 16)
                    sp.dma_start(ik_sample[0, :, 0, :], IKN[0:SB, NT, :]).then_inc(s["early_outputs_stored"], 16)
                    for b in range(4, SB):
                        load_index_keys(b)
                    ge(sp, s["bias_table_copied"], 1)
                    sp.dma_start(d_ut.ap(), UT[0:AH, :]).then_inc(s["bias_table_out"], 16)
                if u == NU - 1:
                    sp.wait_ge(s["bias_table_out"], 16)
                    sp.wait_ge(s["prep_done"], NG)
                    sp.dma_start(BRAW[:, :, :], bass.AP(d_ut, 0, [[1, P], [UL, AH], [1, NEAR]])).then_inc(s["bias_in"], 16)
                    ge(sp, s["state_updated"], NT * NG)
                    for hh in range(2):
                        sp.dma_start(s_prompt[0, 0].rearrange("(j a) k v -> a k j v", a=2)[hh],
                                     ST[hh * HD:(hh + 1) * HD, :, hh * HD:(hh + 1) * HD]).then_inc(s["early_outputs_stored"], 16)
                    load_rows(sp, NT)
                    load_rows(sp, 0)
                    sp.wait_ge(s["chunk_output_ready"], NT * NG)
                    load_states(sp)
                for i in range(NT + 1):
                    n = JOB0[u] + i
                    if i == late and u + 2 < NU:
                        load_weights(sp, u + 2)
                    if kind in STAGED:
                        ge(sp, s["job_copied"], n + 1)
                        dst = {"gh": d_gh, "ga": d_ga, "q": d_q, "k": d_k}.get(kind)
                        if kind == "v":
                            dst = v_prompt[0, 0, i * P:(i + 1) * P].rearrange("t h d -> t (h d)") if i < NT \
                                else v_sample[0, :, 0].rearrange("t h d -> t (h d)")
                        else:
                            dst = dst[row0(i):row0(i) + rows(i), a * UW:(a + 1) * UW]
                        sp.dma_start(dst, STG[0:rows(i), staged % 4, :]).then_inc(s[f"rows_out{staged % 4}"], 16)
                        staged += 1
                if kind == "hv":
                    ge(sp, s["job_copied"], JOB0[u + 1])
                    sp.dma_start(d_hv.ap()[:, a * UW:(a + 1) * UW], HV[0:SB, NT, a * UW:(a + 1) * UW])\
                        .then_inc(s["hv_out"], 16)
                if u - 3 in HGU:
                    j = HGU.index(u - 3)
                    ge(sp, s["chunk_output_copied"], NT * (j + 1))
                    sp.dma_start(d_ho[0:T, j * P:(j + 1) * P].rearrange("(c s) n -> s c n", s=P), HO[:, :, :])\
                        .then_inc(s["ho_out"], 16)
            sp_tail(sp)

        @block.gpsimd
        def _(gp):
            chain = [0]

            def link(ins):
                chain[0] += 1
                ins.then_inc(s["gp_chain"], 1)
                gp.wait_ge(s["gp_chain"], chain[0])

            gp.memset(IQP[:, :, :], 0.0).then_inc(s["init_gp"], 1)
            gp.memset(RM[:, :], 1.0).then_inc(s["init_gp"], 1)
            gp.wait_ge(s["init_gp"], 2)
            gp.memset(RM[:, 0:T:P], 0.0).then_inc(s["init_gp"], 1)

            def prep(j):
                gp.wait_ge(s["decay_sums_ready"], j + 1)
                ge(gp, s["chunk_output_ready"], NT * j)
                ge(gp, s["state_updated"], NT * j)
                b4 = FB[:, :].rearrange("p (n t) -> p n t", t=SUB)
                ref = b4[:, :, SUB // 2 - 1]
                ge(gp, s["ho_out"], 16 * j)
                gp.tensor_tensor(QD[:, :].rearrange("p (n t) -> p n t", t=SUB), b4, bc(ref, SUB), ALU.subtract)
                b8 = FB[:, :].rearrange("p (c t) -> p c t", t=P)
                o = 0
                for i in range(NSUB):
                    w = SUB * (i + 1)
                    gp.tensor_tensor(KT[:, o:o + NT * w].rearrange("p (c t) -> p c t", t=w),
                                     bc(ref[:, i:NT * NSUB:NSUB], w), b8[:, :, 0:w], ALU.subtract)
                    o += NT * w
                gp.tensor_tensor(DE[:, 1, :], b8[:, :, P - 1], ref[:, NSUB - 1:NT * NSUB:NSUB], ALU.subtract)
                gp.tensor_scalar(DE[:, 0, :], b8[:, :, P - 1], 1.0, 0.0, ALU.mult, ALU.add).then_inc(s["exponents_ready"], 1)
                gp.wait_ge(s["exponentials_ready"], j + 1)
                gp.tensor_tensor(QD[:, :], QD[:, :], QB[:, :], ALU.mult).then_inc(s["q_decayed_ready"], 1)
                gp.tensor_tensor(QI[:, :], QI[:, :], QB[:, :], ALU.mult)
                k8 = HK[:, :].rearrange("p (c t) -> p c t", t=P)
                o = 0
                for i in range(NSUB):
                    w = SUB * (i + 1)
                    kt = KT[:, o:o + NT * w].rearrange("p (c t) -> p c t", t=w)
                    last = gp.tensor_tensor(kt, kt, k8[:, :, 0:w], ALU.mult)
                    o += NT * w
                last.then_inc(s["prep_done"], 1)

            def chunk(kind, j, c):
                n = NT * j + c
                if kind == "intra":
                    gp.wait_ge(s["intra_copied"], n + 1)
                    gp.tensor_tensor(ATB[:, n % 2], ATB[:, n % 2], INM[:, :, :], ALU.mult).then_inc(s["intra_masked"], 1)
                elif kind == "keys":
                    gp.wait_ge(s["state_part_decayed"], n + 1)
                    gp.tensor_tensor(TMP[:, n % 2, :], TMP[:, n % 2, :], BM[:, :], ALU.mult).then_inc(s["state_part_masked"], 1)
                else:
                    gp.wait_ge(s["chunk_output_ready"], n + 1)
                    gp.wait_ge(s["state_part_masked"], n + 1)
                    link(gp.tensor_scalar(ST[:, j, :], ST[:, j, :], DE[:, 0, c:c + 1], 0.0, ALU.mult, ALU.add))
                    gp.tensor_tensor(ST[:, j, :], ST[:, j, :], TMP[:, n % 2, :], ALU.add).then_inc(s["state_updated"], 1)

            gp.wait_ge(s["gain_in"], 16)
            for i in range(NT + 1):
                if i == 3:
                    split_w(gp, 0)
                gp.wait_ge(s["x_squares_ready"], i + 1)
                gp.tensor_tensor(x_buf(i)[0:rows(i)], x_buf(i)[0:rows(i)], LNG[0:rows(i), :], ALU.mult)\
                    .then_inc(s["x_gained"], 1)
            gp.wait_ge(s["const_in"], CONSTS_IN)
            for u in range(NU):
                if u + 1 < NU:
                    split_w(gp, u + 1)
                if u == UIX:
                    for t in range(2, NT):
                        gp.wait_ge(s["index_scores_added"], IH * (t - 1))
                        diag = SC[:, SC0[t] + P * t:SC0[t] + P * (t + 1)]
                        gp.affine_select(out=diag, in_=diag, compare_op=ALU.is_ge, fill=UNSEEN, base=0,
                                         pattern=[[-1, P]], channel_multiplier=1).then_inc(s["index_scores_causal"], 1)
                    gp.wait_ge(s["sample_index_ready"], 1)
                    gp.wait_ge(s["index_products_ready"], IH * 6)
                    gp.wait_ge(s["bias_table_ready"], 1)
                    gp.wait_ge(s["early_outputs_stored"], 32)
                    gp.memset(ATB[:, :, :, :], 0.0)
                    gp.memset(QT[:, :, :], 0.0)
                    gp.memset(ST[:, :, :], 0.0).then_inc(s["init_gp"], 1)
                    gp.wait_ge(s["init_gp"], 4)
                if u - 1 in HGU:
                    prep(HGU.index(u - 1))
                for n in range(JOB0[u], JOB0[u + 1]):
                    for event in EVENTS.get(n, ()):
                        chunk(*event)
            gp_tail(gp, link)

        @block.scalar
        def _(act):
            chain = [0]

            def link(ins):
                chain[0] += 1
                ins.then_inc(s["act_chain"], 1)
                act.wait_ge(s["act_chain"], chain[0])

            def squares(g):
                act.wait_ge(s[f"x_in{g}"], 48)
                for i in range(3 * g, 3 * g + 3):
                    r = rows(i)
                    ge(act, s["x_squares_ready"], i)
                    act.activation(JA[0:r, :], x_buf(i)[0:r], ACT.Square,
                                   accum_out=STAT[0:r, 0, i:i + 1]).then_inc(s["x_squares_ready"], 1)

            def scale_x(g):
                act.wait_ge(s["rstd_done"], g + 1)
                for i in range(3 * g, 3 * g + 3):
                    r = rows(i)
                    act.wait_ge(s["x_gained"], i + 1)
                    act.activation(x_buf(i)[0:r], x_buf(i)[0:r], ACT.Copy, scale=STAT[0:r, 3, i:i + 1])\
                        .then_inc(s["x_normed"], 1)

            def high_x(g):
                for i in range(3 * g, 3 * g + 3):
                    for h in range(2):
                        n = 2 * i + h
                        act.wait_ge(s["x_transposed"], n + 1)
                        src = ps(6 + n % 2).rearrange("p (k t) -> p k t", t=P)[:, :, 0:rows(i)]
                        act.activation(XH[:, 4 * h:4 * h + 4, row0(i):row0(i) + rows(i)], src, ACT.Copy)\
                            .then_inc(s["x_high_ready"], 1)

            def high_w(u):
                w = width(u)
                if NU > u >= 2:
                    act.wait_ge(s["job_done"], JOB0[u - 1])
                if u > NU + 1:
                    act.wait_ge(s["job_done"], JOB0[u - 1])
                for h in range(2):
                    act.wait_ge(s[f"weights_in{h}"], 16 * (u + 1))
                    act.activation(WH[:, u % 2, 4 * h:4 * h + 4, 0:w], WR[:, h, :, 0:w], ACT.Copy)\
                        .then_inc(s["weights_high_ready"], 1)

            def prep_log(j):
                act.wait_ge(s["job_copied"], JOB0[HGU[j] + 1])
                if j == 0:
                    act.wait_ge(s["lb_terms_ready"], 2)
                c = slice(j, j + 1)
                act.activation(KSS[:, j, :], FS[:, j, :], ACT.Identity, scale=NOML[:, c], bias=OML[:, c])
                act.activation(FS[:, j, :], FS[:, j, :], ACT.Identity, scale=OML[:, c], bias=LB[:, c])
                act.activation(HK[:, :], FB[:, :], ACT.Identity, scale=NOML[:, c], bias=OML[:, c])
                act.activation(FB[:, :], FB[:, :], ACT.Ln, scale=OML[:, c], bias=LB[:, c]).then_inc(s["decay_logs_ready"], 1)

            def prep_exp(j):
                act.wait_ge(s["exponents_ready"], j + 1)
                act.activation(QD[:, :], QD[:, :], ACT.Exp)
                act.activation(QI[:, :], FB[:, :], ACT.Exp)
                act.activation(KT[:, :], KT[:, :], ACT.Exp)
                act.activation(DE[:, :, :], DE[:, :, :], ACT.Exp).then_inc(s["exponentials_ready"], 1)
                act.wait_ge(s["q_decayed_ready"], j + 1)
                for hh in range(2):
                    r = slice(hh * HD, hh * HD + HD)
                    last = act.activation(QT[r, hh, :], QD[r, :], ACT.Copy)
                last.then_inc(s["q_by_head_ready"], 1)

            def chunk(kind, j, c):
                n = NT * j + c
                if kind == "intra":
                    act.wait_ge(s["intra_products_ready"], n + 1)
                    ge(act, s["chunk_output_ready"], n - 1)
                    src = ps(6 + n % 2, 256).rearrange("p (i h t) -> p i h t", h=2, t=SUB)
                    for i in range(NSUB):
                        w = SUB * (i + 1)
                        act.activation(ATB[0:w, n % 2, :, i * SUB:(i + 1) * SUB], src[0:w, i], ACT.Copy)
                    act.activation(KTN[:, n % 2, :], ps(6 + n % 2, P, o=256), ACT.Copy).then_inc(s["intra_copied"], 1)
                elif kind == "keys":
                    act.wait_ge(s["state_part_ready"], n + 1)
                    ge(act, s["state_updated"], n - 1)
                    act.activation(TMP[:, n % 2, :], ps(5, P), ACT.Copy, scale=DE[:, 1, c:c + 1])\
                        .then_inc(s["state_part_decayed"], 1)
                else:
                    act.wait_ge(s["chunk_output_ready"], n + 1)
                    if c == 0:
                        ge(act, s["ho_out"], 16 * j)
                    if c == 0:
                        act.wait_ge(s["q_by_head_ready"], j + 1)
                    for hh in range(2):
                        act.activation(ps(4, HD, o=P + hh * HD), ps(4, HD, o=hh * HD), ACT.Square, scale=HD ** -0.5,
                                       accum_out=SHO[:, 0, c, 2 * j + hh:2 * j + hh + 1])
                    act.activation(HO[:, c, :], ps(4, P), ACT.Copy, scale=HD ** -0.5).then_inc(s["chunk_output_copied"], 1)

            staged = [0]

            def evac(u, q):
                kind, a = UNITS[u]
                form, i, c = jobs(u)[q]
                n = JOB0[u] + q
                act.wait_ge(s["job_done"], n + 1)
                bank = n % PJ
                r = rows(i) if form == "N" else P
                if kind == "iq":
                    t0, cw = CHUNKS[c]
                    lo, hi = max(2 * P - t0, 0), min(T - t0, cw)
                    j = 2 * a + i
                    dst = slice(t0 + lo - 2 * P, t0 + hi - 2 * P)
                    act.activation(IQS[0:HD, 2 * j, dst], ps(bank, hi - lo, HD, o=lo), ACT.Copy)
                    last = act.activation(IQS[HD:P, 2 * j + 1, dst], ps(bank, hi - lo, P, HD, lo), ACT.Copy)
                    if c == 2:
                        act.wait_ge(s["init_gp"], 1)
                        iqp = IQP[:, :, :].rearrange("p a b -> p (a b)")
                        for hh in range(2):
                            for b2 in range(2):
                                last = act.activation(
                                    iqp[b2 * HD:(b2 + 1) * HD, 8 * b2 + 2 * j + hh:4 * BR:BR + 16],
                                    ps(bank, SB, (hh + 1) * HD, hh * HD, 256)[:, b2:SB:2], ACT.Copy)
                elif kind == "ix":
                    t0, cw = CHUNKS[c]
                    hi = min(T - t0, cw)
                    act.activation(IXT[0:XW, t0:t0 + cw], ps(bank, cw, XW), ACT.Copy)
                    act.activation(IA[0:HD, t0:t0 + hi], ps(bank, hi, HD), ACT.Copy)
                    last = act.activation(IB[HD:P, t0:t0 + hi], ps(bank, hi, HD), ACT.Copy)
                elif kind == "hg":
                    t0, cw = CHUNKS[c]
                    hi = min(T - t0, cw)
                    dst, samp, fn = ((FB, FS, ACT.Sigmoid), (QB, QSS, ACT.Silu))[i]
                    if q == 0 and a > 0:
                        act.wait_ge(s["prep_done"], a)
                    last = act.activation(dst[:, t0:t0 + hi], ps(bank, hi), fn)
                    if c == 2:
                        last = act.activation(samp[:, a, :], ps(bank, SB, o=hi), fn)
                elif kind == "hv":
                    last = act.activation(HV[0:r, i, a * UW:(a + 1) * UW], ps(bank, UW, r), ACT.Copy)
                elif kind in STAGED:
                    g = staged[0]
                    ge(act, s[f"rows_out{g % 4}"], 16 * (g // 4))
                    last = act.activation(STG[0:r, g % 4, :], ps(bank, UW, r),
                                          ACT.Silu if kind in ("gh", "ga") else ACT.Copy)
                    if kind in ("q", "k"):
                        h0 = AH if kind == "k" else a * 4
                        for h in range(4):
                            last = act.activation(ps(bank, HD, r, o=UW + h * HD), ps(bank, HD, r, o=h * HD), ACT.Square,
                                                  accum_out=SQK[0:r, 0, i, h0 + h:h0 + h + 1])
                    staged[0] += 1
                last.then_inc(s["job_copied"], 1)

            act.wait_ge(s["init_dve"], 1)
            squares(0)
            high_w(0)
            squares(1)
            scale_x(0)
            squares(2)
            scale_x(1)
            high_x(0)
            scale_x(2)
            high_x(1)
            high_x(2)
            act.wait_ge(s["const_in"], CONSTS_IN)
            act.wait_ge(s["init_dve"], 2)
            act.activation(ANR[:, :], ANT[:, :], ACT.Copy)
            act.activation(IDB[:, :], IDN[:, :], ACT.Copy)
            act.activation(E8B[0:8, :], E8[0:8, :], ACT.Copy)
            act.activation(TRI[:, :], TRF[:, :], ACT.Copy).then_inc(s["init_act"], 1)
            act.activation(LB[:, :], OML[:, :], ACT.Sigmoid).then_inc(s["lb_ready"], 1)

            act.wait_ge(s["bias_table_ready"], 1)
            act.activation(UT[0:AH, :], ps(6, UL, AH), ACT.Copy, scale=8.0).then_inc(s["bias_table_copied"], 1)
            for u in range(NU):
                if u + 1 < NU:
                    high_w(u + 1)
                for q in range(len(jobs(u))):
                    evac(u, q)
                    if u - 1 in HGU and q == 1:
                        prep_log(HGU.index(u - 1))
                    for event in EVENTS.get(JOB0[u] + q, ()):
                        chunk(*event)
                if u - 1 in HGU:
                    prep_exp(HGU.index(u - 1))
                if u == UIX:
                    act.wait_ge(s["job_copied"], JOB0[UIX + 1])
                    act.activation(IKNEW[0:HD, :], IXT[0:HD, T:TT:2], ACT.Copy)
                    act.activation(IKNEW[HD:P, :], IXT[0:HD, T + 1:TT:2], ACT.Copy).then_inc(s["new_index_keys_ready"], 1)
                    for g, (lo, hi) in enumerate(((0, 5), (5, NT), (NT, NT + 1))):
                        act.wait_ge(s["index_rows_transposed"], min(g, 1) + 1)
                        r = rows(lo)
                        src = ps(6 + min(g, 1), 512, r)[:, (lo - 5 * min(g, 1)) * XW:(hi - 5 * min(g, 1)) * XW]\
                            .rearrange("p (i n) -> p i n", n=XW)
                        act.activation(IW[0:r, lo:hi, :], src[:, :, HD:XW], ACT.Copy, scale=float(IH ** -0.5 * HD ** -0.5))
                        act.activation(IKN[0:r, lo:hi, :], src[:, :, 0:HD], ACT.Copy).then_inc(s["index_rows_copied"], 1)
                    for m in range(IH * 6):
                        w = P * (m // IH + 3)
                        act.wait_ge(s["index_products_ready"], m + 1)
                        ge(act, s["index_scores_added"], m - 1)
                        act.activation(RB[:, m % 2, 0:w], ps(2 * (m % 2), w), ACT.Relu).then_inc(s["index_relu_ready"], 1)
                    act.wait_ge(s["early_outputs_stored"], 32)
                    act.wait_ge(s["sample_index_done"], 4)
                    act.activation(RSM[0:BR, :], ps(4, PAST + 1, BR), ACT.Relu).then_inc(s["sample_index_relu"], 1)
            act_tail(act, link, high_w)

        @block.vector
        def _(dve):
            chain = [0]

            def link(ins):
                chain[0] += 1
                ins.then_inc(s["dve_chain"], 1)
                dve.wait_ge(s["dve_chain"], chain[0])

            dve.memset(STAT[:, 0, :], 1.0)
            dve.memset(SQK[:, 0, :, :], 1.0)
            dve.memset(CNT[:, :], 0.0)
            dve.memset(U[:, :], 0).then_inc(s["init_dve"], 1)
            dve.wait_ge(s["init_dve"], 1)

            def x_norm(g):
                c = slice(3 * g, 3 * g + 3)
                dve.wait_ge(s["x_squares_ready"], 3 * g + 3)
                link(dve.tensor_scalar(STAT[:, 1, c], STAT[:, 0, c], 1.0 / D, EPS, ALU.mult, ALU.add))
                inverse_root(dve, link, STAT[:, 3, c], STAT[:, 1, c], STAT[:, 2, c], s["rstd_done"])

            def low_x(g):
                for i in range(3 * g, 3 * g + 3):
                    for h in range(2):
                        n = 2 * i + h
                        dve.wait_ge(s["x_high_ready"], n + 1)
                        src = ps(6 + n % 2).rearrange("p (k t) -> p k t", t=P)[:, :, 0:rows(i)]
                        c = slice(row0(i), row0(i) + rows(i))
                        dve.tensor_tensor(XL[:, 4 * h:4 * h + 4, c], src, f(XH[:, 4 * h:4 * h + 4, c]), ALU.subtract)\
                            .then_inc(s["x_low_ready"], 1)

            x_norm(0)
            x_norm(1)
            x_norm(2)
            low_x(0)
            low_x(1)
            low_x(2)
            dve.wait_ge(s["const_in"], CONSTS_IN)
            dve.tensor_copy(BITI[:, :], BITF[:, :])
            dve.tensor_tensor(OML[:, :], LBR[:, 0, :], LBR[:, 1, :], ALU.subtract).then_inc(s["init_dve"], 1)
            dve.wait_ge(s["lb_ready"], 1)
            dve.tensor_scalar(OML[:, :], LB[:, :], -1.0, 1.0, ALU.mult, ALU.add).then_inc(s["lb_terms_ready"], 1)
            dve.tensor_scalar(NOML[:, :], LB[:, :], 1.0, -1.0, ALU.mult, ALU.add).then_inc(s["lb_terms_ready"], 1)
            for u in range(UIX):
                for q, (form, i, c) in enumerate(jobs(u)):
                    n = JOB0[u] + q
                    t0, cw = CHUNKS[c]
                    lo, hi = max(2 * P - t0, 0), min(T - t0, cw)
                    j = 2 * UNITS[u][1] + i
                    dst = slice(t0 + lo - 2 * P, t0 + hi - 2 * P)
                    dve.wait_ge(s["job_copied"], n + 1)
                    dve.tensor_tensor(IQS[HD:P, 2 * j, dst], ps(n % PJ, hi - lo, HD, o=lo), f(IQS[0:HD, 2 * j, dst]),
                                      ALU.subtract)
                    dve.tensor_tensor(IQS[0:HD, 2 * j + 1, dst], ps(n % PJ, hi - lo, P, HD, lo),
                                      f(IQS[HD:P, 2 * j + 1, dst]), ALU.subtract).then_inc(s["index_q_low_ready"], 1)
            for c, (t0, cw) in enumerate(CHUNKS):
                n = JOB0[UIX] + c
                hi = min(T - t0, cw)
                dve.wait_ge(s["job_copied"], n + 1)
                for stack in (IB[0:HD, t0:t0 + hi], IA[HD:P, t0:t0 + hi]):
                    ins = dve.tensor_tensor(stack, ps(n % PJ, hi, HD), f(IA[0:HD, t0:t0 + hi]), ALU.subtract)
                ins.then_inc(s["index_low_ready"], 1)
            dve.wait_ge(s["index_weights_spread"], 1)
            link(dve.tensor_tensor(HMT[0:BR, :], ps(7, IH, BR), HM[0:BR, 0:8], ALU.mult))
            link(dve.reduce_sum(IWC[0:BR, :], HMT[0:BR, :], axis=AX.X))
            dve.tensor_scalar(WSEL[0:BR, :], HM[0:BR, 8:16], IWC[0:BR, 0:1], None, ALU.mult).then_inc(s["index_weights_selected"], 1)
            for m in range(IH * 6):
                t, h = m // IH + 2, m % IH
                w = P * (t + 1)
                sc = SC[:, SC0[t]:SC0[t] + w]
                dve.wait_ge(s["index_relu_ready"], m + 1)
                if h == 0:
                    ins = dve.tensor_scalar(sc, RB[:, m % 2, 0:w], IW[:, t, h:h + 1], None, ALU.mult)
                else:
                    dve.wait_ge(s["index_scores_added"], m)
                    ins = dve.scalar_tensor_tensor(sc, RB[:, m % 2, 0:w], IW[:, t, h:h + 1], sc, ALU.mult, ALU.add)
                ins.then_inc(s["index_scores_added"], 1)

            dve.wait_ge(s["sample_index_summed"], 1)
            dve.tensor_copy(SCS[0:SB, 0:PAST + 1], ps(0, PAST + 1, SB)).then_inc(s["sample_index_ready"], 1)
            dve.wait_ge(s["index_scores_causal"], 6)
            dve.wait_ge(s["sample_index_ready"], 1)
            tiles = [(t - 2, P, SC[:, SC0[t]:SC0[t] + P * (t + 1)], P * (t + 1)) for t in range(2, NT)]
            tiles.append((6, SB, SCS[0:SB, 0:PAST + 1], PAST + 1))

            def count(threshold, op, done):
                for k, r, sc, w in tiles:
                    dve.tensor_scalar(JK[0:r, 0:w], sc, threshold(k, r), None, op, ALU.add,
                                      accum_out=CNT[0:r, k:k + 1]).then_inc(s["dve_chain"], 1)
                    dve.wait_ge(s["dve_chain"], done + k + 1)

            count(lambda k, r: 0.0, ALU.is_ge, chain[0])
            chain[0] += 7
            link(dve.tensor_scalar(XM[:, :], CNT[:, :], float(TOPK), -1.0, ALU.is_lt, ALU.mult))
            def rounds(a, b):
                start = chain[0]
                with dve.Fori(a, b) as it:
                    done = (it - a) * 10 + start
                    dve.scalar_tensor_tensor(CAND[:, :], U[:, :], BITI[:, bass.ds(it, 1)], XM[:, :],
                                             ALU.bitwise_or, ALU.bitwise_xor).then_inc(s["dve_chain"], 1)
                    dve.wait_ge(s["dve_chain"], done + 1)
                    count(lambda k, r: CAND[0:r, k:k + 1].bitcast(F32), ALU.is_ge, done + 1)
                    dve.tensor_scalar(HIT[:, :], CNT[:, :], float(TOPK), BITF[:, bass.ds(it, 1)],
                                      ALU.is_ge, ALU.mult).then_inc(s["dve_chain"], 1)
                    dve.wait_ge(s["dve_chain"], done + 9)
                    dve.tensor_tensor(U[:, :], U[:, :], HIT[:, :], ALU.bitwise_or).then_inc(s["dve_chain"], 1)
                    dve.wait_ge(s["dve_chain"], done + 10)
                chain[0] = start + 10 * (b - a)

            def scan(j):
                dve.wait_ge(s["decay_logs_ready"], j + 1)
                dve.tensor_tensor_scan(FB[:, :], RM[:, :], FB[:, :], 0.0, ALU.mult, ALU.add)\
                    .then_inc(s["decay_sums_ready"], 1)

            def masks():
                link(dve.tensor_tensor(CAND[:, :], U[:, :], XM[:, :], ALU.bitwise_xor))
                count(lambda k, r: CAND[0:r, k:k + 1].bitcast(F32), ALU.is_gt, chain[0])
                chain[0] += 7
                link(dve.tensor_scalar(NEED[:, :], CNT[:, :], -1.0, float(TOPK), ALU.mult, ALU.add))
                for k, r, sc, w in tiles:
                    thr = CAND[0:r, k:k + 1].bitcast(F32)
                    link(dve.tensor_scalar(JK[0:r, 0:w], sc, thr, None, ALU.is_equal))
                    link(dve.tensor_tensor_scan(CU[0:r, 0:w], JK[0:r, 0:w], JK[0:r, 0:w], 0.0, ALU.add, ALU.max))
                    link(dve.scalar_tensor_tensor(CU[0:r, 0:w], CU[0:r, 0:w], NEED[0:r, k:k + 1], JK[0:r, 0:w],
                                                  ALU.is_le, ALU.mult))
                    link(dve.scalar_tensor_tensor(JK[0:r, 0:w], sc, thr, CU[0:r, 0:w], ALU.is_gt, ALU.add))
                    m = MSK[:, SC0[k + 2]:SC0[k + 2] + w] if k < 6 else MSKS[0:SB, 0:w]
                    dve.tensor_scalar(m, JK[0:r, 0:w], -1.0, -NEG, ALU.add, ALU.mult).then_inc(s["masks_ready"], 1)
                    dve.wait_ge(s["masks_ready"], k + 1)

            rounds(0, 4)
            scan(0)
            rounds(4, 13)
            scan(1)
            rounds(13, 22)
            scan(2)
            rounds(22, ROUNDS)
            scan(3)
            masks()
            dve_tail(dve, link)

        @block.tensor
        def _(pe):
            def transpose_x(i):
                pe.wait_ge(s["x_normed"], i + 1)
                for h in range(2):
                    n = 2 * i + h
                    ge(pe, s["x_low_ready"], n - 1)
                    if n == 0:
                        pe.wait_ge(s["ident_in"], 16)
                    for k in range(4):
                        last = pe.transpose(ps(6 + n % 2, rows(i), o=k * P), x_buf(i)[0:rows(i), (4 * h + k) * P:(4 * h + k + 1) * P],
                                            IDN[0:rows(i), 0:rows(i)])
                    last.then_inc(s["x_transposed"], 1)

            def chunk(kind, j, c):
                n = NT * j + c
                bank = 6 + n % 2
                v = HV[:, c, j * P:(j + 1) * P]
                if kind == "intra":
                    if c == 0:
                        pe.wait_ge(s["prep_done"], j + 1)
                        pe.wait_ge(s["q_by_head_ready"], j + 1)
                    ge(pe, s["intra_copied"], n - 1)
                    o = 0
                    for i in range(NSUB):
                        w = SUB * (i + 1)
                        pe.matmul(ps(bank, 2 * SUB, w, o=2 * SUB * i), KT[:, o + c * w:o + (c + 1) * w],
                                  QT[:, :, c * P + i * SUB:c * P + (i + 1) * SUB], start=True, stop=True)
                        o += NT * w
                    o -= NT * P
                    pe.transpose(ps(bank, P, o=256), KT[:, o + c * P:o + (c + 1) * P], IDN[:, :]).then_inc(s["intra_products_ready"], 1)
                elif kind == "keys":
                    pe.wait_ge(s["intra_copied"], n + 1)
                    ge(pe, s["state_part_decayed"], n)
                    pe.matmul(ps(5, P), KTN[:, n % 2, :], v, start=True, stop=True).then_inc(s["state_part_ready"], 1)
                else:
                    ge(pe, s["state_updated"], n)
                    ge(pe, s["chunk_output_copied"], n)
                    if n == 0:
                        pe.wait_ge(s["init_gp"], 4)
                    pe.matmul(ps(4, P), QI[:, c * P:(c + 1) * P], ST[:, j, :], start=True, stop=False)
                    pe.wait_ge(s["intra_masked"], n + 1)
                    for hh in range(2):
                        last = pe.matmul(ps(4, HD, o=hh * HD), ATB[:, n % 2, hh, :], v[:, hh * HD:(hh + 1) * HD],
                                         start=False, stop=hh == 1)
                    last.then_inc(s["chunk_output_ready"], 1)

            def unit(u, transpose_mix=None):
                w = width(u)
                sl = u % 2
                pe.wait_ge(s["weights_low_ready"], 2 * u + 2)
                for q, (form, i, c) in enumerate(jobs(u)):
                    n = JOB0[u] + q
                    m = n - PJ
                    if u == NU and q < NT:
                        transpose_mix(q + 1)
                    if u == 0 and q == 2:
                        for x in range(6, NT + 1):
                            transpose_x(x)
                        pe.wait_ge(s["x_low_ready"], 2 * (NT + 1))
                        pe.wait_ge(s["const_in"], CONSTS_IN)
                        pe.matmul(ps(6, UL, AH), REL[0:32, :], OH[0:32, :], start=True, stop=True).then_inc(s["bias_table_ready"], 1)
                    if m >= JOB0[NU]:
                        pe.wait_ge(s["y_ready"], m - JOB0[NU] + 1)
                    elif m >= 0:
                        pe.wait_ge(s["job_copied"], m + 1)
                        if m < JOB0[UIX]:
                            pe.wait_ge(s["index_q_low_ready"], m + 1)
                    if u == 0:
                        pe.wait_ge(s["x_low_ready"], 6 * (c + 1))
                    if u >= NU:
                        pe.wait_ge(s["mix_low_ready"], 2 * (i + 1))
                    for k in range(KC):
                        for x, ww in ((XH, WH), (XL, WH), (XH, WL)):
                            first, final = k == 0 and x is XH and ww is WH, k == KC - 1 and ww is WL
                            if form == "T":
                                t0, cw = CHUNKS[c]
                                m_ = XW if u == UIX else P
                                last = pe.matmul(ps(n % PJ, cw, m_), ww[:, sl, k, i * P:i * P + m_], x[:, k, t0:t0 + cw],
                                                 start=first, stop=final)
                            else:
                                last = pe.matmul(ps(n % PJ, w, rows(i)), x[:, k, row0(i):row0(i) + rows(i)],
                                                 ww[:, sl, k, 0:w], start=first, stop=final)
                    last.then_inc(s["job_done"], 1)
                    for event in EVENTS.get(n, ()):
                        chunk(*event)

            for i in range(6):
                transpose_x(i)
            for u in range(UIX + 1):
                unit(u)
            pe.wait_ge(s["init_act"], 1)
            pe.wait_ge(s["bias_table_copied"], 1)
            pe.wait_ge(s["job_copied"], JOB0[UIX + 1])
            for g, (lo, hi) in enumerate(((0, 5), (5, NT + 1))):
                for i in range(lo, hi):
                    last = pe.transpose(ps(6 + g, XW, rows(i), o=(i - lo) * XW), IXT[0:XW, row0(i):row0(i) + rows(i)],
                                        IDN[0:XW, 0:XW])
                last.then_inc(s["index_rows_transposed"], 1)
            pe.wait_ge(s["index_low_ready"], 3)
            pe.wait_ge(s["index_rows_copied"], 3)
            pe.matmul(ps(7, IH, BR), E8[0:8, :], IW[0:8, NT, :], start=True, stop=True).then_inc(s["index_weights_spread"], 1)

            def sample_products(bp):
                sl = bp % 2
                pe.wait_ge(s[f"index_pages_in{sl}"], 256 * (bp // 2 + 1))
                for c in range(2):
                    pe.matmul(ps(4 + c, 512, BR), IQP[:, bp, :], IKT[:, sl, c * 512:(c + 1) * 512], start=bp == 0, stop=bp == 3)
                pe.matmul(ps(6, 1, BR), IQP[:, bp, :], IKNEW[:, bp:bp + 1], start=bp == 0, stop=bp == 3)\
                    .then_inc(s["sample_index_done"], 1)

            pe.wait_ge(s["new_index_keys_ready"], 1)
            for m in range(IH * 6):
                t, h = m // IH + 2, m % IH
                if m == 2 * IH:
                    for bp in (0, 1):
                        sample_products(bp)
                ge(pe, s["index_relu_ready"], m - 1)
                for c0 in range(0, P * (t + 1), 512):
                    w = min(512, P * (t + 1) - c0)
                    for kk, stack in enumerate((IA, IB)):
                        last = pe.matmul(ps(2 * (m % 2) + c0 // 512, w), IQS[:, h, (t - 2) * P:(t - 1) * P],
                                         stack[:, c0:c0 + w], start=kk == 0, stop=kk == 1)
                last.then_inc(s["index_products_ready"], 1)
            pe.wait_ge(s["index_relu_ready"], IH * 6)
            for bp in (2, 3):
                sample_products(bp)
            pe.wait_ge(s["sample_index_relu"], 1)
            pe.wait_ge(s["index_weights_selected"], 1)
            for c, w in ((0, 512), (1, 512), (2, 1)):
                last = pe.matmul(ps(c, w, SB), WSEL[0:BR, :], RSM[0:BR, c * 512:c * 512 + w], start=True, stop=True)
            last.then_inc(s["sample_index_summed"], 1)
            pe.wait_ge(s["sample_index_ready"], 1)
            for u in range(UIX + 1, NU):
                unit(u)
            pe_tail(pe, unit)


_OUTS = [(1, T, D), (SB, 1, D), (1, 1, T, KVH, HD), (1, 1, T, KVH, HD), (1, 1, T, HD), (1, 1, HH, HD, HD),
         (1, SB, 1, KVH, HD), (1, SB, 1, KVH, HD), (1, SB, 1, HD), (1, SB, HH, HD, HD)]


def _columns():
    q, k, v, ga, iq, ix, hq, hf, hi, gh = 0, 512, 768, 1024, 1536, 2048, 2120, 2632, 3144, 3656
    part = {"iq": iq, "hv": hi, "q": q, "k": k, "v": v, "gh": gh, "ga": ga}
    out = []
    for kind, a in UNITS:
        if kind == "ix":
            out.append([(ix + IH, HD), (ix, IH)])
        elif kind == "hg":
            out.append([(hf + a * P, P), (hq + a * P, P)])
        else:
            out.append([(part[kind] + a * UW, UW)])
    return out


def _bucket(n):
    n = max(n, 0)
    if n < 16:
        return n
    large = 16 + int(np.float32(np.log(np.float32(n) / np.float32(16)) / np.float32(np.log(128 / 16))) * np.float32(16))
    return min(large, 31)


def _constants():
    oh = np.zeros((32, UL), np.float32)
    for m in range(UL):
        oh[_bucket(255 - m), m] += 1
        oh[31, m] -= 1
    bits = np.tile((2.0 ** np.arange(ROUNDS - 1, -1, -1)).astype(np.float32), (P, 1))
    e8 = np.zeros((2, 8, BR), np.float32)
    for b in range(SB):
        for h in range(AH):
            e8[0, b, b * AH + h] = 1
            e8[1, h, b * AH + h] = 1
    masks = np.zeros((P, 674), np.float32)
    sidx = np.arange(P)[:, None]
    masks[:, 0:256] = np.tile(sidx <= np.arange(P)[None], (1, 2))
    masks[:, 256:384] = (sidx // HD == np.arange(P)[None] // HD)
    for b in range(SB):
        for h in range(AH):
            masks[b * AH + h, 656 + h] = 1
            masks[b * AH + h, 664 + b] = 1
            masks[b * AH + h, 672 + h // 2 % 2] = 1
    masks[:, 400:528] = np.where(np.arange(P)[None] <= sidx, 0.0, NEG)
    masks[:, 528:656] = np.eye(P)[::-1]
    return {"c_ident": np.eye(P, dtype=np.float32), "c_oh": oh, "c_bits": bits, "c_e8": e8, "c_masks": masks}


def kernel(**inputs):
    import concourse.bacc as _bacc
    from concourse.bass_utils import run_bass_kernel_spmd as _run

    x = {k: np.asarray(v) for k, v in inputs.items()}
    w_in, w_out = x["w_in"][0], x["w_out"][0]

    def unit_layout(w):
        return w.reshape(2, 4, P, -1).transpose(0, 2, 1, 3)

    cols = _columns()
    parts = [np.concatenate([w_in[:, c:c + n] for c, n in cs], axis=1) for cs in cols]
    main = [unit_layout(w) for u, w in enumerate(parts) if u != UIX]
    main += [unit_layout(w_out[:, c * UW:(c + 1) * UW]) for c in range(NUO)]
    data = {
        "x_prompt": x["x_prompt"], "x_sample": x["x_sample"],
        "w_main": np.stack(main), "w_ix": unit_layout(parts[UIX]),
        "cache_kt": x["cache_k"][0].reshape(-1, P, 2, P).transpose(0, 3, 2, 1),
        "cache_v": x["cache_v"][0].reshape(-1, P, UW),
        "cache_ikt": x["cache_ik"][0].transpose(0, 2, 1),
        "state": x["state_hgrn"][0].reshape(SB, NG, 2, HD, HD).transpose(2, 3, 0, 1, 4),
        "pages": x["page_table"].reshape(1, -1),
        "rel": x["rel_bias"],
        "ln_g": np.broadcast_to(x["ln_g"][0], (P, D)),
        "q_g": np.broadcast_to(x["q_norm_g"][0], (P, HD)), "k_g": np.broadcast_to(x["k_norm_g"][0], (P, HD)),
        "hn_g": np.broadcast_to(x["hgrn_norm_g"][0], (P, HD)),
        "lbs": x["hgrn_lb"].reshape(2, NG, P).transpose(2, 0, 1),
        **_constants(),
    }
    nc = _bacc.Bacc("TRN2", target_bir_lowering=False, num_devices=1)
    arrays, args = {}, []
    for name, a in data.items():
        a = np.ascontiguousarray(a)
        arrays[f"in_{name}"] = a
        args.append(nc.dram_tensor(f"in_{name}", a.shape, mybir.dt.from_np(a.dtype), kind="ExternalInput").ap())
    for i, shape in enumerate(_OUTS):
        args.append(nc.dram_tensor(f"out_{i}", shape, F32, kind="ExternalOutput").ap())
    hymba_step(nc, *args)
    r = _run(nc, [arrays], core_ids=[0])
    return tuple(r.results[0][f"out_{i}"] for i in range(len(_OUTS)))
```
